# Optimizing a Trainium2 kernel written in Bass

```python
import jax
import jax.numpy as jnp
from jax import lax
import numpy as np
import math

D_MODEL = 1024
BATCH = 1
SEQ = 256
DEPTH = 2

HEAD_DIM = 64
A_WIDTH = D_MODEL // 2
A_HEADS = A_WIDTH // HEAD_DIM
CHUNK = 128
B_WIDTH = D_MODEL // 2
CONV_WIDTH = 31
IN_WIDTH = 2 * A_WIDTH + 2 * B_WIDTH
ATTN_HEADS = D_MODEL // HEAD_DIM
DILATED_PATTERNS = ((128, 1), (512, 4), (2048, 16))
BLOCK = 128
ROPE_THETA = 10000.0
D_FF = 2816
FFN_CONV_WIDTH = 3
EPS = 1e-6
NEG = -1e30


def rms_norm(x, g):
    xf = x.astype(jnp.float32)
    y = xf * lax.rsqrt(jnp.mean(xf * xf, axis=-1, keepdims=True) + EPS)
    return (y * g.astype(jnp.float32)).astype(x.dtype)

def layer_norm(x, g, b):
    xf = x.astype(jnp.float32)
    mu = jnp.mean(xf, axis=-1, keepdims=True)
    var = jnp.mean(jnp.square(xf - mu), axis=-1, keepdims=True)
    y = (xf - mu) * lax.rsqrt(var + EPS)
    return (y * g.astype(jnp.float32) + b.astype(jnp.float32)).astype(x.dtype)

def causal_dwconv(x, w, b):
    k = w.shape[0]
    y = lax.conv_general_dilated(
        x, w[:, None, :].astype(x.dtype), window_strides=(1,),
        padding=[(k - 1, 0)], dimension_numbers=('NWC', 'WIO', 'NWC'),
        feature_group_count=x.shape[-1])
    return y + b.astype(x.dtype)

def rotary(x, pos):
    half = x.shape[-1] // 2
    inv = ROPE_THETA ** (-jnp.arange(half, dtype=jnp.float32) / half)
    ang = pos.astype(jnp.float32)[:, None] * inv[None, :]
    cos = jnp.cos(ang)[None, :, None, :]
    sin = jnp.sin(ang)[None, :, None, :]
    xf = x.astype(jnp.float32)
    x1, x2 = xf[..., :half], xf[..., half:]
    out = jnp.concatenate([x1 * cos - x2 * sin, x2 * cos + x1 * sin], axis=-1)
    return out.astype(x.dtype)

def chunked_spatial_gating(z, ln_g, ln_b, w_s, b_s):
    u, v = jnp.split(z, 2, axis=-1)
    v = layer_norm(v, ln_g, ln_b)
    bn, s, _ = v.shape
    v = v.reshape(bn, s // CHUNK, CHUNK, A_HEADS, HEAD_DIM)
    causal = jnp.tril(jnp.ones((CHUNK, CHUNK), dtype=bool))
    w = jnp.where(causal, w_s, jnp.zeros_like(w_s))
    mixed = jnp.einsum('hts,bcshd->bcthd', w, v) + b_s.T[None, None, :, :, None]
    return u * mixed.reshape(bn, s, A_WIDTH)

def conformer_conv(z, conv_w, conv_b, ln_g, ln_b):
    a, g = jnp.split(z, 2, axis=-1)
    h = a * jax.nn.sigmoid(g)
    h = causal_dwconv(h, conv_w, conv_b)
    h = layer_norm(h, ln_g, ln_b)
    return jax.nn.silu(h)

def dilated_branch(q, k, v, window, dilation):
    bn, s, h, dh = q.shape
    span = dilation * BLOCK
    s_pad = -(-s // span) * span
    seq_len = s_pad // dilation
    nb = seq_len // BLOCK
    reach = window // dilation

    def strided(t):
        t = jnp.pad(t, [(0, 0), (0, s_pad - s), (0, 0), (0, 0)])
        t = t.reshape(bn, seq_len, dilation, h, dh).transpose(0, 2, 1, 3, 4)
        return t.reshape(bn, dilation, nb, BLOCK, h, dh)

    def with_prev(t):
        prev = jnp.pad(t, [(0, 0), (0, 0), (1, 0), (0, 0), (0, 0), (0, 0)])[:, :, :-1]
        return jnp.concatenate([prev, t], axis=3)

    qs = strided(q)
    kw = with_prev(strided(k))
    vw = with_prev(strided(v))
    qi = jnp.arange(BLOCK)[:, None]
    kj = jnp.arange(2 * BLOCK)[None, :]
    dist = BLOCK + qi - kj
    band = (dist >= 0) & (dist <= reach)
    blk = jnp.arange(nb)[:, None, None]
    valid = band[None] & ((blk > 0) | (kj[None] >= BLOCK))

    scores = jnp.einsum('brnqhd,brnkhd->brnhqk', qs, kw).astype(jnp.float32)
    scores = scores * (HEAD_DIM ** -0.5)
    scores = jnp.where(valid[None, None, :, None], scores, NEG)
    m = jnp.max(scores, axis=-1, keepdims=True)
    p = jnp.exp(scores - m)
    l = jnp.sum(p, axis=-1, keepdims=True)
    o = jnp.einsum('brnhqk,brnkhd->brnqhd', p / l, vw.astype(jnp.float32))
    lse = (m + jnp.log(l))[..., 0]

    o = o.reshape(bn, dilation, seq_len, h, dh).transpose(0, 2, 1, 3, 4)
    o = o.reshape(bn, s_pad, h, dh)[:, :s]
    lse = lse.transpose(0, 1, 2, 4, 3).reshape(bn, dilation, seq_len, h)
    lse = lse.transpose(0, 2, 1, 3).reshape(bn, s_pad, h)[:, :s]
    return o, lse

def dilated_attention(q, k, v):
    outs, lses = [], []
    for window, dilation in DILATED_PATTERNS:
        o, lse = dilated_branch(q, k, v, window, dilation)
        outs.append(o)
        lses.append(lse)
    wts = jax.nn.softmax(jnp.stack(lses, axis=0), axis=0)
    return jnp.einsum('pbsh,pbshd->bshd', wts, jnp.stack(outs, axis=0))

def conv_ffn(x, norm_g, w_up, conv_w, conv_b, w_down):
    h = rms_norm(x, norm_g)
    u = causal_dwconv(h @ w_up, conv_w, conv_b)
    gate, val = jnp.split(u, 2, axis=-1)
    return x + (jax.nn.silu(gate) * val) @ w_down

def first_inputs(seed: int = 0) -> dict:
    key = jax.random.key(seed)
    keys = iter(jax.random.split(key, 32))
    n_even = (DEPTH + 1) // 2
    n_odd = DEPTH // 2
    f32 = jnp.float32

    def nrm(shape, scale):
        return jax.random.normal(next(keys), shape, f32) * scale

    def gain(shape):
        return 1.0 + nrm(shape, 0.02)

    return {
        'x': nrm((BATCH, SEQ, D_MODEL), 1.0),
        'even_norm_g': gain((n_even, D_MODEL)),
        'even_w_in': nrm((n_even, D_MODEL, IN_WIDTH), D_MODEL ** -0.5),
        'even_b_in': nrm((n_even, IN_WIDTH), 0.02),
        'even_v_ln_g': gain((n_even, A_WIDTH)),
        'even_v_ln_b': nrm((n_even, A_WIDTH), 0.02),
        'even_w_s': nrm((n_even, A_HEADS, CHUNK, CHUNK), CHUNK ** -0.5),
        'even_b_s': gain((n_even, A_HEADS, CHUNK)),
        'even_conv_w': nrm((n_even, CONV_WIDTH, B_WIDTH), CONV_WIDTH ** -0.5),
        'even_conv_b': nrm((n_even, B_WIDTH), 0.02),
        'even_conv_ln_g': gain((n_even, B_WIDTH)),
        'even_conv_ln_b': nrm((n_even, B_WIDTH), 0.02),
        'even_w_out': nrm((n_even, A_WIDTH + B_WIDTH, D_MODEL), (A_WIDTH + B_WIDTH) ** -0.5),
        'odd_norm_g': gain((n_odd, D_MODEL)),
        'odd_w_qkv': nrm((n_odd, D_MODEL, 3 * D_MODEL), D_MODEL ** -0.5),
        'odd_w_o': nrm((n_odd, D_MODEL, D_MODEL), D_MODEL ** -0.5),
        'ffn_norm_g': gain((DEPTH, D_MODEL)),
        'ffn_w_up': nrm((DEPTH, D_MODEL, 2 * D_FF), D_MODEL ** -0.5),
        'ffn_conv_w': nrm((DEPTH, FFN_CONV_WIDTH, 2 * D_FF), FFN_CONV_WIDTH ** -0.5),
        'ffn_conv_b': nrm((DEPTH, 2 * D_FF), 0.02),
        'ffn_w_down': nrm((DEPTH, D_FF, D_MODEL), D_FF ** -0.5),
        'final_norm_g': gain((D_MODEL,)),
    }

def first_block(x, even_norm_g, even_w_in, even_b_in, even_v_ln_g, even_v_ln_b,
              even_w_s, even_b_s, even_conv_w, even_conv_b, even_conv_ln_g,
              even_conv_ln_b, even_w_out, odd_norm_g, odd_w_qkv, odd_w_o,
              ffn_norm_g, ffn_w_up, ffn_conv_w, ffn_conv_b, ffn_w_down,
              final_norm_g):
    bn, s, _ = x.shape
    pos = jnp.arange(s)
    for i in range(DEPTH):
        j = i // 2
        if i % 2 == 0:
            h = rms_norm(x, even_norm_g[j])
            z = h @ even_w_in[j] + even_b_in[j]
            za = jax.nn.gelu(z[..., :2 * A_WIDTH])
            zb = z[..., 2 * A_WIDTH:]
            ya = chunked_spatial_gating(za, even_v_ln_g[j], even_v_ln_b[j],
                                        even_w_s[j], even_b_s[j])
            yb = conformer_conv(zb, even_conv_w[j], even_conv_b[j],
                                even_conv_ln_g[j], even_conv_ln_b[j])
            x = x + jnp.concatenate([ya, yb], axis=-1) @ even_w_out[j]
        else:
            h = rms_norm(x, odd_norm_g[j])
            qkv = (h @ odd_w_qkv[j]).reshape(bn, s, 3, ATTN_HEADS, HEAD_DIM)
            q = rotary(qkv[:, :, 0], pos)
            k = rotary(qkv[:, :, 1], pos)
            v = qkv[:, :, 2]
            o = dilated_attention(q, k, v).astype(x.dtype).reshape(bn, s, D_MODEL)
            x = x + o @ odd_w_o[j]
        x = conv_ffn(x, ffn_norm_g[i], ffn_w_up[i], ffn_conv_w[i], ffn_conv_b[i],
                     ffn_w_down[i])
    return rms_norm(x, final_norm_g)


DEPTH_2 = 1

N_BRANCH = 3
BRANCH_WIDTH = 512
SSM_HEADS = 8
SSM_HEAD_DIM = 64
SSM_INNER = 512
SSM_GROUPS = 2
SSM_STATE = 128
SSM_CONV = 4
SSD_CHUNK = 128
SSM_XBC = SSM_INNER + 2 * SSM_GROUPS * SSM_STATE
SB_HEADS = 4
SB_HEAD_DIM = 128
SB_INNER = 512
SB_BLOCK = 128
GDN_HEADS = 4
GDN_HEAD_DIM = 128
GDN_INNER = 512
GDN_CONV = 4
GDN_CHUNK = 64
MOE_GROUPS = 4
EXPERTS_PER_GROUP = 8
N_EXPERTS = 32
MOE_TOP_K = 2
EXPERT_FF = 512
MOE_BLOCK = 128
IN_SPLITS = (SSM_INNER, SSM_XBC, SSM_HEADS, 3 * SB_INNER, 3 * GDN_INNER, GDN_HEADS, GDN_HEADS, GDN_INNER, N_BRANCH * D_MODEL)
IN_COLS = SSM_INNER + SSM_XBC + SSM_HEADS + 3 * SB_INNER + 3 * GDN_INNER + 2 * GDN_HEADS + GDN_INNER + N_BRANCH * D_MODEL


def rms_norm_2(x, g):
    xf = x.astype(jnp.float32)
    y = xf * lax.rsqrt(jnp.mean(xf * xf, axis=-1, keepdims=True) + EPS)
    return (y * g.astype(jnp.float32)).astype(x.dtype)

def l2_norm(x):
    xf = x.astype(jnp.float32)
    return xf * lax.rsqrt(jnp.sum(xf * xf, axis=-1, keepdims=True) + EPS)

def causal_conv(x, w, b=None):
    k, ch = w.shape
    y = lax.conv_general_dilated(x, w[:, None, :].astype(x.dtype), window_strides=(1,), padding=[(k - 1, 0)],
                                 dimension_numbers=("NWC", "WIO", "NWC"), feature_group_count=ch)
    if b is not None:
        y = y + b.astype(x.dtype)
    return y

def ssd_chunked(xs, dt, a, bm, cm):
    bsz, s, h, p = xs.shape
    n = bm.shape[-1]
    nc = s // SSD_CHUNK
    xdt = (xs * dt[..., None]).reshape(bsz, nc, SSD_CHUNK, h, p)
    adt = (dt * a).reshape(bsz, nc, SSD_CHUNK, h).transpose(0, 3, 1, 2)
    bm = bm.reshape(bsz, nc, SSD_CHUNK, h, n)
    cm = cm.reshape(bsz, nc, SSD_CHUNK, h, n)
    a_cum = jnp.cumsum(adt, axis=-1)
    tril = jnp.tril(jnp.ones((SSD_CHUNK, SSD_CHUNK), bool))
    seg = jnp.exp(jnp.where(tril, a_cum[..., :, None] - a_cum[..., None, :], -jnp.inf))
    scores = jnp.einsum("bclhn,bcshn->bhcls", cm, bm) * seg
    y_diag = jnp.einsum("bhcls,bcshp->bclhp", scores, xdt)
    decay_states = jnp.exp(a_cum[..., -1:] - a_cum).transpose(0, 2, 3, 1)
    states = jnp.einsum("bclhn,bclhp->bchpn", bm, xdt * decay_states[..., None])
    chunk_decay = jnp.exp(a_cum[..., -1])

    def step(hstate, inp):
        st, dec = inp
        return hstate * dec[..., None, None] + st, hstate

    h0 = jnp.zeros((bsz, h, p, n), xs.dtype)
    _, states_in = lax.scan(step, h0, (states.transpose(1, 0, 2, 3, 4), chunk_decay.transpose(2, 0, 1)))
    states_in = states_in.transpose(1, 0, 2, 3, 4)
    c_dec = cm * jnp.exp(a_cum).transpose(0, 2, 3, 1)[..., None]
    y_off = jnp.einsum("bclhn,bchpn->bclhp", c_dec, states_in)
    return (y_diag + y_off).reshape(bsz, s, h, p)

def mamba2_branch(z, xbc, dt_raw, conv_w, conv_b, dt_bias, a_log, d_skip, norm_g):
    bsz, s, _ = z.shape
    xbc = jax.nn.silu(causal_conv(xbc, conv_w, conv_b)).astype(jnp.float32)
    xs, bm, cm = jnp.split(xbc, [SSM_INNER, SSM_INNER + SSM_GROUPS * SSM_STATE], axis=-1)
    xs = xs.reshape(bsz, s, SSM_HEADS, SSM_HEAD_DIM)
    rep = SSM_HEADS // SSM_GROUPS
    bm = jnp.repeat(bm.reshape(bsz, s, SSM_GROUPS, SSM_STATE), rep, axis=2)
    cm = jnp.repeat(cm.reshape(bsz, s, SSM_GROUPS, SSM_STATE), rep, axis=2)
    dt = jax.nn.softplus(dt_raw.astype(jnp.float32) + dt_bias.astype(jnp.float32))
    a = -jnp.exp(a_log.astype(jnp.float32))
    y = ssd_chunked(xs, dt, a, bm, cm) + xs * d_skip.astype(jnp.float32)[:, None]
    gsz = SSM_INNER // SSM_GROUPS
    y = y.reshape(bsz, s, SSM_GROUPS, gsz) * jax.nn.silu(z.astype(jnp.float32)).reshape(bsz, s, SSM_GROUPS, gsz)
    y = rms_norm_2(y, norm_g.reshape(SSM_GROUPS, gsz))
    return y.reshape(bsz, s, SSM_INNER)

def stick_breaking_attention(q, k, v):
    bsz, s, h, d = q.shape
    nblk = s // SB_BLOCK
    blk = SB_BLOCK

    def to_blocks(t):
        return t.astype(jnp.float32).reshape(bsz, nblk, blk, h, d).transpose(0, 3, 1, 2, 4)

    qb = to_blocks(q) * (d ** -0.5)
    kb = to_blocks(k)
    vb = to_blocks(v)
    idx = jnp.arange(blk)
    suffix = (idx[:, None] > idx[None, :]).astype(jnp.float32)
    diag_mask = idx[None, :] < idx[:, None]
    acc = jnp.zeros((bsz, h, nblk, blk), jnp.float32)
    out = jnp.zeros((bsz, h, nblk, blk, d), jnp.float32)
    for o in range(nblk):
        n = nblk - o
        z = jnp.einsum("bhnqd,bhnkd->bhnqk", qb[:, :, o:], kb[:, :, :n])
        log_beta = jax.nn.log_sigmoid(z)
        log_keep = log_beta - z
        if o == 0:
            log_keep = jnp.where(diag_mask, log_keep, 0.0)
        after = jnp.einsum("bhnqj,js->bhnqs", log_keep, suffix) + acc[:, :, o:, :, None]
        att = jnp.exp(log_beta + after)
        if o == 0:
            att = jnp.where(diag_mask, att, 0.0)
        out = out.at[:, :, o:].add(jnp.einsum("bhnqk,bhnkd->bhnqd", att, vb[:, :, :n]))
        acc = acc.at[:, :, o:].add(jnp.sum(log_keep, axis=-1))
    return out.transpose(0, 2, 3, 1, 4).reshape(bsz, s, h, d)

def stick_breaking_branch(qkv, q_norm_g, k_norm_g):
    bsz, s, _ = qkv.shape
    q, k, v = [t.reshape(bsz, s, SB_HEADS, SB_HEAD_DIM) for t in jnp.split(qkv, 3, axis=-1)]
    q = rms_norm_2(q, q_norm_g)
    k = rms_norm_2(k, k_norm_g)
    return stick_breaking_attention(q, k, v).reshape(bsz, s, SB_INNER)

def gated_delta_chunked(q, k, v, g, beta):
    bsz, s, h, dk = q.shape
    dv = v.shape[-1]
    nc = s // GDN_CHUNK
    cs = GDN_CHUNK

    def to_chunks(t):
        return t.reshape(bsz, nc, cs, h, t.shape[-1]).transpose(0, 3, 1, 2, 4)

    q = to_chunks(q * dk ** -0.5)
    k = to_chunks(k)
    v = to_chunks(v)
    g = g.reshape(bsz, nc, cs, h).transpose(0, 3, 1, 2)
    beta = beta.reshape(bsz, nc, cs, h).transpose(0, 3, 1, 2)
    g_cum = jnp.cumsum(g, axis=-1)
    tril_incl = jnp.tril(jnp.ones((cs, cs), bool))
    strict = jnp.tril(jnp.ones((cs, cs), bool), k=-1)
    decay = jnp.exp(jnp.where(tril_incl, g_cum[..., :, None] - g_cum[..., None, :], -jnp.inf))
    k_beta = k * beta[..., None]
    v_beta = v * beta[..., None]
    m = jnp.where(strict, jnp.einsum("bhncd,bhnsd->bhncs", k_beta, k) * decay, 0.0)
    t_mat = m + jnp.eye(cs, dtype=m.dtype)
    rhs = jnp.concatenate([v_beta, k_beta * jnp.exp(g_cum)[..., None]], axis=-1)
    sol = lax.linalg.triangular_solve(t_mat, rhs, left_side=True, lower=True, unit_diagonal=True)
    u, w = sol[..., :dv], sol[..., dv:]
    attn = jnp.where(tril_incl, jnp.einsum("bhncd,bhnsd->bhncs", q, k) * decay, 0.0)
    q_dec = q * jnp.exp(g_cum)[..., None]
    k_dec = k * jnp.exp(g_cum[..., -1:] - g_cum)[..., None]
    chunk_dec = jnp.exp(g_cum[..., -1])

    def step(state, inp):
        qd, kd, u_c, w_c, a_c, dec = inp
        v_new = u_c - jnp.einsum("bhcd,bhde->bhce", w_c, state)
        o = jnp.einsum("bhcd,bhde->bhce", qd, state) + jnp.einsum("bhcs,bhse->bhce", a_c, v_new)
        state = state * dec[..., None, None] + jnp.einsum("bhcd,bhce->bhde", kd, v_new)
        return state, o

    front = lambda t: t.transpose(2, 0, 1, 3, 4)
    s0 = jnp.zeros((bsz, h, dk, dv), q.dtype)
    _, o = lax.scan(step, s0, (front(q_dec), front(k_dec), front(u), front(w), front(attn), chunk_dec.transpose(2, 0, 1)))
    return o.transpose(1, 0, 3, 2, 4).reshape(bsz, s, h, dv)

def gated_deltanet_branch(qkv, a_raw, b_raw, gate, conv_w, a_log, dt_bias, norm_g):
    bsz, s, _ = qkv.shape
    qkv = jax.nn.silu(causal_conv(qkv, conv_w)).astype(jnp.float32)
    q, k, v = [t.reshape(bsz, s, GDN_HEADS, GDN_HEAD_DIM) for t in jnp.split(qkv, 3, axis=-1)]
    q = l2_norm(q)
    k = l2_norm(k)
    beta = jax.nn.sigmoid(b_raw.astype(jnp.float32))
    g = -jnp.exp(a_log.astype(jnp.float32)) * jax.nn.softplus(a_raw.astype(jnp.float32) + dt_bias.astype(jnp.float32))
    o = gated_delta_chunked(q, k, v, g, beta)
    o = rms_norm_2(o, norm_g) * jax.nn.silu(gate.astype(jnp.float32).reshape(bsz, s, GDN_HEADS, GDN_HEAD_DIM))
    return o.reshape(bsz, s, GDN_INNER)

def hier_moe(h, w_group, b_group, w_router, b_router, w_gate, w_up, w_down):
    n, d = h.shape
    hf = h.astype(jnp.float32)
    group_logits = hf @ w_group.astype(jnp.float32) + b_group.astype(jnp.float32)
    group_prob = jax.nn.softmax(group_logits, axis=-1)
    g_sel = jnp.argmax(group_logits, axis=-1)
    p_group = jnp.take_along_axis(group_prob, g_sel[:, None], axis=1)[:, 0]
    exp_logits = (hf @ w_router.astype(jnp.float32) + b_router.astype(jnp.float32)).reshape(n, MOE_GROUPS, EXPERTS_PER_GROUP)
    in_group = jnp.take_along_axis(exp_logits, g_sel[:, None, None], axis=1)[:, 0]
    top_p, top_i = lax.top_k(jax.nn.softmax(in_group, axis=-1), MOE_TOP_K)
    weights = p_group[:, None] * top_p / jnp.sum(top_p, axis=-1, keepdims=True)
    expert_ids = (g_sel[:, None] * EXPERTS_PER_GROUP + top_i).astype(jnp.int32)
    m = n * MOE_TOP_K
    flat_e = expert_ids.reshape(m)
    flat_tok = jnp.repeat(jnp.arange(n, dtype=jnp.int32), MOE_TOP_K)
    flat_w = weights.reshape(m)
    order = jnp.argsort(flat_e)
    sorted_e = flat_e[order]
    counts = jnp.zeros((N_EXPERTS,), jnp.int32).at[flat_e].add(1)
    padded = (counts + MOE_BLOCK - 1) // MOE_BLOCK * MOE_BLOCK
    start = jnp.cumsum(counts) - counts
    pend = jnp.cumsum(padded)
    pstart = pend - padded
    dest = pstart[sorted_e] + (jnp.arange(m, dtype=jnp.int32) - start[sorted_e])
    n_blocks = -(-m // MOE_BLOCK) + N_EXPERTS
    slot_tok = jnp.full((n_blocks * MOE_BLOCK,), n, jnp.int32).at[dest].set(flat_tok[order])
    slot_w = jnp.zeros((n_blocks * MOE_BLOCK,), jnp.float32).at[dest].set(flat_w[order])
    block_expert = jnp.minimum(jnp.searchsorted(pend, jnp.arange(n_blocks, dtype=jnp.int32) * MOE_BLOCK, side="right"), N_EXPERTS - 1)
    h_pad = jnp.concatenate([h, jnp.zeros((1, d), h.dtype)], axis=0)
    xb = h_pad[slot_tok].reshape(n_blocks, MOE_BLOCK, d)

    def expert_block(args):
        xi, e = args
        return (jax.nn.silu(xi @ w_gate[e]) * (xi @ w_up[e])) @ w_down[e]

    yb = lax.map(expert_block, (xb, block_expert)).reshape(n_blocks * MOE_BLOCK, d)
    y = jax.ops.segment_sum(yb * slot_w[:, None].astype(yb.dtype), slot_tok, num_segments=n + 1)
    return y[:n]

def second_inputs(seed: int = 0) -> dict:
    key = jax.random.key(seed)
    ks = jax.random.split(key, 32)
    f32 = jnp.float32
    L, D = DEPTH_2, D_MODEL

    def nrm(k, shape, scale):
        return jax.random.normal(k, shape, f32) * scale

    def gain(k, shape):
        return 1.0 + 0.02 * jax.random.normal(k, shape, f32)

    def dt_bias_init(k, shape):
        dt = jnp.exp(jax.random.uniform(k, shape, f32, math.log(1e-3), math.log(1e-1)))
        return dt + jnp.log(-jnp.expm1(-dt))

    return {
        "x": nrm(ks[0], (BATCH, SEQ, D), 1.0),
        "c": nrm(ks[1], (BATCH, D), 1.0),
        "w_ada": nrm(ks[2], (L, D, 6 * D), 0.5 * D ** -0.5),
        "b_ada": nrm(ks[3], (L, 6 * D), 0.02),
        "norm_mix": gain(ks[4], (L, D)),
        "norm_ffn": gain(ks[5], (L, D)),
        "w_in": nrm(ks[6], (L, D, IN_COLS), D ** -0.5),
        "ssm_conv_w": nrm(ks[7], (L, SSM_CONV, SSM_XBC), SSM_CONV ** -0.5),
        "ssm_conv_b": nrm(ks[8], (L, SSM_XBC), 0.01),
        "ssm_dt_bias": dt_bias_init(ks[9], (L, SSM_HEADS)),
        "ssm_a_log": jnp.log(jax.random.uniform(ks[10], (L, SSM_HEADS), f32, 1.0, 16.0)),
        "ssm_d": gain(ks[11], (L, SSM_HEADS)),
        "ssm_norm": gain(ks[12], (L, SSM_INNER)),
        "sb_q_norm": gain(ks[13], (L, SB_HEAD_DIM)),
        "sb_k_norm": gain(ks[14], (L, SB_HEAD_DIM)),
        "gdn_conv_w": nrm(ks[15], (L, GDN_CONV, 3 * GDN_INNER), GDN_CONV ** -0.5),
        "gdn_a_log": jnp.log(jax.random.uniform(ks[16], (L, GDN_HEADS), f32, 1.0, 16.0)),
        "gdn_dt_bias": dt_bias_init(ks[17], (L, GDN_HEADS)),
        "gdn_norm": gain(ks[18], (L, GDN_HEAD_DIM)),
        "w_branch": nrm(ks[19], (L, N_BRANCH, BRANCH_WIDTH, D), BRANCH_WIDTH ** -0.5),
        "w_out": nrm(ks[20], (L, D, D), D ** -0.5),
        "w_group": nrm(ks[21], (L, D, MOE_GROUPS), D ** -0.5),
        "b_group": nrm(ks[22], (L, MOE_GROUPS), 0.01),
        "w_router": nrm(ks[23], (L, D, N_EXPERTS), D ** -0.5),
        "b_router": nrm(ks[24], (L, N_EXPERTS), 0.01),
        "w_gate": nrm(ks[25], (L, N_EXPERTS, D, EXPERT_FF), D ** -0.5),
        "w_up": nrm(ks[26], (L, N_EXPERTS, D, EXPERT_FF), D ** -0.5),
        "w_down": nrm(ks[27], (L, N_EXPERTS, EXPERT_FF, D), EXPERT_FF ** -0.5),
    }

def second_block(x, c, w_ada, b_ada, norm_mix, norm_ffn, w_in, ssm_conv_w, ssm_conv_b, ssm_dt_bias, ssm_a_log, ssm_d,
              ssm_norm, sb_q_norm, sb_k_norm, gdn_conv_w, gdn_a_log, gdn_dt_bias, gdn_norm, w_branch, w_out,
              w_group, b_group, w_router, b_router, w_gate, w_up, w_down):
    bsz, s, d = x.shape
    split_points = np.cumsum(IN_SPLITS)[:-1].tolist()
    c_act = jax.nn.silu(c)
    for l in range(DEPTH_2):
        mod = c_act @ w_ada[l] + b_ada[l]
        shift_m, scale_m, gate_m, shift_f, scale_f, gate_f = [t[:, None, :] for t in jnp.split(mod, 6, axis=-1)]
        h = rms_norm_2(x, norm_mix[l]) * (1.0 + scale_m) + shift_m
        proj = h @ w_in[l]
        m_z, m_xbc, m_dt, sb_qkv, g_qkv, g_a, g_b, g_gate, br_gate = jnp.split(proj, split_points, axis=-1)
        y_a = mamba2_branch(m_z, m_xbc, m_dt, ssm_conv_w[l], ssm_conv_b[l], ssm_dt_bias[l], ssm_a_log[l], ssm_d[l], ssm_norm[l])
        y_b = stick_breaking_branch(sb_qkv, sb_q_norm[l], sb_k_norm[l])
        y_c = gated_deltanet_branch(g_qkv, g_a, g_b, g_gate, gdn_conv_w[l], gdn_a_log[l], gdn_dt_bias[l], gdn_norm[l])
        branches = jnp.stack([y_a.astype(x.dtype), y_b.astype(x.dtype), y_c.astype(x.dtype)], axis=2)
        branch_proj = jnp.einsum("bsie,ied->bsid", branches, w_branch[l])
        gates = jax.nn.sigmoid(br_gate.astype(jnp.float32)).astype(x.dtype).reshape(bsz, s, N_BRANCH, d)
        merged = jnp.sum(gates * branch_proj, axis=2)
        x = x + gate_m * (merged @ w_out[l])
        h = rms_norm_2(x, norm_ffn[l]) * (1.0 + scale_f) + shift_f
        y = hier_moe(h.reshape(bsz * s, d), w_group[l], b_group[l], w_router[l], b_router[l], w_gate[l], w_up[l], w_down[l])
        x = x + gate_f * y.reshape(bsz, s, d)
    return x


def setup_inputs(seed=0):
    out = dict(first_inputs(seed))
    for name, value in second_inputs(seed + 1).items():
        if name != "x":
            out[name + "_2"] = value
    return out


def reference(
    x, even_norm_g, even_w_in, even_b_in, even_v_ln_g, even_v_ln_b, even_w_s, even_b_s,
    even_conv_w, even_conv_b, even_conv_ln_g, even_conv_ln_b, even_w_out, odd_norm_g, odd_w_qkv,
    odd_w_o, ffn_norm_g, ffn_w_up, ffn_conv_w, ffn_conv_b, ffn_w_down, final_norm_g, c_2,
    w_ada_2, b_ada_2, norm_mix_2, norm_ffn_2, w_in_2, ssm_conv_w_2, ssm_conv_b_2, ssm_dt_bias_2,
    ssm_a_log_2, ssm_d_2, ssm_norm_2, sb_q_norm_2, sb_k_norm_2, gdn_conv_w_2, gdn_a_log_2,
    gdn_dt_bias_2, gdn_norm_2, w_branch_2, w_out_2, w_group_2, b_group_2, w_router_2,
    b_router_2, w_gate_2, w_up_2, w_down_2,
):
    x = first_block(
        x, even_norm_g, even_w_in, even_b_in, even_v_ln_g, even_v_ln_b, even_w_s, even_b_s,
        even_conv_w, even_conv_b, even_conv_ln_g, even_conv_ln_b, even_w_out, odd_norm_g,
        odd_w_qkv, odd_w_o, ffn_norm_g, ffn_w_up, ffn_conv_w, ffn_conv_b, ffn_w_down,
        final_norm_g,
    )
    return second_block(
        x, c_2, w_ada_2, b_ada_2, norm_mix_2, norm_ffn_2, w_in_2, ssm_conv_w_2, ssm_conv_b_2,
        ssm_dt_bias_2, ssm_a_log_2, ssm_d_2, ssm_norm_2, sb_q_norm_2, sb_k_norm_2, gdn_conv_w_2,
        gdn_a_log_2, gdn_dt_bias_2, gdn_norm_2, w_branch_2, w_out_2, w_group_2, b_group_2,
        w_router_2, b_router_2, w_gate_2, w_up_2, w_down_2,
    )


_drawn_inputs = setup_inputs


def setup_inputs(seed=0):
    import zlib

    import numpy as np

    out = dict(_drawn_inputs(seed))
    spreads = {}
    factors = {'even_b_in': 2.859,
     'even_v_ln_g': 6.631,
     'even_v_ln_b': 7.511,
     'even_b_s': 4.526,
     'even_conv_ln_g': 4.176,
     'even_conv_ln_b': 5.17,
     'odd_norm_g': 6.122,
     'ffn_norm_g': 2.906,
     'ffn_conv_b': 2.672,
     'norm_mix_2': 7.35,
     'norm_ffn_2': 6.083,
     'ssm_conv_b_2': 32.589,
     'ssm_d_2': 64.0,
     'ssm_norm_2': 29.573,
     'sb_q_norm_2': 8.0,
     'sb_k_norm_2': 8.0,
     'gdn_norm_2': 8.0,
     'b_group_2': 64.0,
     'b_router_2': 8.0}
    for name, (base, spread) in spreads.items():
        noise = np.random.default_rng([zlib.crc32(name.encode()), seed]).standard_normal(out[name].shape)
        drawn = base * np.exp(spread * noise) if base else spread * noise
        out[name] = jnp.asarray(drawn.astype(out[name].dtype))
    for name, factor in factors.items():
        out[name] = (out[name] * factor).astype(out[name].dtype)
    return out
```

```python
from contextlib import ExitStack

import numpy as np

import concourse.bass as bass
from concourse import mybir

F32 = mybir.dt.float32
I32 = mybir.dt.int32
ALU = mybir.AluOpType
ACT = mybir.ActivationFunctionType
AX = mybir.AxisListType.X
ds = bass.ds

P = 128
T = 256
NT = T // P
D = 1024
KD = D // P
HALF = 512
KH = HALF // P
CONV = 31
FF = 2816
KF = FF // P
HEADS = 16
HD = 64
EPS = 1e-6
NEG = -1e30
RING = 4
E = 32
EG = 4
SLOTS = 64
PASSES = T // SLOTS
NE = E * PASSES

Z0, XBC0, DT0, SB0, GQ0, GAB0, GG0, BR0 = 0, 512, 1536, 1544, 3080, 4616, 4624, 5136


def col_layout():
    sizes = [("even_norm", 8), ("b_in", 16), ("vln_g", 4), ("vln_b", 4), ("conv_w", CONV * 4), ("conv_b", 4),
             ("cln_g", 4), ("cln_b", 4), ("odd_norm", 8), ("ffn_norm", 16), ("ffn_cw", 2 * 3 * 44),
             ("ffn_cb", 2 * 44), ("final_norm", 8), ("c", 8), ("b_ada", 48), ("norm_mix", 8), ("norm_ffn", 8),
             ("ssm_cw", 32), ("ssm_cb", 8), ("ssm_norm", 4), ("ssm_d", 4), ("sb_qn", 1), ("sb_kn", 1),
             ("gdn_cw", 48), ("gdn_norm", 1)]
    at, out = 0, {}
    for name, n in sizes:
        out[name] = (at, n)
        at += n
    return out, at


def const_arrays():
    j = np.arange(P)[:, None]
    t = np.arange(P)[None, :]
    same = (j // 64) == (t // 64)
    d = np.arange(P) % HD
    inv = (10000.0 ** (-np.arange(HD // 2, dtype=np.float32) / np.float32(HD // 2))).astype(np.float32)
    ang = (np.arange(T, dtype=np.float32)[None, :] * inv[d % 32][:, None]).astype(np.float32)
    swap = np.zeros((P, P), np.float32)
    for p in range(P):
        if p % HD < 32:
            swap[p + 32, p] = -1.0
        else:
            swap[p - 32, p] = 1.0

    def pattern_bias(q0, k0):
        q = q0 + np.arange(P)[:, None]
        k = k0 + np.arange(P)[None, :]
        n = np.zeros((P, P))
        for dil in (1, 4, 16):
            n += (k <= q) & ((q - k) % dil == 0) & ((q - k) // dil <= P)
        return np.where(n > 0, np.log(np.maximum(n, 1)), NEG)

    out = {
        "ident": j == t, "ones": np.ones((P, P)), "mean512": np.full((P, P), 1.0 / HALF),
        "upto": j <= t, "before": j < t, "after": j > t,
        "cos": np.cos(ang), "sin": np.sin(ang), "swap": swap,
        "bias00": pattern_bias(0, 0), "bias10": pattern_bias(P, 0), "bias11": pattern_bias(P, P),
        "neg_causal": np.where(j <= t, 0.0, NEG),
        "upto64": (j <= t) & same, "ones64": same, "neg_causal64": np.where((j <= t) & same, 0.0, NEG),
        "before64": (j < t) & same,
        "iota": np.tile(np.arange(P) % SLOTS, (P, 1)), "iota_e": np.tile(np.arange(E), (P, 1)),
        "diag32": (j % 32) == np.arange(32)[None, :],
        "eps": np.full((P, 1), EPS), "one": np.ones((P, 1)),
        "pass_shift": np.tile(np.repeat(SLOTS * np.arange(PASSES), E), (P, 1)),
    }
    for n in range(6):
        b = 1 << n
        low = (j // (2 * b) == t // (2 * b)) & (j // b % 2 == 1) & (t // b % 2 == 0)
        out[f"low{n}"] = low
        out[f"lowT{n}"] = low.T
    return {k: np.ascontiguousarray(v, dtype=np.float32) for k, v in out.items()}


ROWS = {"b_s": (0, 1024), "b_route": (1024, 36), "dt_bias": (1060, 8), "gdn_dt_bias": (1068, 4),
        "a_log": (1072, 8), "gdn_a_log": (1080, 4)}
NROWS = 1084


class Seen:

    def __init__(self):
        self.n = {}

    def __call__(self, sem, k=1):
        self.n[sem.name] = self.n.get(sem.name, 0) + k
        return self.now(sem)

    def now(self, sem):
        return self.n.get(sem.name, 0)


class Arena:

    def __init__(self, tensor, size):
        self.t, self.at, self.size = tensor, 0, size

    def take(self, n):
        self.at += n
        assert self.at <= self.size, self.at
        return self.t[:, self.at - n:self.at]


def program(nc, A, out):
    cols, ncols = col_layout()
    consts = const_arrays()
    ctx = ExitStack()
    with ctx:
        def sb(name, shape, dt=F32):
            return ctx.enter_context(nc.sbuf_tensor(name, shape, dt))

        def sem(name):
            return ctx.enter_context(nc.semaphore(name))

        x = sb("x", [P, KD, T])
        h = sb("h", [P, KD, T])
        sq = sb("sq", [P, KD, T])
        rs = sb("rs", [P, 4, T])
        cat = sb("cat", [P, KD, T])
        ring = sb("ring", [P, RING, D])
        colp = sb("colp", [P, ncols])
        nconst = sum(v.shape[1] for v in consts.values())
        cst = sb("cst", [P, nconst])
        rows = sb("rows", [P, NROWS])
        mod = sb("mod", [P, 48])
        gains = sb("gains", [P, 2 * KD])
        c_act = sb("c_act", [P, KD])
        ARENA = 33008
        arena_t = sb("arena", [P, ARENA])
        K, at = {}, 0
        for name, v in consts.items():
            K[name] = cst[:, at:at + v.shape[1]]
            at += v.shape[1]

        def col(name, i=0, n=1):
            a = cols[name][0] + i
            return colp[:, a:a + n]

        def row(name):
            a, m = ROWS[name]
            return rows[:, a:a + m]

        lin = [ctx.enter_context(nc.psum_tensor(f"lin{b}", [P, 512], F32)) for b in range(4)]
        stat = ctx.enter_context(nc.psum_tensor("stat", [P, 4, T], F32))
        mixp = ctx.enter_context(nc.psum_tensor("mixp", [P, 4, T], F32))

        consts_loaded = sem("consts_loaded")
        extra_loaded = sem("extra_loaded")
        panel_loaded = [sem(f"panel_loaded{b}") for b in range(RING)]
        panel_done = sem("panel_done")
        bank_free = [sem(f"bank_free{b}") for b in range(4)]
        sq_ready = sem("sq_ready")
        sums_ready = sem("sums_ready")
        ln_done = sem("ln_done")
        rs_ready = sem("rs_ready")
        mean_ready = sem("mean_ready")
        centred = sem("centred")
        h_ready = sem("h_ready")
        dve_step = sem("dve_step")
        act_step = sem("act_step")
        tap0_done = sem("tap0_done")
        silu_done = sem("silu_done")
        act_tile = sem("act_tile")
        conv_step = sem("conv_step")
        v_normed = sem("v_normed")
        vt_ready = sem("vt_ready")
        vt_copied = sem("vt_copied")
        mixed_ready = sem("mixed_ready")
        ya_ready = sem("ya_ready")
        yb_normed = sem("yb_normed")
        yb_ready = sem("yb_ready")
        rot_ready = sem("rot_ready")
        qk_ready = sem("qk_ready")
        vt1_ready = sem("vt1_ready")
        vt1_copied = sem("vt1_copied")
        scores_ready = sem("scores_ready")
        scores_read = sem("scores_read")
        max_ready = sem("max_ready")
        exp_ready = sem("exp_ready")
        probs_ready = sem("probs_ready")
        pt_ready = sem("pt_ready")
        pt_copied = sem("pt_copied")
        o_ready = sem("o_ready")
        o_copied = sem("o_copied")
        stored = sem("stored")
        events = {}

        def ev(name):
            if name not in events:
                events[name] = sem(name)
            return events[name]

        wsmall = sb("wsmall", [P, KD, 52])
        S2 = Arena(arena_t, ARENA)

        def buf(*shape, of=None):
            n = int(np.prod(shape))
            ap = (of or S2).take(n)
            names = "abcd"[:len(shape)]
            return ap if len(shape) == 1 else ap.rearrange(
                f"p ({' '.join(names)}) -> p {' '.join(names)}", **{k: s for k, s in zip(names[1:], shape[1:])})

        xb = buf(8, T)
        zs = buf(KH, T)
        gq = buf(12, T)
        gg = buf(KH, T)
        sq_kv = buf(12, T)
        ybr = buf(12, T)
        spin, spl, spe = buf(NT, 12), buf(NT, 12), buf(NT, 12)
        adt = buf(NT, 12)
        beta, beta_in, eg, beg, kdec = (buf(NT, 4) for _ in range(5))
        ea = buf(12)
        cums = buf(NT, 24)
        mdec, mdif, gdif = buf(NT, 8), buf(NT, 8), buf(NT, 4)
        qn = buf(1)
        g_kt, g_vt, g_er, g_kb, g_qd, g_dec, g_mt, g_at, g_d, g_dt, g_w, g_ml, g_r2 = (buf(4, T) for _ in range(13))
        g_s = buf(4, P)
        mark = S2.at
        m_xt, m_bt, m_xdd, m_g = buf(NT, HALF), buf(T), buf(HALF), buf(2, T)
        m_er, m_cd, m_h = buf(8, P), buf(8, P), buf(HALF)
        m_seg = cat
        S2.at = mark
        b_vt, b_l, b_lb, b_nk = buf(NT, HALF), buf(4, 3 * P), buf(4, 3 * P), buf(4, 3 * P)
        merged = cat
        S2.at = mark
        gates8, gtmp = buf(8, T), buf(T)

        def zbanks(k):
            ps = (mixp, stat)[k][:, :, :].rearrange("p (b a) t -> p b (a t)", b=2)
            return ps[:, :, 0:3 * P]


        a = Arena(arena_t, ARENA)
        e_wg, e_wu = buf(2, KD, HALF, of=a), buf(2, KD, HALF, of=a)
        e_wd = buf(2, KH, D, of=a)
        h_tm = buf(NT, D, of=a)
        e_sel, e_selw = buf(2, NT, SLOTS, of=a), buf(2, NT, P, of=a)
        e_hg, e_hgT_flat, e_sg, e_hid, e_yb = buf(512, of=a), buf(512, of=a), buf(T, of=a), buf(T, of=a), buf(512, of=a)
        e_hgT = e_hgT_flat.rearrange("p (j h s) -> p j h s", j=4, h=2)
        e_dT = buf(512, of=a)
        e_hidT = e_dT[:, 0:T].rearrange("p (j h s) -> p j h s", j=2, h=2)
        rankp, wp = buf(NT, NE + 2, of=a), buf(NT, NE + 2, of=a)
        r_lg, r_ml, r_oh1, r_oh2, assign, r_rank = (buf(NT, n, of=a) for n in (36, E, E, E, E, E))
        r_goh, r_ge = buf(NT, EG, of=a), buf(NT, EG, of=a)
        r_best, r_at, r_m1, r_m2, r_e2, r_pg, r_w1, r_w2 = (buf(NT, of=a) for _ in range(8))
        r_cnt = buf(1, of=a)
        flag_i = ctx.enter_context(nc.sbuf_tensor("flag_i", [P, 1], I32))[:, :]
        M = {n: sem(f"moe_{n}") for n in ("gu_loaded0", "gu_loaded1", "d_loaded0", "d_loaded1", "sel", "selw", "hg", "hgT",
                                          "silu", "hid", "dT", "yb", "A", "B", "C", "D", "E", "F", "y", "flag")}

        class Panels:

            def __init__(self, eng):
                self.eng, self.n, self.free = eng, 0, [0] * 4

            def done(self, j=0, it=None, per=RING):
                self.eng.wait_ge(panel_done, self.n + j + 1 if it is None else it * per + (self.n + j + 1))
                return (self.n + j) % RING

            def taken(self, j, it=None, per=1):
                b = (self.n + j) % RING
                v = self.free[b] + j // RING + 1
                self.eng.wait_ge(bank_free[b], v if it is None else it * per + v)

            def advance(self, k):
                for _ in range(k):
                    self.free[self.n % RING] += 1
                    self.n += 1

            def advance_down(self):
                self.n += KF
                self.free = [f + 1 for f in self.free]

            def settled(self):
                for b in range(4):
                    self.eng.wait_ge(bank_free[b], self.free[b])

        def panel_src(w, m, k=KD):
            return w.rearrange("(k p) n -> p k n", p=P)[:, 0:k, ds(m * P, P)]

        a = Arena(arena_t, ARENA)
        PADC = CONV - 1
        u0 = a.take(KH * T).rearrange("p (k t) -> p k t", k=KH)
        v0 = a.take(KH * T).rearrange("p (k t) -> p k t", k=KH)
        sg0 = a.take(KH * T).rearrange("p (k t) -> p k t", k=KH)
        hc0 = a.take(KH * (T + PADC)).rearrange("p (k t) -> p k t", k=KH)
        cv0 = a.take(KH * T).rearrange("p (k t) -> p k t", k=KH)
        xc0 = a.take(KH * T).rearrange("p (k t) -> p k t", k=KH)
        vt0 = a.take(NT * HALF).rearrange("p (c f) -> p c f", c=NT)
        ws0 = a.take(8 * P).rearrange("p (h t) -> p h t", h=8)
        wsm0 = a.take(8 * P).rearrange("p (h t) -> p h t", h=8)
        modraw = a.take(48 * 32).rearrange("p (n c) -> p n c", n=48)
        modsel = a.take(48 * 32).rearrange("p (n c) -> p n c", n=48)

        a = Arena(arena_t, ARENA)
        hid = a.take(KF * T).rearrange("p (k t) -> p k t", k=KF)
        ub = a.take(4 * T).rearrange("p (k t) -> p k t", k=4)
        sgf = a.take(2 * T).rearrange("p (k t) -> p k t", k=2)

        a = Arena(arena_t, ARENA)
        qk1 = a.take(16 * T).rearrange("p (k t) -> p k t", k=16)
        qs1 = a.take(2 * T).rearrange("p (k t) -> p k t", k=2)
        rc1 = a.take(2 * T).rearrange("p (k t) -> p k t", k=2)
        v1 = a.take(8 * T).rearrange("p (k t) -> p k t", k=8)
        vt1 = a.take(NT * D).rearrange("p (c f) -> p c f", c=NT)
        SC = 3 * P
        s1 = a.take(4 * SC).rearrange("p (b s) -> p b s", b=4)
        p1 = a.take(4 * SC).rearrange("p (b s) -> p b s", b=4)
        pt1 = a.take(4 * SC).rearrange("p (b s) -> p b s", b=4)
        mx1 = a.take(2 * HEADS)
        l1 = a.take(2 * HEADS)
        r1 = a.take(2 * HEADS)

        block = ctx.enter_context(nc.Block())

        def statbank(n):
            return stat[:, 2 * (n % 2):2 * (n % 2) + 2, :].rearrange("p a t -> p (a t)")

        def mixbank(n):
            return mixp[:, 2 * (n % 2):2 * (n % 2) + 2, :].rearrange("p a t -> p (a t)")

        @block.sync
        def _(sp):
            seen = Seen()
            n_panels = [0]
            panels_seen = Panels(sp)

            def load_panel(dst_shape, src, j=None, it=None, per=RING):
                n = n_panels[0] + (j or 0)
                slot = n % RING
                dst = ring[:, slot, :]
                if dst_shape is not None:
                    dst = dst[:, 0:dst_shape[0] * dst_shape[1]].rearrange("p (k n) -> p k n", k=dst_shape[0])
                if it is not None:
                    sp.wait_ge(panel_done, it * per + (n - RING + 1))
                elif n >= RING:
                    sp.wait_ge(panel_done, n - RING + 1)
                sp.dma_start(dst, src).then_inc(panel_loaded[slot], 16)
                if it is None:
                    n_panels[0] += 1

            def load_columns(w, tiles, k=KD):
                for m in tiles:
                    load_panel((k, P), panel_src(w, m, k))

            sp.dma_start(colp[:, :], A["cols"]).then_inc(consts_loaded, 16)
            sp.dma_start(x[:, :, :], A["x"]).then_inc(consts_loaded, 16)
            sp.dma_start(cst[:, :], A["consts"]).then_inc(consts_loaded, 16)
            for j in range(4):
                load_columns(A["even_w_in"], [12 + j, 8 + j])
                if j == 0:
                    sp.dma_start(rows[:, :], A["rows"].partition_broadcast(P)).then_inc(extra_loaded, 16)
                    sp.dma_start(ws0[:, :, :], A["even_w_s"]).then_inc(extra_loaded, 16)
                    sp.dma_start(wsmall[:, :, :], A["w_small"]).then_inc(extra_loaded, 16)
            load_columns(A["even_w_in"], range(4, 8))
            load_columns(A["even_w_in"], range(0, 4))
            panels_seen.advance(16 + 48)
            with sp.Fori(0, 12) as it:
                for j in range(4):
                    load_panel((KD, P), A["w_ada"].rearrange("(k p) n -> p k n", p=P)[:, :, ds(it * 512 + j * P, P)],
                               j, it)
            n_panels[0] += 48
            load_columns(A["even_w_out"], range(8))
            panels_seen.advance(8)

            def load_ffn(l):
                up = A["ffn_w_up"][l].rearrange("(k p) n -> p k n", p=P)
                with sp.Fori(0, KF // 2) as it:
                    for j in range(4):
                        load_panel((KD, P), up[:, :, ds(it * 2 * P + (j // 2) * P + (j % 2) * FF, P)], j, it)
                n_panels[0] += 2 * KF
                down = A["ffn_w_down"][l].rearrange("(k p) n -> p k n", p=P)
                for k in (0, 1):
                    load_panel(None, down[:, k, :])
                with sp.Fori(0, 4) as it:
                    for j in range(4):
                        load_panel(None, down[:, ds(it * 4 + j + 2, 1), :].rearrange("p k n -> p (k n)"), j, it)
                n_panels[0] += 16
                for k in range(18, 22):
                    load_panel(None, down[:, k, :])
                panels_seen.advance(2 * KF)
                panels_seen.advance_down()

            load_ffn(0)
            load_columns(A["odd_w_qkv"], range(24))
            load_columns(A["odd_w_o"], range(8))
            panels_seen.advance(24 + 8)
            load_ffn(1)
            load_columns(A["w_in"][:, XBC0:DT0], range(8))
            load_columns(A["w_in"][:, Z0:XBC0], range(4))
            load_columns(A["w_in"][:, GQ0:GAB0], range(12))
            load_columns(A["w_in"][:, GG0:BR0], range(4))
            load_columns(A["w_in"][:, SB0:GQ0], range(12))
            panels_seen.advance(40)
            gates = A["w_in"][:, BR0:].rearrange("(k p) n -> p k n", p=P)
            branch = A["w_branch"].rearrange("i (k p) n -> p i k n", p=P)
            with sp.Fori(0, 3) as it:
                for j in range(12):
                    pair, part = j // 3, j % 3
                    if part == 0:
                        src = branch[:, ds(it, 1), :, pair * T:(pair + 1) * T].rearrange("p i k n -> p (i k) n")
                        load_panel((KH, T), src, j, it, 12)
                    else:
                        load_panel((KD, P), gates[:, :, ds(it * D + (2 * pair + part - 1) * P, P)], j, it, 12)
            n_panels[0] += 36
            load_columns(A["w_out"], range(8))
            panels_seen.advance(36)
            panels_seen.settled()
            gate_w = A["w_gate"].rearrange("e (k p) f -> p e k f", p=P)
            up_w = A["w_up"].rearrange("e (k p) f -> p e k f", p=P)
            down_w = A["w_down"].rearrange("e (k p) f -> p e k f", p=P)

            def load_expert(e, s, before=None):
                if before is not None:
                    sp.wait_ge(M["C"], before)
                sp.dma_start(e_wg[:, s, :, :], gate_w[:, e, :, :].rearrange("p e k f -> p (e k) f")).then_inc(M[f"gu_loaded{s}"], 16)
                sp.dma_start(e_wu[:, s, :, :], up_w[:, e, :, :].rearrange("p e k f -> p (e k) f")).then_inc(M[f"gu_loaded{s}"], 16)
                if before is not None:
                    sp.wait_ge(M["E"], before)
                sp.dma_start(e_wd[:, s, :, :], down_w[:, e, :, :].rearrange("p e k f -> p (e k) f")).then_inc(M[f"d_loaded{s}"], 16)

            for s in range(2):
                load_expert(slice(s, s + 1), s)
            with sp.Fori(1, E // 2) as it:
                for s in range(2):
                    load_expert(ds(it * 2 + s, 1), s, it * 2 + (s - 1))
            sp.wait_ge(M["flag"], 1)
            more = sp.value_load(flag_i[0:1, 0:1], min_val=0, max_val=1)
            with sp.If(more == 1):
                for p in range(1, PASSES):
                    with sp.Fori(0, E // 2) as it:
                        for s in range(2):
                            load_expert(ds(it * 2 + s, 1), s, it * 2 + (s - 1 + p * E))
            for half in range(2):
                sp.wait_ge(ev("x_out"), 4 * half + 4)
                sp.dma_start(out[:, 4 * half:4 * half + 4, :], x[:, 4 * half:4 * half + 4, :]).then_inc(stored, 16)
            sp.wait_ge(stored, 32)

        @block.tensor
        def _(pe):
            seen = Seen()
            panels = Panels(pe)

            def panel(j=0, it=None, per=RING):
                n = panels.n + j
                v = 16 * (n // RING + 1)
                pe.wait_ge(panel_loaded[n % RING], v if it is None else it * (16 * per // RING) + v)
                return n % RING

            def bank(b, it=None, per=1, later=0):
                v = panels.free[b] + later
                if it is not None:
                    pe.wait_ge(bank_free[b], it * per + v)
                elif v:
                    pe.wait_ge(bank_free[b], v)

            def product(b, rhs, k=KD):
                w = ring[:, b, 0:k * P].rearrange("p (k n) -> p k n", k=k)
                for i in range(k):
                    mm = pe.matmul(lin[b][:, 0:T], w[:, i, :], rhs[:, i, :], start=i == 0, stop=i == k - 1)
                mm.then_inc(panel_done, 1)

            def linear(rhs, count, k=KD):
                for _ in range(count):
                    b = panel()
                    bank(b)
                    product(b, rhs, k)
                    panels.advance(1)

            def sums(src, groups, k):
                pe.wait_ge(sq_ready, seen(sq_ready))
                if seen.now(ln_done):
                    pe.wait_ge(ln_done, seen.now(ln_done))
                for g in range(groups):
                    for i in range(k):
                        mm = pe.matmul(stat[:, g, :], K["ones"], src[:, g * k + i, :], start=i == 0, stop=i == k - 1,
                                       skip_group_check=True)
                mm.then_inc(sums_ready, 1)
                seen(ln_done)

            def mean(src, n):
                for i in range(KH):
                    mm = pe.matmul(mixp[:, 2 * n, :], K["mean512"], src[:, i, :], start=i == 0, stop=i == KH - 1)
                mm.then_inc(mean_ready, 1)

            def ffn():
                sums(sq, 1, KD)
                pe.wait_ge(h_ready, seen(h_ready))
                with pe.Fori(0, KF // 2) as it:
                    for j in range(4):
                        b = panel(j, it)
                        bank(b, it)
                        product(b, h)
                panels.advance(2 * KF)
                pe.wait_ge(act_tile, seen(act_tile, KF))
                panels.settled()

                def down(b, rhs, first, last):
                    for m in range(KD):
                        mm = pe.matmul(lin[m // 2][:, (m % 2) * T:(m % 2 + 1) * T], ring[:, b, m * P:(m + 1) * P],
                                       rhs, start=first and m % 2 == 0, stop=last, skip_group_check=True)
                    mm.then_inc(panel_done, 1)

                for k in (0, 1):
                    down(panel(k), hid[:, k, :], k == 0, False)
                with pe.Fori(0, 4) as it:
                    for j in range(4):
                        down(panel(j + 2, it), hid[:, ds(it * 4 + (j + 2), 1), :].rearrange("p k t -> p (k t)"), False, False)
                for k in range(18, KF):
                    down(panel(k), hid[:, k, :], False, k == KF - 1)
                panels.advance_down()

            seen(act_tile)
            pe.wait_ge(consts_loaded, 48)
            sums(sq, 1, KD)
            pe.wait_ge(h_ready, seen(h_ready))
            linear(h, 16)
            panels.settled()
            mean(v0, 0)
            pe.wait_ge(silu_done, seen(silu_done))
            with pe.Fori(0, 12) as it:
                for j in range(4):
                    b = panel(j, it)
                    bank(b, it)
                    w = ring[:, b, :].rearrange("p (k n) -> p k n", k=KD)
                    for i in range(KD):
                        for q in range(4):
                            mm = pe.matmul(lin[b][32 * q:32 * q + 32, 0:32], c_act[:, i:i + 1].to_broadcast([P, 32]),
                                           w[:, i, 32 * q:32 * q + 32], start=i == 0, stop=i == KD - 1,
                                           skip_group_check=True)
                    mm.then_inc(panel_done, 1)
            panels.advance(48)
            sums(sq, 1, KH)
            pe.wait_ge(v_normed, 1)
            for c in range(NT):
                for j in range(KH):
                    mm = pe.transpose(mixbank(c)[:, j * P:(j + 1) * P], v0[:, j, c * P:(c + 1) * P], K["ident"])
                mm.then_inc(vt_ready, 1)
            pe.wait_ge(vt_copied, 2)
            for hh in range(8):
                for c in range(NT):
                    mm = pe.matmul(mixp[64 * (hh % 2):64 * (hh % 2) + 64, hh // 2, c * P:(c + 1) * P],
                                   vt0[:, c, hh * HD:(hh + 1) * HD], wsm0[:, hh, :], start=True, stop=True,
                                   skip_group_check=True)
            mm.then_inc(mixed_ready, 1)
            pe.wait_ge(conv_step, CONV * KH)
            pe.wait_ge(ya_ready, 1)
            mean(cv0, 1)
            sums(sq, 1, KH)
            pe.wait_ge(yb_ready, 1)
            linear(cat, 8)
            ffn()
            sums(sq, 1, KD)
            pe.wait_ge(h_ready, seen(h_ready))

            def swap_halves(n):
                b = (qk_first + n) % 4
                pe.wait_ge(bank_free[b], panels.free[b])
                if n >= 2:
                    pe.wait_ge(qk_ready, n - 1)
                pe.matmul(stat[:, 2 * (n % 2), :], K["swap"], qs1[:, n % 2, :], start=True, stop=True)\
                    .then_inc(rot_ready, 1)

            qk_first = panels.n
            for n in range(16):
                linear(h, 1)
                if n:
                    swap_halves(n - 1)
            linear(h, 1)
            swap_halves(15)
            linear(h, 7)
            panels.settled()
            for g in range(4):
                if g >= 2:
                    pe.wait_ge(vt1_copied, g - 1)
                for i in range(4):
                    mm = pe.transpose(mixbank(g)[:, i * P:(i + 1) * P],
                                      v1[:, (g % 2) * 4 + i, (g // 2) * P:(g // 2 + 1) * P], K["ident"])
                mm.then_inc(vt1_ready, 1)
            pe.wait_ge(vt1_copied, 4)
            pe.wait_ge(qk_ready, 16)
            for i in range(HEADS + 2):
                if i < HEADS:
                    if i >= 2:
                        pe.wait_ge(scores_read, i - 1)
                    o = 64 * (i % 2)
                    q, k = qk1[o:o + 64, i // 2, :], qk1[o:o + 64, 8 + i // 2, :]
                    pe.matmul(mixbank(i)[:, 0:P], q[:, 0:P], k[:, 0:P], start=True, stop=True, skip_group_check=True)
                    pe.matmul(mixbank(i)[:, P:3 * P], q[:, P:T], k, start=True, stop=True, skip_group_check=True)\
                        .then_inc(scores_ready, 1)
                if 1 <= i <= HEADS:
                    g = i - 1
                    pe.wait_ge(probs_ready, g + 1)
                    if g >= 2:
                        pe.wait_ge(pt_copied, g - 1)
                    for c in range(3):
                        mm = pe.transpose(statbank(g)[:, c * P:(c + 1) * P], p1[:, g % 4, c * P:(c + 1) * P], K["ident"])
                    mm.then_inc(pt_ready, 1)
                if i >= 2:
                    g = i - 2
                    pe.wait_ge(pt_copied, g + 1)
                    if g >= 8 and g % 2 == 0:
                        pe.wait_ge(o_copied, g // 2 - 3)
                    o = lin[(g // 2) % 4][64 * (g % 2):64 * (g % 2) + 64, :]
                    v = [vt1[:, c, g * HD:(g + 1) * HD] for c in range(NT)]
                    pe.matmul(o[:, 0:P], v[0], pt1[:, g % 4, 0:P], start=True, stop=True, skip_group_check=True)
                    pe.matmul(o[:, P:T], v[0], pt1[:, g % 4, P:2 * P], start=True, stop=False, skip_group_check=True)
                    pe.matmul(o[:, P:T], v[1], pt1[:, g % 4, 2 * P:3 * P], start=False, stop=True, skip_group_check=True)\
                        .then_inc(o_ready, 1)
            pe.wait_ge(o_copied, 8)
            linear(cat, 8)
            ffn()
            sums(sq, 1, KD)
            sums(sq, 1, KD)
            pe.wait_ge(h_ready, seen(h_ready))
            pe.wait_ge(extra_loaded, 48)
            for c in range(NT):
                for i in range(KD):
                    mm = pe.matmul(mixbank(0)[:, c * 16:(c + 1) * 16], h[:, i, c * P:(c + 1) * P], wsmall[:, i, 0:16],
                                   start=i == 0, stop=i == KD - 1, skip_group_check=True)
            mm.then_inc(ev("small_ready"), 1)
            linear(h, 8)
            pe.wait_ge(ev("adt_ready"), 1)
            for c in range(NT):
                for a0, lhs, b0, n in ((0, "upto", 0, 8), (8, "upto64", 8, 4), (12, "ones64", 8, 4), (16, "ones", 0, 8)):
                    mm = pe.matmul(mixbank(1)[:, c * 24 + a0:c * 24 + a0 + n], K[lhs], adt[:, c, b0:b0 + n],
                                   start=True, stop=True, skip_group_check=True)
            mm.then_inc(ev("cums_ready"), 1)
            linear(h, 32)

            def spread(dst, src, table):
                for i in range(4):
                    for c in range(NT):
                        mm = pe.matmul(dst[:, i, c * P:(c + 1) * P], src(i, c).to_broadcast([P, P]), table,
                                       start=True, stop=True, skip_group_check=True)
                return mm

            def turned(dst, pairs, event):
                for i, s in enumerate(pairs):
                    mm = pe.transpose(dst[:, i * P:(i + 1) * P], s, K["ident"])
                mm.then_inc(event, 1)

            pe.wait_ge(ev("xb_ready"), 1)
            pe.wait_ge(ev("cums_copied"), 1)
            for c in range(NT):
                turned(mixbank(c), [xb[:, j, c * P:(c + 1) * P] for j in range(4)], ev("m_xt_turned"))
            turned(statbank(0), [xb[:, 4 + g, 0:P] for g in range(2)], ev("m_bt_turned"))
            for g in range(2):
                for c in range(NT):
                    mm = pe.matmul(statbank(1)[:, g * T + c * P:g * T + (c + 1) * P], xb[:, 4 + g, c * P:(c + 1) * P],
                                   xb[:, 6 + g, c * P:(c + 1) * P], start=True, stop=True, skip_group_check=True)
            mm.then_inc(ev("m_g_ready"), 1)
            pe.wait_ge(ev("m_xt_copied"), 2)
            spread(mixp, lambda i, c: adt[:, c, i:i + 1], K["upto"]).then_inc(ev("m_rows_ready"), 1)
            pe.wait_ge(ev("m_g_copied"), 1)
            spread(stat, lambda i, c: adt[:, c, 4 + i:5 + i], K["upto"]).then_inc(ev("m_rows_ready"), 1)
            pe.wait_ge(ev("m_rows_read"), 1)
            pe.wait_ge(ev("m_rows_exp"), 1)
            pe.wait_ge(ev("m_xdd_ready"), 1)
            for g in range(2):
                mm = pe.matmul(mixbank(0)[:, g * T:(g + 1) * T], m_bt[:, g * P:(g + 1) * P], m_xdd[:, g * T:(g + 1) * T],
                               start=True, stop=True, skip_group_check=True)
            mm.then_inc(ev("m_h_ready"), 1)
            pe.wait_ge(ev("m_rows_read"), 2)
            pe.wait_ge(ev("m_rows_exp"), 2)
            pe.wait_ge(ev("m_h_copied"), 1)
            pe.wait_ge(ev("m_scores_ready"), 1)
            for hh in range(8):
                out_h = stat[64 * (hh % 2):64 * (hh % 2) + 64, hh // 2, :]
                for c in range(NT):
                    pe.matmul(out_h[:, c * P:(c + 1) * P], m_xt[:, c, hh * HD:(hh + 1) * HD], m_seg[:, hh, c * P:(c + 1) * P],
                              start=True, stop=c == 0, skip_group_check=True)
                mm = pe.matmul(out_h[:, P:T], m_h[:, hh * HD:(hh + 1) * HD], m_cd[:, hh, :], start=False, stop=True,
                               skip_group_check=True)
            mm.then_inc(ev("m_y_ready"), 1)
            pe.wait_ge(ev("m_ym_ready"), 1)
            sums(sq, 2, 2)

            sums(sq, 4, 1)
            sums(sq, 4, 1)
            pe.wait_ge(ev("g_k_ready"), 1)
            for c in range(NT):
                turned(mixbank(c), [gq[:, 4 + j, c * P:(c + 1) * P] for j in range(4)], ev("g_kt_turned"))
            for c in range(NT):
                pe.wait_ge(ev("g_kt_copied"), c + 1)
                turned(mixbank(c), [gq[:, 8 + j, c * P:(c + 1) * P] for j in range(4)], ev("g_vt_turned"))
            spread(stat, lambda i, c: beta[:, c, i:i + 1], K["ident"]).then_inc(ev("g_beta_ready"), 1)
            pe.wait_ge(ev("g_vt_copied"), 2)
            spread(mixp, lambda i, c: adt[:, c, 8 + i:9 + i], K["upto64"]).then_inc(ev("g_rows_ready"), 1)
            pe.wait_ge(ev("g_kb_ready"), 1)
            for i in range(4):
                for c in range(NT):
                    mm = pe.matmul(stat[:, i, c * P:(c + 1) * P], gq[:, 4 + i, c * P:(c + 1) * P], g_kb[:, i, c * P:(c + 1) * P],
                                   start=True, stop=True, skip_group_check=True)
            mm.then_inc(ev("g_kk_ready"), 1)
            pe.wait_ge(ev("g_rows_read"), 1)
            pe.wait_ge(ev("g_er_ready"), 1)
            for i in range(4):
                for c in range(NT):
                    mm = pe.matmul(mixp[:, i, c * P:(c + 1) * P], gq[:, 4 + i, c * P:(c + 1) * P], gq[:, i, c * P:(c + 1) * P],
                                   start=True, stop=True, skip_group_check=True)
            mm.then_inc(ev("g_kq_ready"), 1)
            pe.wait_ge(ev("g_mt_ready"), 1)
            for i in range(4):
                for c in range(NT):
                    mm = pe.transpose(stat[:, i, c * P:(c + 1) * P], g_mt[:, i, c * P:(c + 1) * P], K["ident"])
            mm.then_inc(ev("g_m_ready"), 1)
            pe.wait_ge(ev("g_at_ready"), 1)
            blocks = [(i, slice(c * P, (c + 1) * P)) for i in range(4) for c in range(NT)]
            for n in range(1, 6):
                pe.wait_ge(ev("g_d_ready"), n)
                for i, s in blocks:
                    mm = pe.matmul(mixp[:, i, s], g_ml[:, i, s], g_d[:, i, s], start=True, stop=True, skip_group_check=True)
                mm.then_inc(ev("g_w_ready"), 1)
                pe.wait_ge(ev("g_w_copied"), n)
                for i, s in blocks:
                    mm = pe.matmul(stat[:, i, s], g_w[:, i, s], g_dt[:, i, s], start=True, stop=True, skip_group_check=True)
                mm.then_inc(ev("g_ddt_ready"), 1)
                if n < 5:
                    for i, s in blocks:
                        mm = pe.matmul(mixp[:, i, s], g_dt[:, i, s], g_w[:, i, s], start=True, stop=True, skip_group_check=True)
                    mm.then_inc(ev("g_dd_ready"), 1)
            pe.wait_ge(ev("g_dt_final"), 1)
            for i, s in blocks:
                c = s.start // P
                mm = pe.matmul(stat[:, i, s], g_dt[:, i, s], g_vt[:, 2 * c + i // 2, (i % 2) * P:(i % 2 + 1) * P],
                               start=True, stop=True, skip_group_check=True)
            mm.then_inc(ev("g_u_ready"), 1)
            for i, s in blocks:
                c = s.start // P
                mm = pe.matmul(mixp[:, i, s], g_r2[:, 2 * c + i // 2, (i % 2) * P:(i % 2 + 1) * P], g_dt[:, i, s],
                               start=True, stop=True, skip_group_check=True)
            mm.then_inc(ev("g_wt_ready"), 1)
            pe.wait_ge(ev("g_wt_copied"), 1)
            pe.wait_ge(ev("g_u_copied"), 1)
            for ch in range(4):
                c, o = ch // 2, 64 * (ch % 2)
                s = slice(ch * 64, ch * 64 + 64)
                if ch:
                    pe.wait_ge(ev("g_s_ready"), ch)
                    for i in range(4):
                        mm = pe.matmul(mixbank(0)[o:o + 64, i * P:(i + 1) * P], g_w[:, i, s], g_s[:, i, :],
                                       start=True, stop=True, skip_group_check=True)
                    mm.then_inc(ev("g_ws_ready"), 1)
                pe.wait_ge(ev("g_vn_ready"), ch + 1)
                if ch < 3:
                    for i in range(4):
                        mm = pe.matmul(mixbank(1)[:, i * P:(i + 1) * P], g_kt[o:o + 64, 2 * c + i // 2, (i % 2) * P:(i % 2 + 1) * P],
                                       g_ml[o:o + 64, i, c * P:(c + 1) * P], start=True, stop=True, skip_group_check=True)
                    mm.then_inc(ev("g_ds_ready"), 1)
                for i in range(4):
                    mm = pe.matmul(stat[:, i, s], g_ml[o:o + 64, i, c * P:(c + 1) * P], g_at[o:o + 64, i, s],
                                   start=True, stop=ch == 0, skip_group_check=True)
                    if ch:
                        mm = pe.matmul(stat[:, i, s], g_s[:, i, :], g_qd[:, i, s],
                                       start=False, stop=True, skip_group_check=True)
                mm.then_inc(ev("g_o_ready"), 1)
            pe.wait_ge(ev("g_o_read"), 1)
            sums(sq, 4, 1)

            sums(sq, 4, 1)
            sums(sq, 4, 1)
            for c in range(NT):
                turned(mixbank(c), [sq_kv[:, 8 + j, c * P:(c + 1) * P] for j in range(4)], ev("b_vt_turned"))
            pe.wait_ge(ev("b_qk_ready"), 1)
            pe.wait_ge(ev("b_vt_copied"), 2)

            def bbank(i):
                return mixbank(i) if i < 2 else statbank(i)


            for i in range(4):
                pe.matmul(bbank(i)[:, 0:T], sq_kv[:, 4 + i, 0:P], sq_kv[:, i, :], start=True, stop=True, skip_group_check=True)
                mm = pe.matmul(bbank(i)[:, T:3 * P], sq_kv[:, 4 + i, P:T], sq_kv[:, i, P:T], start=True, stop=True,
                               skip_group_check=True)
            mm.then_inc(ev("b_z_ready"), 1)
            pe.wait_ge(ev("b_nk_ready"), 1)
            for i in range(4):
                pe.matmul(bbank(i)[:, 0:T], K["after"], b_nk[:, i, 0:T], start=True, stop=False, skip_group_check=True)
                pe.matmul(bbank(i)[:, P:T], K["ones"], b_nk[:, i, T:3 * P], start=False, stop=True, skip_group_check=True)
                mm = pe.matmul(bbank(i)[:, T:3 * P], K["after"], b_nk[:, i, T:3 * P], start=False, stop=True,
                               skip_group_check=True)
            mm.then_inc(ev("b_after_ready"), 1)
            pe.wait_ge(ev("b_att_ready"), 1)
            for i in range(4):
                o = stat[:, i, :]
                v = [b_vt[:, c, i * P:(i + 1) * P] for c in range(NT)]
                pe.matmul(o[:, 0:P], v[0], b_l[:, i, 0:P], start=True, stop=True, skip_group_check=True)
                pe.matmul(o[:, P:T], v[0], b_l[:, i, P:T], start=True, stop=False, skip_group_check=True)
                mm = pe.matmul(o[:, P:T], v[1], b_l[:, i, T:3 * P], start=False, stop=True, skip_group_check=True)
            mm.then_inc(ev("b_o_ready"), 1)
            pe.wait_ge(ev("branches_ready"), 1)

            with pe.Fori(0, 3) as it:
                for j in range(12):
                    b = panel(j, it, 12)
                    bank(b, it, 3, j // 4)
                    if j % 3:
                        product(b, h)
                        continue
                    w = ring[:, b, :].rearrange("p (k n) -> p k n", k=KH)
                    for m in range(2):
                        for i in range(KH):
                            mm = pe.matmul(lin[b][:, m * T:(m + 1) * T], w[:, i, m * P:(m + 1) * P],
                                           ybr[:, ds(it * KH + i, 1), :].rearrange("p k t -> p (k t)"),
                                           start=i == 0, stop=i == KH - 1, skip_group_check=True)
                    mm.then_inc(panel_done, 1)
            panels.advance(36)
            panels.settled()
            linear(merged, 8)
            sums(sq, 1, KD)
            pe.wait_ge(h_ready, seen(h_ready))
            for c in range(NT):
                for i in range(KD):
                    mm = pe.matmul(mixbank(0)[:, c * 36:(c + 1) * 36], h[:, i, c * P:(c + 1) * P], wsmall[:, i, 16:52],
                                   start=i == 0, stop=i == KD - 1, skip_group_check=True)
            mm.then_inc(ev("logits_ready"), 1)
            for g in range(4):
                if g:
                    pe.wait_ge(ev("ht_copied"), g)
                turned(mixbank(1), [h[:, (g % 2) * 4 + j, (g // 2) * P:(g // 2 + 1) * P] for j in range(4)], ev("ht_turned"))
            pe.wait_ge(ev("assigned"), 1)
            pe.matmul(mixbank(0)[:, 0:E], K["before"], assign[:, 0, :], start=True, stop=True, skip_group_check=True)
            pe.matmul(mixbank(0)[:, E:2 * E], K["before"], assign[:, 1, :], start=True, stop=False, skip_group_check=True)
            pe.matmul(mixbank(0)[:, E:2 * E], K["ones"], assign[:, 0, :], start=False, stop=True, skip_group_check=True)
            pe.matmul(mixbank(0)[:, 2 * E:3 * E], K["ones"], assign[:, 0, :], start=True, stop=False, skip_group_check=True)
            pe.matmul(mixbank(0)[:, 2 * E:3 * E], K["ones"], assign[:, 1, :], start=False, stop=True, skip_group_check=True)\
                .then_inc(ev("ranks_ready"), 1)
            pe.wait_ge(ev("ht_copied"), 4)
            panels.settled()
            pe.wait_ge(M["dT"], 1)
            for b in range(4):
                pe.matmul(lin[b][:, :], e_dT[:, 0:P], h_tm[:, 0, 0:512], start=True, stop=False, skip_group_check=True)

            def moe_gather(s):
                for c in range(NT):
                    for half in range(2):
                        mm = pe.matmul(statbank(0)[64 * half:64 * half + 64, :], e_sel[:, s, c, :],
                                       h_tm[:, c, half * 512:(half + 1) * 512], start=c == 0, stop=c == 1, skip_group_check=True)
                mm.then_inc(M["A"], 1)

            def moe_turn():
                for j in range(4):
                    mm = pe.transpose(statbank(1)[:, j * P:(j + 1) * P], e_hg[:, j * P:(j + 1) * P], K["ident"])
                mm.then_inc(M["B"], 1)

            def moe_combine():
                for j in range(4):
                    for half in range(2):
                        m = half * 4 + j
                        mm = pe.matmul(lin[m // 2][:, (m % 2) * T:(m % 2 + 1) * T], e_yb[64 * half:64 * half + 64, j * P:(j + 1) * P],
                                       e_dT[64 * half:64 * half + 64, T:2 * T], start=False, stop=False, skip_group_check=True)
                return mm

            pe.wait_ge(M["sel"], 1)
            moe_gather(0)
            pe.wait_ge(M["hg"], 1)
            moe_turn()
            pe.wait_ge(M["sel"], 2)
            moe_gather(1)

            def moe_step(it, s):
                pe.wait_ge(M[f"gu_loaded{s}"], it * 32 + 32)
                pe.wait_ge(M["hgT"], it * 2 + (s + 1))
                pe.wait_ge(M["hid"], it * 2 + (s + 1))
                for k in range(KD):
                    lhs = e_hgT[:, k % 4, k // 4, :]
                    for half in range(2):
                        o = mixbank(0)[64 * half:64 * half + 64, :]
                        pe.matmul(o[:, 0:T], lhs, e_wg[:, s, k, half * T:(half + 1) * T], start=k == 0, stop=k == KD - 1,
                                  skip_group_check=True)
                    for half in range(2):
                        o = mixbank(0)[64 * half:64 * half + 64, :]
                        mm = pe.matmul(o[:, T:2 * T], lhs, e_wu[:, s, k, half * T:(half + 1) * T], start=False,
                                       stop=k == KD - 1, skip_group_check=True)
                mm.then_inc(M["C"], 1)
                pe.wait_ge(M["yb"], it * 2 + (s + 1))
                pe.wait_ge(M["dT"], it * 2 + (s + 1))
                moe_combine().then_inc(M["F"], 1)
                pe.wait_ge(M["hg"], it * 2 + (s + 2))
                moe_turn()
                pe.wait_ge(M["hid"], it * 2 + (s + 2))
                pe.wait_ge(M["selw"], it * 2 + (s + 1))
                for j in range(2):
                    pe.transpose(mixbank(1)[:, j * P:(j + 1) * P], e_hid[:, j * P:(j + 1) * P], K["ident"])
                for c in range(NT):
                    mm = pe.transpose(mixbank(1)[:, T + c * P:T + (c + 1) * P], e_selw[:, s, c, :], K["ident"])
                mm.then_inc(M["D"], 1)
                pe.wait_ge(M["sel"], it * 2 + (s + 3))
                moe_gather(s)
                pe.wait_ge(M[f"d_loaded{s}"], it * 16 + 16)
                pe.wait_ge(M["dT"], it * 2 + (s + 2))
                pe.wait_ge(M["hgT"], it * 2 + (s + 2))
                for k in range(4):
                    for half in range(2):
                        mm = pe.matmul(statbank(1)[64 * half:64 * half + 64, :], e_hidT[:, k % 2, k // 2, :],
                                       e_wd[:, s, k, half * 512:(half + 1) * 512], start=k == 0, stop=k == 3, skip_group_check=True)
                mm.then_inc(M["E"], 1)

            def moe_last(e):
                pe.wait_ge(M["yb"], e + 2)
                pe.wait_ge(M["dT"], e + 2)
                moe_combine().then_inc(M["y"], 1)

            with pe.Fori(0, E // 2) as it:
                moe_step(it, 0)
                moe_step(it, 1)
            pe.wait_ge(M["flag"], 1)
            more = pe.value_load(flag_i[0:1, 0:1], min_val=0, max_val=1)
            with pe.If(more == 1):
                with pe.Fori(E // 2, NE // 2) as it:
                    moe_step(it, 0)
                    moe_step(it, 1)
                moe_last(NE - 1)
            with pe.Else():
                moe_last(E - 1)

        @block.scalar
        def _(act):
            seen = Seen()
            panels = Panels(act)

            def norm(src, tiles, groups=1, width=D):
                act.activation(sq[:, 0:tiles, :], src, ACT.Square).then_inc(sq_ready, 1)
                act.wait_ge(sums_ready, seen(sums_ready))
                act.activation(rs[:, 0:groups, :], stat[:, 0:groups, :], ACT.Ln, bias=K["eps"], scale=1.0 / width)\
                    .then_inc(ln_done, 1)
                act.wait_ge(ln_done, seen(ln_done))
                act.activation(rs[:, 0:groups, :], rs[:, 0:groups, :], ACT.Exp, scale=-0.5).then_inc(rs_ready, 1)

            def take(dst, func=ACT.Copy, **kw):
                b = panels.done()
                act.activation(dst, lin[b][:, 0:T], func, **kw).then_inc(bank_free[b], 1)
                panels.advance(1)

            def tap0(dst, b, w, bias):
                act.activation(dst, lin[b][:, 0:T], ACT.Identity, bias=bias, scale=w).then_inc(tap0_done, 1)

            def ffn(l):
                panels.settled()
                norm(x[:, :, :], KD)
                w2 = cols["ffn_cw"][0] + (l * 3 + 2) * 2 * KF
                cb = cols["ffn_cb"][0] + l * 2 * KF
                with act.Fori(0, KF // 2) as it:
                    act.wait_ge(act_tile, it * 2 + (1 + l * KF))
                    for j in range(4):
                        b = panels.done(j, it)
                        tile = j // 2 + KF * (j % 2)
                        tap0(ub[:, j, :], b, colp[:, ds(it * 2 + (w2 + tile), 1)], colp[:, ds(it * 2 + (cb + tile), 1)])
                        if j % 2 == 1:
                            panels.taken(j - 1, it)
                            act.activation(sgf[:, j // 2, :], ub[:, j - 1, :], ACT.Silu).then_inc(silu_done, 1)
                panels.advance(2 * KF)
                panels.advance_down()

            act.wait_ge(consts_loaded, 48)
            norm(x[:, :, :], KD)
            act.activation(c_act[:, :], col("c", 0, KD), ACT.Silu).then_inc(silu_done, 1)
            for j in range(4):
                take(sg0[:, j, :], ACT.Sigmoid, bias=col("b_in", 12 + j))
                panels.advance(1)
            for j in range(4):
                take(v0[:, j, :], ACT.Gelu_apprx_tanh, bias=col("b_in", 4 + j))
            for j in range(4):
                take(u0[:, j, :], ACT.Gelu_apprx_tanh, bias=col("b_in", j))
            with act.Fori(0, 12) as it:
                for j in range(4):
                    b = panels.done(j, it)
                    act.activation(modraw[:, ds(it * 4 + j, 1), :].rearrange("p n c -> p (n c)"), lin[b][:, 0:32], ACT.Copy)\
                        .then_inc(bank_free[b], 1)
            panels.advance(48)
            act.wait_ge(centred, 1)
            norm(xc0, KH, width=HALF)
            act.wait_ge(centred, 2)
            norm(xc0, KH, width=HALF)
            act.wait_ge(yb_normed, 1)
            for j in range(KH):
                ins = act.activation(cat[:, KH + j, :], cv0[:, j, :], ACT.Silu, bias=col("cln_b", j))
            ins.then_inc(yb_ready, 1)
            panels.advance(8)
            ffn(0)
            panels.settled()
            norm(x[:, :, :], KD)
            for n in range(16):
                if n >= 2:
                    act.wait_ge(qk_ready, n - 1)
                take(qs1[:, n % 2, :])
            for n in range(8):
                take(v1[:, n, :])
            for i in range(HEADS + 1):
                if i < HEADS:
                    act.wait_ge(max_ready, i + 1)
                    if i >= 4:
                        act.wait_ge(pt_ready, i - 3)
                    for c, (a0, a1) in enumerate(((0, P), (P, 3 * P))):
                        ins = act.activation(p1[:, i % 4, a0:a1], s1[:, i % 4, a0:a1], ACT.Exp,
                                             bias=mx1[:, 2 * i + c:2 * i + c + 1], accum_out=l1[:, 2 * i + c:2 * i + c + 1])
                    ins.then_inc(exp_ready, 1)
                if i >= 1:
                    g = i - 1
                    act.wait_ge(pt_ready, g + 1)
                    if g >= 4:
                        act.wait_ge(o_ready, g - 3)
                    act.activation(pt1[:, g % 4, :], statbank(g)[:, 0:SC], ACT.Copy).then_inc(pt_copied, 1)
            panels.advance(8)
            ffn(1)
            def step(ins):
                ins.then_inc(act_step, 1)
                act.wait_ge(act_step, seen(act_step))

            def conv_tiles(dst, count, w, bias, done):
                for n in range(count + 1):
                    if n < count:
                        tap0(dst[:, n, :], panels.done(n), w(n), bias(n))
                    if n:
                        panels.taken(n - 1)
                        ins = act.activation(dst[:, n - 1, :], dst[:, n - 1, :], ACT.Silu)
                ins.then_inc(done, 1)
                panels.advance(count)

            panels.settled()
            norm(x[:, :, :], KD)
            act.wait_ge(ev("x_final"), 1)
            norm(x[:, :, :], KD)
            act.wait_ge(ev("small_in"), 1)
            act.wait_ge(extra_loaded, 48)
            act.activation(ea, rows[:, ROWS["a_log"][0]:ROWS["a_log"][0] + 12], ACT.Exp)
            act.activation(beta_in, beta_in, ACT.Exp, scale=-1.0)
            step(act.activation(spe, spin, ACT.Abs))
            step(act.activation(spe, spe, ACT.Exp, scale=-1.0))
            act.activation(spl, spe, ACT.Ln, bias=K["one"]).then_inc(ev("small_act"), 1)
            conv_tiles(xb, 8, lambda n: col("ssm_cw", 24 + n), lambda n: col("ssm_cb", n), ev("xb_ready"))
            act.wait_ge(ev("cums_copied"), 1)
            act.activation(mdec, mdif, ACT.Exp)
            act.activation(kdec, gdif, ACT.Exp)
            act.activation(eg, cums[:, :, 8:12], ACT.Exp).then_inc(ev("decays_ready"), 1)
            for j in range(4):
                take(zs[:, j, :], ACT.Silu)
            conv_tiles(gq, 12, lambda n: col("gdn_cw", 36 + n), lambda n: 0.0, ev("gq_ready"))
            for j in range(4):
                take(gg[:, j, :], ACT.Silu)
            for j in range(12):
                take(sq_kv[:, j, :])
            for k, ps in ((0, mixp), (1, stat)):
                act.wait_ge(ev("m_rows_ready"), k + 1)
                act.activation(m_er[:, 4 * k:4 * k + 4, :], ps[:, :, P:T], ACT.Exp).then_inc(ev("m_rows_exp"), 1)
                act.wait_ge(ev("m_rows_read"), k + 1)
                seg = m_seg[:, 4 * k:4 * k + 4, :]
                act.activation(seg, seg, ACT.Exp).then_inc(ev("m_seg_exp"), 1)
            act.wait_ge(ev("m_ym_ready"), 1)
            norm(ybr[:, 0:4, :], 4, 2, T)
            act.wait_ge(ev("gq_ready"), 1)
            act.wait_ge(ev("ya_done"), 1)
            norm(gq[:, 0:4, :], 4, 4, 1)
            act.wait_ge(ev("g_q_ready"), 1)
            norm(gq[:, 4:8, :], 4, 4, 1)
            act.wait_ge(ev("g_rows_ready"), 1)
            act.activation(g_er, mixp[:, :, :], ACT.Exp).then_inc(ev("g_er_ready"), 1)
            act.wait_ge(ev("g_rows_read"), 1)
            act.activation(g_dec, g_dec, ACT.Exp).then_inc(ev("g_dec_ready"), 1)
            for n in range(1, 6):
                act.wait_ge(ev("g_w_ready"), n)
                act.activation(g_w, mixp[:, :, :], ACT.Copy).then_inc(ev("g_w_copied"), 1)
            act.wait_ge(ev("g_wt_ready"), 1)
            act.activation(g_w, mixp[:, :, :], ACT.Copy).then_inc(ev("g_wt_copied"), 1)
            act.wait_ge(ev("g_o_read"), 1)
            norm(ybr[:, 8:12, :], 4, 4, P)
            act.wait_ge(ev("yc_done"), 1)
            panels.settled()
            norm(sq_kv[:, 0:4, :], 4, 4, P)
            act.wait_ge(ev("b_q_ready"), 1)
            norm(sq_kv[:, 4:8, :], 4, 4, P)
            act.wait_ge(ev("b_z_ready"), 1)
            for k in range(2):
                step(act.activation(b_l[:, 2 * k:2 * k + 2, :], zbanks(k), ACT.Abs))
            step(act.activation(b_l, b_l, ACT.Exp, scale=-1.0))
            act.activation(b_l, b_l, ACT.Ln, bias=K["one"]).then_inc(ev("b_l_ready"), 1)
            act.wait_ge(ev("b_lb_ready"), 1)
            act.activation(b_l, b_lb, ACT.Exp).then_inc(ev("b_exp_ready"), 1)
            act.wait_ge(ev("branches_ready"), 1)
            with act.Fori(0, 3) as it:
                act.wait_ge(ev("gated"), it * 8 + 1)
                for j in range(12):
                    if j % 3:
                        b = panels.done(j, it, 12)
                        act.activation(gates8[:, 2 * (j // 3) + j % 3 - 1, :], lin[b][:, 0:T], ACT.Sigmoid)\
                            .then_inc(bank_free[b], 1)
            panels.advance(36 + 8)
            panels.settled()
            norm(x[:, :, :], KD)
            act.wait_ge(ev("route_in"), 1)
            act.activation(r_ge, r_ge, ACT.Exp).then_inc(ev("group_exp"), 1)
            act.wait_ge(ev("top_in"), 1)
            act.activation(r_e2, r_e2, ACT.Exp).then_inc(ev("top_exp"), 1)
            act.wait_ge(M["B"], 1)
            act.activation(e_hgT_flat, statbank(1), ACT.Copy).then_inc(M["hgT"], 1)

            def moe_step(it, s):
                act.wait_ge(M["C"], it * 2 + (s + 1))
                act.wait_ge(M["hid"], it * 2 + (s + 1))
                act.activation(e_sg, mixbank(0)[:, 0:T], ACT.Silu).then_inc(M["silu"], 1)
                act.wait_ge(M["B"], it * 2 + (s + 2))
                act.activation(e_hgT_flat, statbank(1), ACT.Copy).then_inc(M["hgT"], 1)
                act.wait_ge(M["E"], it * 2 + (s + 1))
                act.activation(e_yb, statbank(1), ACT.Copy).then_inc(M["yb"], 1)

            with act.Fori(0, E // 2) as it:
                moe_step(it, 0)
                moe_step(it, 1)
            act.wait_ge(M["flag"], 1)
            more = act.value_load(flag_i[0:1, 0:1], min_val=0, max_val=1)
            with act.If(more == 1):
                with act.Fori(E // 2, NE // 2) as it:
                    moe_step(it, 0)
                    moe_step(it, 1)

        @block.vector
        def _(dve):
            seen = Seen()
            panels = Panels(dve)

            def link(ins):
                ins.then_inc(dve_step, 1)
                dve.wait_ge(dve_step, seen(dve_step))

            def scale_stream(gain):
                dve.wait_ge(rs_ready, seen(rs_ready))
                for k in range(KD):
                    ins = dve.scalar_tensor_tensor(h[:, k, :], x[:, k, :], gain(k), rs[:, 0, :], ALU.mult, ALU.mult)
                return ins

            def residual(count, gate=None):
                for m in range(count):
                    b = panels.done()
                    if gate is None:
                        ins = dve.tensor_tensor(x[:, m, :], x[:, m, :], lin[b][:, 0:T], ALU.add)
                    else:
                        ins = dve.scalar_tensor_tensor(x[:, m, :], lin[b][:, 0:T], gate(m), x[:, m, :], ALU.mult, ALU.add)
                    ins.then_inc(bank_free[b], 1)
                    panels.advance(1)

            def ffn(l):
                panels.settled()
                scale_stream(lambda k: col("ffn_norm", l * KD + k)).then_inc(h_ready, 1)
                first = cols["ffn_cw"][0] + l * 3 * 2 * KF
                base = seen.now(dve_step)
                taps = l * 2 * KF
                with dve.Fori(0, KF // 2) as it:
                    for j in range(4):
                        b = (panels.n + j) % 4
                        dve.wait_ge(tap0_done, it * 4 + (taps + j + 1))
                        tile = first + j // 2 + KF * (j % 2)
                        dve.scalar_tensor_tensor(ub[:, j, 1:T], lin[b][:, 0:T - 1], colp[:, ds(it * 2 + (tile + 2 * KF), 1)],
                                                 ub[:, j, 1:T], ALU.mult, ALU.add).then_inc(dve_step, 1)
                        dve.wait_ge(dve_step, it * 4 + (base + j + 1))
                        dve.scalar_tensor_tensor(ub[:, j, 2:T], lin[b][:, 0:T - 2], colp[:, ds(it * 2 + tile, 1)],
                                                 ub[:, j, 2:T], ALU.mult, ALU.add).then_inc(bank_free[b], 1)
                        if j % 2 == 1:
                            dve.wait_ge(silu_done, it * 2 + (1 + l * KF + j // 2 + 1))
                            panels.taken(j, it)
                            dve.tensor_tensor(hid[:, ds(it * 2 + j // 2, 1), :].rearrange("p k t -> p (k t)"),
                                              sgf[:, j // 2, :], ub[:, j, :], ALU.mult).then_inc(act_tile, 1)
                seen(dve_step, 2 * KF)
                panels.advance(2 * KF)
                dve.wait_ge(panel_done, panels.n + KF)
                for b in range(4):
                    dve.tensor_tensor(x[:, 2 * b:2 * b + 2, :], x[:, 2 * b:2 * b + 2, :],
                                      lin[b][:, :].rearrange("p (m t) -> p m t", m=2), ALU.add).then_inc(bank_free[b], 1)
                panels.advance_down()

            def centre(src, n):
                dve.wait_ge(mean_ready, n + 1)
                dve.tensor_tensor(xc0, src, mixp[:, 2 * n:2 * n + 1, :].broadcast_to([P, KH, T]), ALU.subtract)\
                    .then_inc(centred, 1)
                dve.wait_ge(centred, n + 1)

            dve.memset(hc0[:, :, 0:PADC], 0.0).then_inc(act_tile, 1)
            dve.wait_ge(act_tile, 1)
            dve.wait_ge(consts_loaded, 48)
            scale_stream(lambda k: col("even_norm", k)).then_inc(h_ready, 1)
            for j in range(KH):
                panels.taken(0)
                b = panels.done(1)
                dve.scalar_tensor_tensor(hc0[:, j, PADC:], lin[b][:, 0:T], col("b_in", 8 + j), sg0[:, j, :], ALU.add, ALU.mult)\
                    .then_inc(bank_free[b], 1)
                panels.advance(2)
            panels.advance(8)
            for b in (1, 3):
                dve.wait_ge(bank_free[b], 2)
            for j in range(KH):
                dve.tensor_scalar(cv0[:, j, :], hc0[:, j, 0:T], col("conv_w", j), col("conv_b", j), ALU.mult, ALU.add)\
                    .then_inc(conv_step, 1)
            with dve.Fori(1, CONV) as tap:
                for j in range(KH):
                    dve.wait_ge(conv_step, tap * KH + (j - 3))
                    dve.scalar_tensor_tensor(cv0[:, j, :], hc0[:, j, ds(tap, T)], colp[:, ds(tap * KH + (cols["conv_w"][0] + j), 1)],
                                             cv0[:, j, :], ALU.mult, ALU.add).then_inc(conv_step, 1)
            dve.wait_ge(extra_loaded, 48)
            link(dve.tensor_tensor(wsm0, ws0, K["upto"].unsqueeze(1).broadcast_to([P, 8, P]), ALU.mult))
            panels.settled()
            centre(v0, 0)
            dve.wait_ge(rs_ready, seen(rs_ready))
            for j in range(KH):
                ins = dve.scalar_tensor_tensor(v0[:, j, :], xc0[:, j, :], col("vln_g", j), rs[:, 0, :], ALU.mult, ALU.mult)
            link(ins)
            for j in range(KH):
                ins = dve.tensor_scalar(v0[:, j, :], v0[:, j, :], col("vln_b", j), None, ALU.add)
            ins.then_inc(v_normed, 1)
            for c in range(NT):
                dve.wait_ge(vt_ready, c + 1)
                dve.tensor_copy(vt0[:, c, :], mixbank(c)).then_inc(vt_copied, 1)
            dve.wait_ge(mixed_ready, 1)
            bs = row("b_s").rearrange("p (j two t) -> p j two t", two=2, t=P)
            for half in range(2):
                for c in range(NT):
                    o = 64 * half
                    ins = dve.tensor_tensor(xc0[o:o + 64, :, c * P:(c + 1) * P], mixp[o:o + 64, :, c * P:(c + 1) * P],
                                            bs[o:o + 64, :, half, :], ALU.add)
            link(ins)
            dve.tensor_tensor(cat[:, 0:KH, :], xc0, u0, ALU.mult).then_inc(ya_ready, 1)
            dve.wait_ge(ya_ready, 1)
            dve.wait_ge(conv_step, CONV * KH)
            centre(cv0, 1)
            dve.wait_ge(rs_ready, seen(rs_ready))
            for j in range(KH):
                ins = dve.scalar_tensor_tensor(cv0[:, j, :], xc0[:, j, :], col("cln_g", j), rs[:, 0, :], ALU.mult, ALU.mult)
            ins.then_inc(yb_normed, 1)
            panels.advance(48)
            panels.settled()
            link(dve.tensor_tensor(modsel, modraw, K["diag32"].unsqueeze(1).broadcast_to([P, 48, 32]), ALU.mult))
            link(dve.tensor_reduce(mod[:, :], modsel, AX, ALU.add))
            link(dve.tensor_tensor(mod[:, :], mod[:, :], col("b_ada", 0, 48), ALU.add))
            for half, name in ((0, "norm_mix"), (1, "norm_ffn")):
                link(dve.scalar_tensor_tensor(gains[:, half * KD:(half + 1) * KD], mod[:, (3 * half + 1) * KD:(3 * half + 2) * KD],
                                              1.0, col(name, 0, KD), ALU.add, ALU.mult))
            residual(8)
            ffn(0)
            panels.settled()
            scale_stream(lambda k: col("odd_norm", k)).then_inc(h_ready, 1)
            for n in range(16):
                panels.taken(0)
                panels.advance(1)
                link(dve.tensor_tensor(rc1[:, 0, :], qs1[:, n % 2, :], K["cos"], ALU.mult))
                dve.wait_ge(rot_ready, n + 1)
                link(dve.tensor_tensor(rc1[:, 1, :], stat[:, 2 * (n % 2), :], K["sin"], ALU.mult))
                dve.tensor_tensor(qk1[:, n, :], rc1[:, 0, :], rc1[:, 1, :], ALU.add).then_inc(qk_ready, 1)
                dve.wait_ge(qk_ready, n + 1)
            panels.advance(8)
            for g in range(4):
                dve.wait_ge(vt1_ready, g + 1)
                dve.tensor_copy(vt1[:, g // 2, (g % 2) * 512:(g % 2 + 1) * 512], mixbank(g)).then_inc(vt1_copied, 1)
            a0 = list(K).index("bias00")
            bias_at = sum(v.shape[1] for v in list(consts.values())[:a0])
            bias = cst[:, bias_at:bias_at + SC]
            for i in range(HEADS + 2):
                if i < HEADS:
                    dve.wait_ge(scores_ready, i + 1)
                    if i >= 4:
                        dve.wait_ge(exp_ready, i - 3)
                    dve.scalar_tensor_tensor(s1[:, i % 4, :], mixbank(i)[:, 0:SC], HD ** -0.5, bias, ALU.mult, ALU.add)\
                        .then_inc(scores_read, 1)
                    dve.wait_ge(scores_read, i + 1)
                    for c, (a0, a1) in enumerate(((0, P), (P, 3 * P))):
                        ins = dve.tensor_reduce(mx1[:, 2 * i + c:2 * i + c + 1], s1[:, i % 4, a0:a1], AX, ALU.max, negate=True)
                    ins.then_inc(max_ready, 1)
                if 1 <= i <= HEADS:
                    g = i - 1
                    dve.wait_ge(exp_ready, g + 1)
                    link(dve.reciprocal(r1[:, 2 * g:2 * g + 2], l1[:, 2 * g:2 * g + 2]))
                    for c, (a0, a1) in enumerate(((0, P), (P, 3 * P))):
                        ins = dve.tensor_scalar(p1[:, g % 4, a0:a1], p1[:, g % 4, a0:a1], r1[:, 2 * g + c:2 * g + c + 1],
                                                None, ALU.mult)
                    ins.then_inc(probs_ready, 1)
                if i >= 2 and i % 2 == 1:
                    j = (i - 2) // 2
                    dve.wait_ge(o_ready, 2 * j + 2)
                    dve.tensor_copy(cat[:, j, :], lin[j % 4][:, 0:T]).then_inc(o_copied, 1)
            residual(8)
            ffn(1)
            panels.settled()
            dve.wait_ge(rs_ready, seen(rs_ready))
            for k in range(KD):
                ins = dve.scalar_tensor_tensor(x[:, k, :], x[:, k, :], col("final_norm", k), rs[:, 0, :], ALU.mult, ALU.mult)
            ins.then_inc(ev("x_final"), 1)
            dve.wait_ge(ev("x_final"), 1)

            def modulated(half):
                link(scale_stream(lambda k: gains[:, half * KD + k:half * KD + k + 1]))
                for k in range(KD):
                    ins = dve.tensor_scalar(h[:, k, :], h[:, k, :], mod[:, 3 * half * KD + k:3 * half * KD + k + 1], None, ALU.add)
                ins.then_inc(h_ready, 1)

            def conv_tiles(dst, count, tap_w, taps):
                for n in range(count):
                    b = (panels.n + n) % 4
                    dve.wait_ge(tap0_done, convs[0] + n + 1)
                    for s in range(1, taps):
                        ins = dve.scalar_tensor_tensor(dst[:, n, s:T], lin[b][:, 0:T - s], tap_w(taps - 1 - s, n),
                                                       dst[:, n, s:T], ALU.mult, ALU.add)
                        if s < taps - 1:
                            link(ins)
                        else:
                            ins.then_inc(bank_free[b], 1)
                convs[0] += count
                panels.advance(count)

            modulated(0)
            dve.wait_ge(ev("small_ready"), 1)
            sm = mixbank(0)[:, 0:32].rearrange("p (c n) -> p c n", c=NT)
            a0 = ROWS["dt_bias"][0]
            link(dve.tensor_tensor(spin, sm[:, :, 0:12], rows[:, a0:a0 + 12].unsqueeze(1).broadcast_to([P, NT, 12]), ALU.add))
            dve.tensor_copy(beta_in, sm[:, :, 12:16]).then_inc(ev("small_in"), 1)
            dve.wait_ge(ev("small_act"), 1)
            link(dve.scalar_tensor_tensor(spl, spin, 0.0, spl, ALU.max, ALU.add))
            link(dve.tensor_scalar(beta_in, beta_in, 1.0, None, ALU.add))
            link(dve.reciprocal(beta, beta_in))
            dve.scalar_tensor_tensor(adt, spl, -1.0, ea.unsqueeze(1).broadcast_to([P, NT, 12]), ALU.mult, ALU.mult)\
                .then_inc(ev("adt_ready"), 1)
            convs = [4 * KF]
            conv_tiles(xb, 8, lambda t, n: col("ssm_cw", t * 8 + n), 4)
            dve.wait_ge(ev("cums_ready"), 1)
            link(dve.tensor_copy(cums, mixbank(1)[:, 0:48].rearrange("p (c n) -> p c n", c=NT)))
            link(dve.tensor_tensor(mdif, cums[:, :, 16:24], cums[:, :, 0:8], ALU.subtract))
            dve.tensor_tensor(gdif, cums[:, :, 12:16], cums[:, :, 8:12], ALU.subtract).then_inc(ev("cums_copied"), 1)
            panels.advance(4)
            conv_tiles(gq, 12, lambda t, n: col("gdn_cw", t * 12 + n), 4)
            panels.advance(16)
            dve.wait_ge(ev("decays_ready"), 1)
            link(dve.tensor_tensor(beg, beta, eg, ALU.mult))

            panels.settled()
            dve.wait_ge(ev("xb_ready"), 1)
            for c in range(NT):
                dve.wait_ge(ev("m_xt_turned"), c + 1)
                dve.tensor_tensor(m_xt[:, c, :].rearrange("p (h d) -> p h d", d=HD), mixbank(c).rearrange("p (h d) -> p h d", d=HD),
                                  spl[:, c, 0:8].unsqueeze(2).broadcast_to([P, 8, HD]), ALU.mult).then_inc(ev("m_xt_copied"), 1)
            dve.wait_ge(ev("m_g_ready"), 1)
            link(dve.tensor_copy(m_bt, statbank(0)[:, 0:T]))
            dve.tensor_copy(m_g, statbank(1).rearrange("p (g t) -> p g t", g=2)).then_inc(ev("m_g_copied"), 1)
            dve.wait_ge(ev("m_xt_copied"), 1)
            dve.tensor_tensor(m_xdd.rearrange("p (h d) -> p h d", d=HD), m_xt[:, 0, :].rearrange("p (h d) -> p h d", d=HD),
                              mdec[:, 0, :].unsqueeze(2).broadcast_to([P, 8, HD]), ALU.mult).then_inc(ev("m_xdd_ready"), 1)

            def rows_to_decays(dst, ps, cum, mask):
                for c in range(NT):
                    s = slice(c * P, (c + 1) * P)
                    ins = dve.tensor_tensor(dst[:, :, s], ps[:, :, s], cum(c).unsqueeze(2).broadcast_to([P, 4, P]), ALU.subtract)
                link(ins)
                for c in range(NT):
                    s = slice(c * P, (c + 1) * P)
                    ins = dve.tensor_tensor(dst[:, :, s], dst[:, :, s], mask.unsqueeze(1).broadcast_to([P, 4, P]), ALU.add)
                return ins

            for k, ps in ((0, mixp), (1, stat)):
                dve.wait_ge(ev("m_rows_exp"), k + 1)
                rows_to_decays(m_seg[:, 4 * k:4 * k + 4, :], ps, lambda c: cums[:, c, 4 * k:4 * k + 4], K["neg_causal"])\
                    .then_inc(ev("m_rows_read"), 1)
            dve.wait_ge(ev("m_rows_exp"), 2)
            for k in range(2):
                ins = dve.tensor_tensor(m_cd[:, 4 * k:4 * k + 4, :], m_er[:, 4 * k:4 * k + 4, :],
                                        xb[:, 6 + k:7 + k, P:T].broadcast_to([P, 4, P]), ALU.mult)
            link(ins)
            dve.wait_ge(ev("m_h_ready"), 1)
            dve.tensor_copy(m_h, mixbank(0)).then_inc(ev("m_h_copied"), 1)
            dve.wait_ge(ev("m_seg_exp"), 2)
            dve.wait_ge(ev("m_g_copied"), 1)
            for k in range(2):
                seg = m_seg[:, 4 * k:4 * k + 4, :]
                ins = dve.tensor_tensor(seg, seg, m_g[:, k:k + 1, :].broadcast_to([P, 4, T]), ALU.mult)
            ins.then_inc(ev("m_scores_ready"), 1)
            dve.wait_ge(ev("m_y_ready"), 1)
            for j in range(4):
                ins = dve.scalar_tensor_tensor(ybr[:, j, :], xb[:, j, :], col("ssm_d", j), stat[:, j, :], ALU.mult, ALU.add)
            link(ins)
            dve.tensor_tensor(ybr[:, 0:4, :], ybr[:, 0:4, :], zs, ALU.mult).then_inc(ev("m_ym_ready"), 1)
            dve.wait_ge(ev("m_ym_ready"), 1)
            dve.wait_ge(rs_ready, seen(rs_ready))
            for j in range(4):
                ins = dve.scalar_tensor_tensor(ybr[:, j, :], ybr[:, j, :], col("ssm_norm", j), rs[:, j // 2, :], ALU.mult, ALU.mult)
            ins.then_inc(ev("ya_done"), 1)
            dve.wait_ge(ev("gq_ready"), 1)
            dve.wait_ge(rs_ready, seen(rs_ready))
            dve.scalar_tensor_tensor(gq[:, 0:4, :], gq[:, 0:4, :], P ** -0.5, rs[:, :, :], ALU.mult, ALU.mult).then_inc(ev("g_q_ready"), 1)
            dve.wait_ge(rs_ready, seen(rs_ready))
            dve.tensor_tensor(gq[:, 4:8, :], gq[:, 4:8, :], rs[:, :, :], ALU.mult).then_inc(ev("g_k_ready"), 1)

            def per_head(ap):
                return ap.unsqueeze(2).broadcast_to([P, 4, P])

            def tokens(buf, c):
                return buf[:, 2 * c:2 * c + 2, :].rearrange("p a t -> p (a t)").rearrange("p (h d) -> p h d", h=4)

            for c in range(NT):
                dve.wait_ge(ev("g_kt_turned"), c + 1)
                dve.tensor_copy(tokens(g_kt, c), mixbank(c).rearrange("p (h d) -> p h d", h=4)).then_inc(ev("g_kt_copied"), 1)
            for c in range(NT):
                dve.wait_ge(ev("g_vt_turned"), c + 1)
                dve.tensor_tensor(tokens(g_vt, c), mixbank(c).rearrange("p (h d) -> p h d", h=4), per_head(beta[:, c, :]),
                                  ALU.mult).then_inc(ev("g_vt_copied"), 1)
            dve.wait_ge(ev("g_beta_ready"), 1)
            dve.wait_ge(ev("g_k_ready"), 1)
            dve.tensor_tensor(g_kb, gq[:, 4:8, :], stat[:, :, :], ALU.mult).then_inc(ev("g_kb_ready"), 1)
            dve.wait_ge(ev("g_kt_copied"), 2)
            for c in range(NT):
                ins = dve.tensor_tensor(tokens(g_r2, c), tokens(g_kt, c), per_head(beg[:, c, :]), ALU.mult)
            link(ins)
            for c in range(NT):
                ins = dve.tensor_tensor(tokens(g_kt, c), tokens(g_kt, c), per_head(kdec[:, c, :]), ALU.mult)
            link(ins)
            dve.wait_ge(ev("g_er_ready"), 1)
            rows_to_decays(g_dec, mixp, lambda c: cums[:, c, 8:12], K["neg_causal64"]).then_inc(ev("g_rows_read"), 1)
            link(dve.tensor_tensor(g_qd, gq[:, 0:4, :], g_er, ALU.mult))
            dve.wait_ge(ev("g_dec_ready"), 1)

            def masks(name):
                return K[name].unsqueeze(1).broadcast_to([P, 8, P])

            def flat(ap):
                return ap.rearrange("p h (c t) -> p (h c) t", t=P)

            dve.wait_ge(ev("g_kk_ready"), 1)
            link(dve.tensor_tensor(g_mt, stat[:, :, :], g_dec, ALU.mult))
            dve.tensor_tensor(flat(g_mt), flat(g_mt), masks("before64"), ALU.mult).then_inc(ev("g_mt_ready"), 1)
            dve.wait_ge(ev("g_mt_ready"), 1)
            dve.wait_ge(ev("g_kq_ready"), 1)
            dve.tensor_tensor(g_at, mixp[:, :, :], g_dec, ALU.mult).then_inc(ev("g_at_ready"), 1)
            link(dve.tensor_tensor(flat(g_dt), flat(g_mt), masks("lowT0"), ALU.mult))
            link(dve.tensor_tensor(flat(g_dt), masks("ident"), flat(g_dt), ALU.subtract))
            link(dve.tensor_tensor(flat(g_ml), flat(g_mt), masks("lowT1"), ALU.mult))
            dve.wait_ge(ev("g_m_ready"), 1)
            link(dve.tensor_tensor(flat(g_d), flat(stat[:, :, :]), masks("low0"), ALU.mult))
            dve.tensor_tensor(flat(g_d), masks("ident"), flat(g_d), ALU.subtract).then_inc(ev("g_d_ready"), 1)
            dve.wait_ge(ev("g_d_ready"), 1)
            for n in range(1, 6):
                dve.wait_ge(ev("g_ddt_ready"), n)
                if n < 5:
                    link(dve.tensor_tensor(flat(g_ml), flat(g_mt), masks(f"lowT{n + 1}"), ALU.mult))
                    dve.wait_ge(ev("g_dd_ready"), n)
                    link(dve.tensor_tensor(g_dt, g_dt, stat[:, :, :], ALU.subtract))
                    dve.tensor_tensor(g_d, g_d, mixp[:, :, :], ALU.subtract).then_inc(ev("g_d_ready"), 1)
                    dve.wait_ge(ev("g_d_ready"), n + 1)
                else:
                    dve.tensor_tensor(g_dt, g_dt, stat[:, :, :], ALU.subtract).then_inc(ev("g_dt_final"), 1)
            dve.wait_ge(ev("g_u_ready"), 1)
            dve.tensor_copy(g_kb, stat[:, :, :]).then_inc(ev("g_u_copied"), 1)
            dve.wait_ge(ev("g_u_copied"), 1)
            for ch in range(4):
                c, o = ch // 2, 64 * (ch % 2)
                vn, u = g_ml[o:o + 64, :, c * P:(c + 1) * P], g_kb[o:o + 64, :, c * P:(c + 1) * P]
                if ch:
                    dve.wait_ge(ev("g_ws_ready"), ch)
                    dve.tensor_tensor(vn, u, mixbank(0)[o:o + 64, :].rearrange("p (h d) -> p h d", h=4), ALU.subtract)\
                        .then_inc(ev("g_vn_ready"), 1)
                else:
                    dve.tensor_copy(vn, u).then_inc(ev("g_vn_ready"), 1)
                if ch == 3:
                    break
                dve.wait_ge(ev("g_ds_ready"), ch + 1)
                dve.wait_ge(ev("g_o_ready"), ch + 1)
                ds_ = mixbank(1).rearrange("p (h d) -> p h d", h=4)
                if ch:
                    for i in range(4):
                        ins = dve.scalar_tensor_tensor(g_s[:, i, :], g_s[:, i, :], g_er[:, i, ch * 64 + 63:ch * 64 + 64],
                                                       ds_[:, i, :], ALU.mult, ALU.add)
                else:
                    ins = dve.tensor_copy(g_s, ds_)
                ins.then_inc(ev("g_s_ready"), 1)
                dve.wait_ge(ev("g_s_ready"), ch + 1)
            dve.wait_ge(ev("g_o_ready"), 4)
            dve.tensor_copy(ybr[:, 8:12, :], stat[:, :, :]).then_inc(ev("g_o_read"), 1)
            dve.wait_ge(ev("g_o_read"), 1)
            dve.wait_ge(rs_ready, seen(rs_ready))
            link(dve.scalar_tensor_tensor(ybr[:, 8:12, :], ybr[:, 8:12, :], col("gdn_norm"), rs[:, :, :], ALU.mult, ALU.mult))
            dve.tensor_tensor(ybr[:, 8:12, :], ybr[:, 8:12, :], gg, ALU.mult).then_inc(ev("yc_done"), 1)
            link(dve.tensor_scalar(qn, col("sb_qn"), P ** -0.5, None, ALU.mult))
            dve.wait_ge(rs_ready, seen(rs_ready))
            dve.scalar_tensor_tensor(sq_kv[:, 0:4, :], sq_kv[:, 0:4, :], qn, rs[:, :, :], ALU.mult, ALU.mult).then_inc(ev("b_q_ready"), 1)
            dve.wait_ge(rs_ready, seen(rs_ready))
            dve.scalar_tensor_tensor(sq_kv[:, 4:8, :], sq_kv[:, 4:8, :], col("sb_kn"), rs[:, :, :], ALU.mult, ALU.mult)\
                .then_inc(ev("b_qk_ready"), 1)
            for c in range(NT):
                dve.wait_ge(ev("b_vt_turned"), c + 1)
                dve.tensor_copy(b_vt[:, c, :], mixbank(c)).then_inc(ev("b_vt_copied"), 1)
            dve.wait_ge(ev("b_l_ready"), 1)
            for k in range(2):
                s = slice(2 * k, 2 * k + 2)
                dve.scalar_tensor_tensor(b_lb[:, s, :], zbanks(k), 0.0, b_l[:, s, :], ALU.min, ALU.subtract)
                ins = dve.scalar_tensor_tensor(b_nk[:, s, :], zbanks(k), 0.0, b_l[:, s, :], ALU.max, ALU.add)
            link(ins)
            before = K["before"].unsqueeze(1).broadcast_to([P, 4, P])
            dve.tensor_tensor(b_nk[:, :, 0:P], b_nk[:, :, 0:P], before, ALU.mult)
            dve.tensor_tensor(b_nk[:, :, T:3 * P], b_nk[:, :, T:3 * P], before, ALU.mult).then_inc(ev("b_nk_ready"), 1)
            dve.wait_ge(ev("b_after_ready"), 1)
            for k in range(2):
                s = slice(2 * k, 2 * k + 2)
                ins = dve.tensor_tensor(b_lb[:, s, :], b_lb[:, s, :], zbanks(k), ALU.subtract)
            ins.then_inc(ev("b_lb_ready"), 1)
            dve.wait_ge(ev("b_exp_ready"), 1)
            dve.tensor_tensor(b_l[:, :, 0:P], b_l[:, :, 0:P], before, ALU.mult)
            dve.tensor_tensor(b_l[:, :, T:3 * P], b_l[:, :, T:3 * P], before, ALU.mult).then_inc(ev("b_att_ready"), 1)
            dve.memset(merged[:, :, :], 0.0).then_inc(ev("gated"), 1)
            dve.wait_ge(ev("gated"), 1)
            dve.wait_ge(ev("b_o_ready"), 1)
            dve.tensor_copy(ybr[:, 4:8, :], stat[:, :, :]).then_inc(ev("branches_ready"), 1)
            base = seen.now(dve_step)
            with dve.Fori(0, 3) as it:
                for j in range(0, 12, 3):
                    b = panels.done(j, it, 12)
                    for m in range(2):
                        u = 2 * (j // 3) + m
                        panels.taken(j + 1 + m, it, 3)
                        dve.tensor_tensor(gtmp, gates8[:, u, :], lin[b][:, m * T:(m + 1) * T], ALU.mult).then_inc(ev("gated"), 1)
                        dve.wait_ge(ev("gated"), it * 8 + (u + 2))
                        ins = dve.tensor_tensor(merged[:, u, :], merged[:, u, :], gtmp, ALU.add)
                        if m == 0:
                            ins.then_inc(dve_step, 1)
                            dve.wait_ge(dve_step, it * 4 + (base + j // 3 + 1))
                        else:
                            ins.then_inc(bank_free[b], 1)
                            panels.taken(j, it, 3)
            seen(dve_step, 12)
            panels.advance(36)
            residual(8, lambda m: mod[:, 2 * KD + m:2 * KD + m + 1])
            panels.settled()
            modulated(1)
            dve.memset(e_dT, 0.0).then_inc(M["dT"], 1)
            dve.memset(e_yb, 0.0).then_inc(M["yb"], 1)
            dve.memset(e_sg, 0.0).then_inc(M["hid"], 1)
            dve.wait_ge(ev("logits_ready"), 1)
            a0 = ROWS["b_route"][0]
            link(dve.tensor_tensor(r_lg, mixbank(0)[:, 0:72].rearrange("p (c n) -> p c n", c=NT),
                                   rows[:, a0:a0 + 36].unsqueeze(1).broadcast_to([P, NT, 36]), ALU.add))

            def wide(ap, n):
                return ap.unsqueeze(2).broadcast_to([P, NT, n])

            def iota(n):
                return K["iota_e"][:, 0:n].unsqueeze(1).broadcast_to([P, NT, n])

            def first_max(onehot, values, best, n):
                link(dve.tensor_reduce(best, values, AX, ALU.max))
                link(dve.tensor_tensor(onehot, values, wide(best, n), ALU.is_equal))
                link(dve.scalar_tensor_tensor(onehot, onehot, -1000.0, iota(n), ALU.mult, ALU.add))
                link(dve.tensor_reduce(r_at, onehot, AX, ALU.min))
                link(dve.tensor_scalar(r_at, r_at, 1000.0, None, ALU.add))
                link(dve.tensor_tensor(onehot, iota(n), wide(r_at, n), ALU.is_equal))

            groups, experts = r_lg[:, :, 0:EG], r_lg[:, :, EG:EG + E]
            first_max(r_goh, groups, r_best, EG)
            dve.tensor_tensor(r_ge, groups, wide(r_best, EG), ALU.subtract).then_inc(ev("route_in"), 1)
            for c in range(NT):
                v = experts[:, c, :].rearrange("p (g e) -> p g e", g=EG)
                dst = r_ml[:, c, :].rearrange("p (g e) -> p g e", g=EG)
                mask = r_goh[:, c, :].unsqueeze(2).broadcast_to([P, EG, E // EG])
                link(dve.tensor_tensor(dst, v, mask, ALU.mult))
            link(dve.tensor_scalar(r_goh, r_goh, -1.0, -NEG, ALU.add, ALU.mult))
            for c in range(NT):
                dst = r_ml[:, c, :].rearrange("p (g e) -> p g e", g=EG)
                mask = r_goh[:, c, :].unsqueeze(2).broadcast_to([P, EG, E // EG])
                link(dve.tensor_tensor(dst, dst, mask, ALU.add))
            first_max(r_oh1, r_ml, r_m1, E)
            link(dve.scalar_tensor_tensor(r_ml, r_oh1, NEG, r_ml, ALU.mult, ALU.add))
            first_max(r_oh2, r_ml, r_m2, E)
            dve.tensor_tensor(r_e2, r_m2, r_m1, ALU.subtract).then_inc(ev("top_in"), 1)
            dve.tensor_tensor(assign, r_oh1, r_oh2, ALU.add).then_inc(ev("assigned"), 1)
            dve.wait_ge(ev("assigned"), 1)
            for g in range(4):
                dve.wait_ge(ev("ht_turned"), g + 1)
                dve.tensor_copy(h_tm[:, g // 2, (g % 2) * 512:(g % 2 + 1) * 512], mixbank(1)).then_inc(ev("ht_copied"), 1)
            dve.wait_ge(ev("group_exp"), 1)
            link(dve.tensor_reduce(r_pg, r_ge, AX, ALU.add))
            link(dve.reciprocal(r_pg, r_pg))
            dve.wait_ge(ev("top_exp"), 1)
            link(dve.tensor_scalar(r_w1, r_e2, 1.0, None, ALU.add))
            link(dve.reciprocal(r_w1, r_w1))
            link(dve.tensor_tensor(r_w1, r_w1, r_pg, ALU.mult))
            link(dve.tensor_tensor(r_w2, r_w1, r_e2, ALU.mult))
            link(dve.tensor_tensor(r_oh1, r_oh1, wide(r_w1, E), ALU.mult))
            link(dve.tensor_tensor(r_oh2, r_oh2, wide(r_w2, E), ALU.mult))
            link(dve.memset(rankp, -1.0))
            link(dve.memset(wp, 0.0))
            dve.wait_ge(ev("ranks_ready"), 1)
            ranks = mixbank(0)[:, 0:2 * E].rearrange("p (c n) -> p c n", c=NT)
            link(dve.scalar_tensor_tensor(r_rank, ranks, 1.0, assign, ALU.add, ALU.mult))
            link(dve.tensor_scalar(r_rank, r_rank, -1.0, None, ALU.add))
            for p in range(PASSES):
                dve.tensor_scalar(rankp[:, :, p * E:(p + 1) * E], r_rank, -float(p * SLOTS), None, ALU.add)
                ins = dve.tensor_tensor(wp[:, :, p * E:(p + 1) * E], r_oh1, r_oh2, ALU.add)
            link(ins)
            link(dve.tensor_reduce(r_cnt, mixbank(0)[:, 2 * E:3 * E], AX, ALU.max))
            dve.tensor_scalar(flag_i, r_cnt, float(SLOTS), None, ALU.is_gt).then_inc(M["flag"], 1)

            def select(dst, e):
                for c in range(NT):
                    ins = dve.tensor_scalar(dst[:, c, :], K["iota"][:, 0:SLOTS], rankp[:, c, e], None, ALU.is_equal)
                ins.then_inc(M["sel"], 1)

            def weigh(dst, e):
                for c in range(NT):
                    ins = dve.tensor_scalar(dst[:, c, :], K["iota"], rankp[:, c, e], wp[:, c, e], ALU.is_equal, ALU.mult)
                ins.then_inc(M["selw"], 1)

            def gathered():
                dve.tensor_copy(e_hg, statbank(0)).then_inc(M["hg"], 1)

            select(e_sel[:, 0, :, :], slice(0, 1))
            select(e_sel[:, 1, :, :], slice(1, 2))
            weigh(e_selw[:, 0, :, :], slice(0, 1))
            dve.wait_ge(M["A"], 1)
            gathered()
            dve.wait_ge(M["A"], 2)
            dve.wait_ge(M["B"], 1)
            gathered()

            def moe_step(it, s):
                dve.wait_ge(M["A"], it * 2 + (s + 1))
                select(e_sel[:, s, :, :], ds(it * 2 + (s + 2), 1))
                dve.wait_ge(M["silu"], it * 2 + (s + 1))
                dve.tensor_tensor(e_hid, e_sg, mixbank(0)[:, T:2 * T], ALU.mult).then_inc(M["hid"], 1)
                dve.wait_ge(M["D"], it * 2 + (s + 1))
                dve.tensor_copy(e_dT, mixbank(1)).then_inc(M["dT"], 1)
                weigh(e_selw[:, 1 - s, :, :], ds(it * 2 + (s + 1), 1))
                dve.wait_ge(M["A"], it * 2 + (s + 3))
                gathered()

            with dve.Fori(0, E // 2) as it:
                moe_step(it, 0)
                moe_step(it, 1)
            more = dve.value_load(flag_i[0:1, 0:1], min_val=0, max_val=1)
            with dve.If(more == 1):
                with dve.Fori(E // 2, NE // 2) as it:
                    moe_step(it, 0)
                    moe_step(it, 1)
            dve.wait_ge(M["y"], 1)
            for m in range(KD):
                dve.scalar_tensor_tensor(x[:, m, :], lin[m // 2][:, (m % 2) * T:(m % 2 + 1) * T],
                                         mod[:, 5 * KD + m:5 * KD + m + 1], x[:, m, :], ALU.mult, ALU.add)\
                    .then_inc(ev("x_out"), 1)


WEIGHTS = ["even_w_in", "even_w_out", "odd_w_qkv", "odd_w_o", "ffn_w_up", "ffn_w_down", "w_ada"]


def kernel(**inputs):
    import numpy as _np
    import concourse.bacc as _bacc
    from concourse import mybir as _mybir
    from concourse.bass_utils import run_bass_kernel_spmd as _run

    def tiles(v):
        return _np.asarray(v).reshape(-1, P).T

    g = {k: _np.asarray(v) for k, v in inputs.items()}
    source = {
        "even_norm": g["even_norm_g"], "b_in": g["even_b_in"], "vln_g": g["even_v_ln_g"], "vln_b": g["even_v_ln_b"],
        "conv_w": g["even_conv_w"], "conv_b": g["even_conv_b"], "cln_g": g["even_conv_ln_g"], "cln_b": g["even_conv_ln_b"],
        "odd_norm": g["odd_norm_g"], "ffn_norm": g["ffn_norm_g"], "ffn_cw": g["ffn_conv_w"], "ffn_cb": g["ffn_conv_b"],
        "final_norm": g["final_norm_g"], "c": g["c_2"], "b_ada": g["b_ada_2"], "norm_mix": g["norm_mix_2"],
        "norm_ffn": g["norm_ffn_2"], "ssm_cw": g["ssm_conv_w_2"], "ssm_cb": g["ssm_conv_b_2"], "ssm_norm": g["ssm_norm_2"],
        "ssm_d": _np.repeat(g["ssm_d_2"], HD), "sb_qn": g["sb_q_norm_2"], "sb_kn": g["sb_k_norm_2"],
        "gdn_cw": g["gdn_conv_w_2"], "gdn_norm": g["gdn_norm_2"],
    }
    layout, _ = col_layout()
    arrays = {
        "cols": _np.ascontiguousarray(_np.concatenate([tiles(source[k]) for k in layout], axis=1)),
        "x": _np.ascontiguousarray(g["x"][0].T.reshape(KD, P, T).transpose(1, 0, 2)),
        "consts": _np.concatenate(list(const_arrays().values()), axis=1),
        "rows": _np.concatenate([v.reshape(-1) for v in (
            g["even_b_s"], g["b_group_2"], g["b_router_2"], g["ssm_dt_bias_2"], g["gdn_dt_bias_2"], g["ssm_a_log_2"],
            g["gdn_a_log_2"])]),
        "even_w_s": _np.ascontiguousarray(g["even_w_s"][0].transpose(2, 0, 1)),
        "w_small": _np.ascontiguousarray(_np.concatenate(
            [g["w_in_2"][0][:, DT0:DT0 + 8], g["w_in_2"][0][:, GAB0:GAB0 + 8], g["w_group_2"][0], g["w_router_2"][0]],
            axis=1).reshape(KD, P, 52).transpose(1, 0, 2)),
        "even_w_in": g["even_w_in"][0], "even_w_out": g["even_w_out"][0], "odd_w_qkv": g["odd_w_qkv"][0],
        "odd_w_o": g["odd_w_o"][0], "ffn_w_up": g["ffn_w_up"], "ffn_w_down": g["ffn_w_down"], "w_ada": g["w_ada_2"][0],
        "w_in": g["w_in_2"][0], "w_branch": g["w_branch_2"][0], "w_out": g["w_out_2"][0],
        "w_gate": g["w_gate_2"][0], "w_up": g["w_up_2"][0], "w_down": g["w_down_2"][0],
    }
    nc = _bacc.Bacc("TRN2", target_bir_lowering=False, num_devices=1)
    aps = {k: nc.dram_tensor(f"in_{k}", v.shape, _mybir.dt.float32, kind="ExternalInput").ap() for k, v in arrays.items()}
    out = nc.dram_tensor("out_x", (P, KD, T), _mybir.dt.float32, kind="ExternalOutput").ap()
    program(nc, aps, out)
    r = _run(nc, [{f"in_{k}": v for k, v in arrays.items()}], core_ids=[0])
    y = r.results[0]["out_x"]
    return y.transpose(2, 1, 0).reshape(1, T, D)
```

```python
from contextlib import ExitStack

import numpy as np

import concourse.bass as bass
from concourse import mybir

F32 = mybir.dt.float32
F32R = mybir.dt.float32r
I32 = mybir.dt.int32
ALU = mybir.AluOpType
ACT = mybir.ActivationFunctionType
AX = mybir.AxisListType.X
ds = bass.ds

P = 128
T = 256
NT = T // P
D = 1024
KD = D // P
HALF = 512
KH = HALF // P
CONV = 31
FF = 2816
KF = FF // P
HEADS = 16
HD = 64
EPS = 1e-6
NEG = -1e30
RING = 4
ADA0 = 24
E = 32
EG = 4
SLOTS = 64
PASSES = T // SLOTS
NE = E * PASSES

Z0, XBC0, DT0, SB0, GQ0, GAB0, GG0, BR0 = 0, 512, 1536, 1544, 3080, 4616, 4624, 5136


LN_PANELS = 16
OUT0 = LN_PANELS + ADA0
QKV1 = OUT0 + KD + 3 * KF
ADA1 = QKV1 + 3 * KD
OUT1 = ADA1 + 48 - ADA0
BLOCK2 = OUT1 + KD + 3 * KF


def is_split(n):
    return OUT0 <= n < ADA1 or OUT1 <= n < BLOCK2


def splits_before(n):
    return sum(is_split(m) for m in range(n))


POOL_SLOT = 3


def lower_parts(n, slots):
    return sum(is_split(m) and m % RING in slots for m in range(n))


def col_layout():
    sizes = [("even_norm", 8), ("b_in", 16), ("vln_g", 4), ("vln_b", 4), ("conv_w", CONV * 4), ("conv_b", 4),
             ("cln_g", 4), ("cln_b", 4), ("odd_norm", 8), ("ffn_norm", 16), ("ffn_cw", 2 * 3 * 44),
             ("ffn_cb", 2 * 44), ("final_norm", 8), ("c", 8), ("b_ada", 48), ("norm_mix", 8), ("norm_ffn", 8),
             ("ssm_cw", 32), ("ssm_cb", 8), ("ssm_norm", 4), ("ssm_d", 4), ("sb_qn", 1), ("sb_kn", 1),
             ("gdn_cw", 48), ("gdn_norm", 1)]
    at, out = 0, {}
    for name, n in sizes:
        out[name] = (at, n)
        at += n
    return out, at


def const_arrays():
    j = np.arange(P)[:, None]
    t = np.arange(P)[None, :]
    same = (j // 64) == (t // 64)
    d = np.arange(P) % HD
    inv = (10000.0 ** (-np.arange(HD // 2, dtype=np.float32) / np.float32(HD // 2))).astype(np.float32)
    ang = (np.arange(T, dtype=np.float32)[None, :] * inv[d % 32][:, None]).astype(np.float32)
    swap = np.zeros((P, P), np.float32)
    for p in range(P):
        if p % HD < 32:
            swap[p + 32, p] = -1.0
        else:
            swap[p - 32, p] = 1.0

    def pattern_bias(q0, k0):
        q = q0 + np.arange(P)[:, None]
        k = k0 + np.arange(P)[None, :]
        n = np.zeros((P, P))
        for dil in (1, 4, 16):
            n += (k <= q) & ((q - k) % dil == 0) & ((q - k) // dil <= P)
        return np.where(n > 0, np.log(np.maximum(n, 1)), NEG)

    out = {
        "eps": np.full((P, 1), EPS), "one": np.ones((P, 1)), "ones": np.ones((P, P)),
        "ident": j == t, "mean512": np.full((P, P), 1.0 / HALF),
        "upto": j <= t, "before": j < t, "after": j > t,
        "cos": np.cos(ang), "sin": np.sin(ang), "swap": swap,
        "bias00": pattern_bias(0, 0), "bias10": pattern_bias(P, 0), "bias11": pattern_bias(P, P),
        "neg_causal": np.where(j <= t, 0.0, NEG),
        "upto64": (j <= t) & same, "ones64": same, "neg_causal64": np.where((j <= t) & same, 0.0, NEG),
        "before64": (j < t) & same,
        "iota": np.tile(np.arange(P) % SLOTS, (P, 1)), "iota_e": np.tile(np.arange(E), (P, 1)),
        "diag32": (j % 32) == np.arange(32)[None, :],
    }
    for n in range(6):
        b = 1 << n
        low = (j // (2 * b) == t // (2 * b)) & (j // b % 2 == 1) & (t // b % 2 == 0)
        if n == 0:
            out["low0"] = low
        out[f"lowT{n}"] = low.T
    return {k: np.ascontiguousarray(v, dtype=np.float32) for k, v in out.items()}


ROWS = {"b_s": (0, 1024), "b_route": (1024, 36), "dt_bias": (1060, 8), "gdn_dt_bias": (1068, 4),
        "a_log": (1072, 8), "gdn_a_log": (1080, 4)}
NROWS = 1084


class Seen:

    def __init__(self):
        self.n = {}

    def __call__(self, sem, k=1):
        self.n[sem.name] = self.n.get(sem.name, 0) + k
        return self.now(sem)

    def now(self, sem):
        return self.n.get(sem.name, 0)


class Arena:

    def __init__(self, tensor, size):
        self.t, self.at, self.size = tensor, 0, size

    def take(self, n):
        self.at += n
        assert self.at <= self.size, self.at
        return self.t[:, self.at - n:self.at]


def program(nc, A, out):
    cols, ncols = col_layout()
    consts = const_arrays()
    ctx = ExitStack()
    with ctx:
        def sb(name, shape, dt=F32):
            return ctx.enter_context(nc.sbuf_tensor(name, shape, dt))

        def sem(name):
            return ctx.enter_context(nc.semaphore(name))

        x = sb("x", [P, KD, T])
        h = sb("h", [P, KD, T])
        sq = sb("sq", [P, KD, T])
        rs = sb("rs", [P, 4, T])
        cat = sb("cat", [P, KD, T])
        ring = sb("ring", [P, RING, D])
        colp = sb("colp", [P, ncols])
        nconst = sum(v.shape[1] for v in consts.values())
        cst = sb("cst", [P, nconst])
        rows = sb("rows", [P, NROWS])
        mod = sb("mod", [P, 48])
        gains = sb("gains", [P, 2 * KD])
        modraw = sb("modraw", [P, 24, 32])[:, :, :]
        c_act = sb("c_act", [P, KD])
        ARENA = 33008
        K, at = {}, 0
        for name, v in consts.items():
            K[name] = cst[:, at:at + v.shape[1]]
            at += v.shape[1]

        def col(name, i=0, n=1):
            a = cols[name][0] + i
            return colp[:, a:a + n]

        def row(name):
            a, m = ROWS[name]
            return rows[:, a:a + m]

        with ExitStack() as first_block:
            def sb1(name, shape, dt=F32, stack=first_block):
                return stack.enter_context(nc.sbuf_tensor(name, shape, dt))

            w_hi, w_lo = sb1("w_hi", [P, RING, D], F32R), sb1("w_lo", [P, RING, D], F32R)
            r_hi, r_lo = sb1("r_hi", [P, KD, T], F32R), sb1("r_lo", [P, KD, T], F32R)
            with ExitStack() as mixers:
                MIXERS = 14016
                mixers_t = sb1("mixers", [P, MIXERS], stack=mixers)
            hid_hi, hid_lo = sb1("hid_hi", [P, KF, T], F32R), sb1("hid_lo", [P, KF, T], F32R)
            ub = sb1("ub", [P, 4, T])
            sgf = sb1("sgf", [P, 2, T])
        arena_t = sb("arena", [P, ARENA])

        lin = [ctx.enter_context(nc.psum_tensor(f"lin{b}", [P, 512], F32)) for b in range(4)]
        stat = ctx.enter_context(nc.psum_tensor("stat", [P, 4, T], F32))
        mixp = ctx.enter_context(nc.psum_tensor("mixp", [P, 4, T], F32))

        consts_loaded = sem("consts_loaded")
        extra_loaded = sem("extra_loaded")
        panel_loaded = [sem(f"panel_loaded{b}") for b in range(RING)]
        panel_done = sem("panel_done")
        w_hi_ready = sem("w_hi_ready")
        w_split = sem("w_split")
        w_split_pool = sem("w_split_pool")
        r_split = sem("r_split")
        bank_free = [sem(f"bank_free{b}") for b in range(4)]
        sq_ready = sem("sq_ready")
        sums_ready = sem("sums_ready")
        ln_done = sem("ln_done")
        rs_ready = sem("rs_ready")
        mean_ready = sem("mean_ready")
        centred = sem("centred")
        h_ready = sem("h_ready")
        dve_step = sem("dve_step")
        act_step = sem("act_step")
        tap0_done = sem("tap0_done")
        silu_done = sem("silu_done")
        act_tile = sem("act_tile")
        conv_step = sem("conv_step")
        v_normed = sem("v_normed")
        vt_ready = sem("vt_ready")
        vt_copied = sem("vt_copied")
        mixed_ready = sem("mixed_ready")
        ya_ready = sem("ya_ready")
        yb_normed = sem("yb_normed")
        yb_ready = sem("yb_ready")
        rot_ready = sem("rot_ready")
        qk_ready = sem("qk_ready")
        vt1_ready = sem("vt1_ready")
        vt1_copied = sem("vt1_copied")
        scores_ready = sem("scores_ready")
        scores_read = sem("scores_read")
        max_ready = sem("max_ready")
        exp_ready = sem("exp_ready")
        probs_ready = sem("probs_ready")
        pt_ready = sem("pt_ready")
        pt_copied = sem("pt_copied")
        o_ready = sem("o_ready")
        o_copied = sem("o_copied")
        mod_copied = sem("mod_copied")
        stored = sem("stored")
        events = {}

        def ev(name):
            if name not in events:
                events[name] = sem(name)
            return events[name]

        wsmall = sb("wsmall", [P, KD, 52])
        S2 = Arena(arena_t, ARENA)

        def buf(*shape, of=None):
            n = int(np.prod(shape))
            ap = (of or S2).take(n)
            names = "abcd"[:len(shape)]
            return ap if len(shape) == 1 else ap.rearrange(
                f"p ({' '.join(names)}) -> p {' '.join(names)}", **{k: s for k, s in zip(names[1:], shape[1:])})

        xb = buf(8, T)
        zs = buf(KH, T)
        gq = buf(12, T)
        gg = buf(KH, T)
        sq_kv = buf(12, T)
        ybr = buf(12, T)
        spin, spl, spe = buf(NT, 12), buf(NT, 12), buf(NT, 12)
        adt = buf(NT, 12)
        beta, beta_in, eg, beg, kdec = (buf(NT, 4) for _ in range(5))
        ea = buf(12)
        cums = buf(NT, 24)
        mdec, mdif, gdif = buf(NT, 8), buf(NT, 8), buf(NT, 4)
        qn = buf(1)
        g_kt, g_vt, g_er, g_kb, g_qd, g_dec, g_mt, g_at, g_d, g_dt, g_w, g_ml, g_r2 = (buf(4, T) for _ in range(13))
        g_s = buf(4, P)
        mark = S2.at
        m_xt, m_bt, m_xdd, m_g = buf(NT, HALF), buf(T), buf(HALF), buf(2, T)
        m_er, m_cd, m_h = buf(8, P), buf(8, P), buf(HALF)
        m_seg = cat
        S2.at = mark
        b_vt, b_l, b_lb, b_nk = buf(NT, HALF), buf(4, 3 * P), buf(4, 3 * P), buf(4, 3 * P)
        merged = cat
        BRANCHES = (0, 2, 1)
        gates8, gtmp = xb, zs[:, 0, :]
        gated = sem("gated")

        def zbanks(k):
            ps = (mixp, stat)[k][:, :, :].rearrange("p (b a) t -> p b (a t)", b=2)
            return ps[:, :, 0:3 * P]


        a = Arena(arena_t, ARENA)
        e_wg, e_wu = buf(2, KD, HALF, of=a), buf(2, KD, HALF, of=a)
        e_wd = buf(2, KH, D, of=a)
        h_tm = buf(NT, D, of=a)
        e_sel, e_selw = buf(2, NT, SLOTS, of=a), buf(2, NT, P, of=a)
        e_hg, e_hgT_flat, e_sg, e_hid, e_yb = buf(512, of=a), buf(512, of=a), buf(T, of=a), buf(T, of=a), buf(512, of=a)
        e_hgT = e_hgT_flat.rearrange("p (j h s) -> p j h s", j=4, h=2)
        e_dT = buf(512, of=a)
        e_hidT = e_dT[:, 0:T].rearrange("p (j h s) -> p j h s", j=2, h=2)
        rankp, wp = buf(NT, NE + 2, of=a), buf(NT, NE + 2, of=a)
        r_lg, r_ml, r_oh1, r_oh2, assign, r_rank = (buf(NT, n, of=a) for n in (36, E, E, E, E, E))
        r_goh, r_ge = buf(NT, EG, of=a), buf(NT, EG, of=a)
        r_best, r_at, r_m1, r_m2, r_e2, r_pg, r_w1, r_w2 = (buf(NT, of=a) for _ in range(8))
        r_cnt = buf(1, of=a)
        flag_i = ctx.enter_context(nc.sbuf_tensor("flag_i", [P, 1], I32))[:, :]
        M = {n: sem(f"moe_{n}") for n in ("gu_loaded0", "gu_loaded1", "d_loaded0", "d_loaded1", "sel", "selw", "hg", "hgT",
                                          "silu", "hid", "dT", "yb", "A", "B", "C", "D", "E", "F", "y", "flag")}

        class Panels:

            def __init__(self, eng):
                self.eng, self.n, self.free = eng, 0, [0] * 4

            def done(self, j=0, it=None, per=RING):
                self.eng.wait_ge(panel_done, self.n + j + 1 if it is None else it * per + (self.n + j + 1))
                return (self.n + j) % RING

            def taken(self, j, it=None, per=1):
                b = (self.n + j) % RING
                v = self.free[b] + j // RING + 1
                self.eng.wait_ge(bank_free[b], v if it is None else it * per + v)

            def advance(self, k):
                for _ in range(k):
                    self.free[self.n % RING] += 1
                    self.n += 1

            def advance_down(self):
                self.n += KF
                self.free = [f + 1 for f in self.free]

            def settled(self):
                for b in range(4):
                    self.eng.wait_ge(bank_free[b], self.free[b])

        def wait_split(eng, n, it=None):
            slots = (POOL_SLOT,) if n % RING == POOL_SLOT else [s for s in range(RING) if s != POOL_SLOT]
            event = w_split_pool if n % RING == POOL_SLOT else w_split
            v = lower_parts(n, slots) + 1
            eng.wait_ge(event, v if it is None else it * len(slots) + v)

        def panel_src(w, m, k=KD):
            return w.rearrange("(k p) n -> p k n", p=P)[:, 0:k, ds(m * P, P)]

        a = Arena(mixers_t, MIXERS)
        PADC = CONV - 1
        u0 = a.take(KH * T).rearrange("p (k t) -> p k t", k=KH)
        v0 = a.take(KH * T).rearrange("p (k t) -> p k t", k=KH)
        sg0 = a.take(KH * T).rearrange("p (k t) -> p k t", k=KH)
        hc0 = a.take(KH * (T + PADC)).rearrange("p (k t) -> p k t", k=KH)
        cv0 = a.take(KH * T).rearrange("p (k t) -> p k t", k=KH)
        xc0 = a.take(KH * T).rearrange("p (k t) -> p k t", k=KH)
        vt0 = a.take(NT * HALF).rearrange("p (c f) -> p c f", c=NT)
        ws0 = a.take(8 * P).rearrange("p (h t) -> p h t", h=8)
        wsm0 = a.take(8 * P).rearrange("p (h t) -> p h t", h=8)

        a = Arena(mixers_t, MIXERS)
        qk1 = a.take(16 * T).rearrange("p (k t) -> p k t", k=16)
        qs1 = a.take(2 * T).rearrange("p (k t) -> p k t", k=2)
        rc1 = a.take(2 * T).rearrange("p (k t) -> p k t", k=2)
        v1 = a.take(8 * T).rearrange("p (k t) -> p k t", k=8)
        vt1 = a.take(NT * D).rearrange("p (c f) -> p c f", c=NT)
        SC = 3 * P
        s1 = a.take(4 * SC).rearrange("p (b s) -> p b s", b=4)
        p1 = a.take(4 * SC).rearrange("p (b s) -> p b s", b=4)
        pt1 = a.take(4 * SC).rearrange("p (b s) -> p b s", b=4)
        mx1 = a.take(2 * HEADS)
        l1 = a.take(2 * HEADS)
        r1 = a.take(2 * HEADS)

        block = ctx.enter_context(nc.Block())

        def statbank(n):
            return stat[:, 2 * (n % 2):2 * (n % 2) + 2, :].rearrange("p a t -> p (a t)")

        def mixbank(n):
            return mixp[:, 2 * (n % 2):2 * (n % 2) + 2, :].rearrange("p a t -> p (a t)")

        def downbank(n):
            return statbank(n) if n < 2 else mixbank(n)

        @block.sync
        def _(sp):
            seen = Seen()
            n_panels = [0]
            panels_seen = Panels(sp)

            def load_panel(dst_shape, src, j=None, it=None, per=RING):
                n = n_panels[0] + (j or 0)
                slot = n % RING
                dst = ring[:, slot, :]
                if dst_shape is not None:
                    dst = dst[:, 0:dst_shape[0] * dst_shape[1]].rearrange("p (k n) -> p k n", k=dst_shape[0])
                if n >= RING and is_split(n - RING):
                    wait_split(sp, n - RING, it)
                elif it is not None:
                    sp.wait_ge(panel_done, it * per + (n - RING + 1))
                elif n >= RING:
                    sp.wait_ge(panel_done, n - RING + 1)
                sp.dma_start(dst, src).then_inc(panel_loaded[slot], 16)
                if it is None:
                    n_panels[0] += 1

            def load_columns(w, tiles, k=KD):
                for m in tiles:
                    load_panel((k, P), panel_src(w, m, k))

            sp.dma_start(x[:, :, :], A["x"]).then_inc(consts_loaded, 16)
            early = 2 + P
            sp.dma_start(cst[:, 0:early], A["consts"][:, 0:early]).then_inc(consts_loaded, 16)
            sp.dma_start(colp[:, :], A["cols"]).then_inc(consts_loaded, 16)
            for j in range(4):
                load_columns(A["even_w_in"], [12 + j, 8 + j])
                if j == 1:
                    sp.dma_start(cst[:, early:], A["consts"][:, early:]).then_inc(extra_loaded, 16)
                    sp.dma_start(rows[:, :], A["rows"].partition_broadcast(P)).then_inc(extra_loaded, 16)
                    sp.dma_start(ws0[:, :, :], A["even_w_s"]).then_inc(extra_loaded, 16)
                    sp.dma_start(wsmall[:, :, :], A["w_small"]).then_inc(extra_loaded, 16)
            load_columns(A["even_w_in"], range(4, 8))
            load_columns(A["even_w_in"], range(0, 4))
            panels_seen.advance(16 + ADA0)
            with sp.Fori(0, ADA0 // 4) as it:
                for j in range(4):
                    load_panel((KD, P), A["w_ada"].rearrange("(k p) n -> p k n", p=P)[:, :, ds(it * 512 + j * P, P)],
                               j, it)
            n_panels[0] += ADA0
            load_columns(A["even_w_out"], range(8))
            panels_seen.advance(8)

            def load_ffn(l):
                up = A["ffn_w_up"][l].rearrange("(k p) n -> p k n", p=P)
                with sp.Fori(0, KF // 2) as it:
                    for j in range(4):
                        load_panel((KD, P), up[:, :, ds(it * 2 * P + (j // 2) * P + (j % 2) * FF, P)], j, it)
                n_panels[0] += 2 * KF
                down = A["ffn_w_down"][l].rearrange("(k p) n -> p k n", p=P)
                for k in (0, 1):
                    load_panel(None, down[:, k, :])
                with sp.Fori(0, 4) as it:
                    for j in range(4):
                        load_panel(None, down[:, ds(it * 4 + j + 2, 1), :].rearrange("p k n -> p (k n)"), j, it)
                n_panels[0] += 16
                for k in range(18, 22):
                    load_panel(None, down[:, k, :])
                panels_seen.advance(2 * KF)
                panels_seen.advance_down()

            load_ffn(0)
            load_columns(A["odd_w_qkv"], range(24))
            load_columns(A["w_ada"], range(ADA0, 48))
            load_columns(A["odd_w_o"], range(8))
            panels_seen.advance(24)
            panels_seen.n += 48 - ADA0
            panels_seen.advance(8)
            load_ffn(1)
            load_columns(A["w_in"][:, XBC0:DT0], range(8))
            load_columns(A["w_in"][:, Z0:XBC0], range(4))
            load_columns(A["w_in"][:, GQ0:GAB0], range(12))
            load_columns(A["w_in"][:, SB0:GQ0], range(12))
            load_columns(A["w_in"][:, GG0:BR0], range(4))
            panels_seen.advance(40)
            gates = A["w_in"][:, BR0:].rearrange("(k p) n -> p k n", p=P)
            for i in BRANCHES:
                for j in range(12):
                    pair, part = j // 3, j % 3
                    if part == 0:
                        load_panel((KH, T), A["w_branch"][i].rearrange("(k p) n -> p k n", p=P)[:, :, pair * T:(pair + 1) * T])
                    else:
                        tile = i * KD + 2 * pair + part - 1
                        load_panel((KD, P), gates[:, :, tile * P:(tile + 1) * P])
            load_columns(A["w_out"], range(8))
            panels_seen.advance(36)
            panels_seen.settled()
            gate_w = A["w_gate"].rearrange("e (k p) f -> p e k f", p=P)
            up_w = A["w_up"].rearrange("e (k p) f -> p e k f", p=P)
            down_w = A["w_down"].rearrange("e (k p) f -> p e k f", p=P)

            def load_expert(e, s, before=None):
                if before is not None:
                    sp.wait_ge(M["C"], before)
                sp.dma_start(e_wg[:, s, :, :], gate_w[:, e, :, :].rearrange("p e k f -> p (e k) f")).then_inc(M[f"gu_loaded{s}"], 16)
                sp.dma_start(e_wu[:, s, :, :], up_w[:, e, :, :].rearrange("p e k f -> p (e k) f")).then_inc(M[f"gu_loaded{s}"], 16)
                if before is not None:
                    sp.wait_ge(M["E"], before)
                sp.dma_start(e_wd[:, s, :, :], down_w[:, e, :, :].rearrange("p e k f -> p (e k) f")).then_inc(M[f"d_loaded{s}"], 16)

            for s in range(2):
                load_expert(slice(s, s + 1), s)
            with sp.Fori(1, E // 2) as it:
                for s in range(2):
                    load_expert(ds(it * 2 + s, 1), s, it * 2 + (s - 1))
            sp.wait_ge(M["flag"], 1)
            more = sp.value_load(flag_i[0:1, 0:1], min_val=0, max_val=1)
            with sp.If(more == 1):
                for p in range(1, PASSES):
                    with sp.Fori(0, E // 2) as it:
                        for s in range(2):
                            load_expert(ds(it * 2 + s, 1), s, it * 2 + (s - 1 + p * E))
            for half in range(2):
                sp.wait_ge(ev("x_out"), 4 * half + 4)
                sp.dma_start(out[:, 4 * half:4 * half + 4, :], x[:, 4 * half:4 * half + 4, :]).then_inc(stored, 16)
            sp.wait_ge(stored, 32)

        @block.tensor
        def _(pe):
            seen = Seen()
            panels = Panels(pe)

            def panel(j=0, it=None, per=RING):
                n = panels.n + j
                v = 16 * (n // RING + 1)
                pe.wait_ge(panel_loaded[n % RING], v if it is None else it * (16 * per // RING) + v)
                return n % RING

            def bank(b, it=None, per=1, later=0):
                v = panels.free[b] + later
                if it is not None:
                    pe.wait_ge(bank_free[b], it * per + v)
                elif v:
                    pe.wait_ge(bank_free[b], v)

            def split_panel(j=0, it=None):
                n = panels.n + j
                wait_split(pe, n, it)
                return n % RING

            def split_matmul(o, w, r, start, stop):
                slot, c = w
                pe.matmul(o, w_hi[:, slot, c], r[0], start=start, stop=False, skip_group_check=True)
                pe.matmul(o, w_hi[:, slot, c], r[1], start=False, stop=False, skip_group_check=True)
                return pe.matmul(o, w_lo[:, slot, c], r[0], start=False, stop=stop, skip_group_check=True)

            def split_linear(b, first=False):
                for i in range(KD):
                    if first:
                        pe.wait_ge(h_ready, seen(h_ready))
                    mm = split_matmul(lin[b][:, 0:T], (b, slice(i * P, (i + 1) * P)), (r_hi[:, i, :], r_lo[:, i, :]),
                                      i == 0, i == KD - 1)
                mm.then_inc(panel_done, 1)

            def product(b, rhs, k=KD, first=False):
                w = ring[:, b, 0:k * P].rearrange("p (k n) -> p k n", k=k)
                for i in range(k):
                    if first:
                        pe.wait_ge(h_ready, seen(h_ready))
                    mm = pe.matmul(lin[b][:, 0:T], w[:, i, :], rhs[:, i, :], start=i == 0, stop=i == k - 1)
                mm.then_inc(panel_done, 1)

            def linear(rhs, count, k=KD, first=False):
                for m in range(count):
                    b = split_panel() if rhs is None else panel()
                    bank(b)
                    if rhs is None:
                        split_linear(b, first and m == 0)
                    else:
                        product(b, rhs, k, first and m == 0)
                    panels.advance(1)

            def stream_sum(tiles, into=0):
                if tiles[0] == 0 and seen.now(ln_done):
                    pe.wait_ge(ln_done, seen.now(ln_done))
                pe.wait_ge(sq_ready, seen(sq_ready))
                for m in tiles:
                    mm = pe.matmul(stat[:, 0, :], K["ones"], sq[:, m, :], start=m == 0, stop=m == KD - 1,
                                   skip_group_check=True)
                if m == KD - 1:
                    mm.then_inc(sums_ready, 1)
                    seen(ln_done)

            def project(rhs):
                for m in range(KD):
                    linear(rhs, 1)
                    if m >= 2:
                        stream_sum([m - 2])
                for m in (KD - 2, KD - 1):
                    stream_sum([m])

            def sums(src, groups, k):
                pe.wait_ge(sq_ready, seen(sq_ready))
                if seen.now(ln_done):
                    pe.wait_ge(ln_done, seen.now(ln_done))
                for g in range(groups):
                    for i in range(k):
                        mm = pe.matmul(stat[:, g, :], K["ones"], src[:, g * k + i, :], start=i == 0, stop=i == k - 1,
                                       skip_group_check=True)
                mm.then_inc(sums_ready, 1)
                seen(ln_done)

            def mean(src, n):
                for i in range(KH):
                    mm = pe.matmul(mixp[:, 2 * n, :], K["mean512"], src[:, i, :], start=i == 0, stop=i == KH - 1)
                mm.then_inc(mean_ready, 1)

            def ffn():
                for j in range(4):
                    b = split_panel(j)
                    bank(b)
                    split_linear(b, first=j == 0)
                with pe.Fori(1, KF // 2) as it:
                    for j in range(4):
                        b = split_panel(j, it)
                        bank(b, it)
                        split_linear(b)
                panels.advance(2 * KF)
                base = seen.now(act_tile)
                seen(act_tile, KF)

                def down(b, k, first, last):
                    parts = [t[:, k, :].rearrange("p k t -> p (k t)") for t in (hid_hi, hid_lo)]
                    for m in range(KD):
                        mm = split_matmul(downbank(m // 2)[:, (m % 2) * T:(m % 2 + 1) * T], (b, slice(m * P, (m + 1) * P)),
                                          parts, first and m % 2 == 0, last)
                    mm.then_inc(panel_done, 1)

                for k in (0, 1):
                    pe.wait_ge(act_tile, base + k + 1)
                    down(split_panel(k), slice(k, k + 1), k == 0, False)
                with pe.Fori(0, 4) as it:
                    for j in range(4):
                        pe.wait_ge(act_tile, it * 4 + (base + j + 3))
                        down(split_panel(j + 2, it), ds(it * 4 + (j + 2), 1), False, False)
                for k in range(18, KF):
                    pe.wait_ge(act_tile, base + k + 1)
                    down(split_panel(k), slice(k, k + 1), False, k == KF - 1)
                panels.advance_down()
                for b in range(4):
                    stream_sum([2 * b, 2 * b + 1])

            def modulation(b, dst):
                w = ring[:, b, :].rearrange("p (k n) -> p k n", k=KD)
                for i in range(KD):
                    for q in range(4):
                        mm = pe.matmul(dst[32 * q:32 * q + 32, :], c_act[:, i:i + 1].to_broadcast([P, 32]),
                                       w[:, i, 32 * q:32 * q + 32], start=i == 0, stop=i == KD - 1, skip_group_check=True)
                mm.then_inc(panel_done, 1)

            seen(act_tile, 2)
            pe.wait_ge(consts_loaded, 48)
            for m in range(KD):
                stream_sum([m])
            linear(h, 16, first=True)
            panels.settled()
            pe.wait_ge(extra_loaded, 64)
            mean(v0, 0)
            pe.wait_ge(silu_done, seen(silu_done))
            with pe.Fori(0, ADA0 // 4) as it:
                for j in range(4):
                    b = panel(j, it)
                    bank(b, it)
                    modulation(b, lin[b][:, 0:32])
            panels.advance(ADA0)
            sums(sq, 1, KH)
            pe.wait_ge(v_normed, 1)
            for c in range(NT):
                for j in range(KH):
                    mm = pe.transpose(mixbank(c)[:, j * P:(j + 1) * P], v0[:, j, c * P:(c + 1) * P], K["ident"])
                mm.then_inc(vt_ready, 1)
            pe.wait_ge(vt_copied, 2)
            for hh in range(8):
                for c in range(NT):
                    mm = pe.matmul(mixp[64 * (hh % 2):64 * (hh % 2) + 64, hh // 2, c * P:(c + 1) * P],
                                   vt0[:, c, hh * HD:(hh + 1) * HD], wsm0[:, hh, :], start=True, stop=True,
                                   skip_group_check=True)
            mm.then_inc(mixed_ready, 1)
            pe.wait_ge(conv_step, CONV * KH)
            pe.wait_ge(ya_ready, 1)
            mean(cv0, 1)
            sums(sq, 1, KH)
            pe.wait_ge(r_split, 1 + KH)
            project(None)
            ffn()

            def swap_halves(n):
                b = (qk_first + n) % 4
                pe.wait_ge(bank_free[b], panels.free[b])
                if n >= 2:
                    pe.wait_ge(qk_ready, n - 1)
                pe.matmul(stat[:, 2 * (n % 2), :], K["swap"], qs1[:, n % 2, :], start=True, stop=True)\
                    .then_inc(rot_ready, 1)

            qk_first = panels.n
            for n in range(16):
                linear(None, 1, first=n == 0)
                if n:
                    swap_halves(n - 1)
            linear(None, 1)
            swap_halves(15)
            linear(None, 7)
            panels.settled()
            for g in range(4):
                if g >= 2:
                    pe.wait_ge(vt1_copied, g - 1)
                for i in range(4):
                    mm = pe.transpose(mixbank(g)[:, i * P:(i + 1) * P],
                                      v1[:, (g % 2) * 4 + i, (g // 2) * P:(g // 2 + 1) * P], K["ident"])
                mm.then_inc(vt1_ready, 1)
            pe.wait_ge(vt1_copied, 4)
            pe.wait_ge(qk_ready, 16)
            for i in range(HEADS + 3):
                if i < HEADS:
                    if i >= 2:
                        pe.wait_ge(scores_read, i - 1)
                    o = 64 * (i % 2)
                    q, k = qk1[o:o + 64, i // 2, :], qk1[o:o + 64, 8 + i // 2, :]
                    pe.matmul(mixbank(i)[:, 0:P], q[:, 0:P], k[:, 0:P], start=True, stop=True, skip_group_check=True)
                    pe.matmul(mixbank(i)[:, P:3 * P], q[:, P:T], k, start=True, stop=True, skip_group_check=True)\
                        .then_inc(scores_ready, 1)
                if i < HEADS and i % 2 == 1:
                    g = i // 2
                    if g >= 2:
                        pe.wait_ge(mod_copied, g - 1)
                    for r in range(3):
                        b = panel()
                        modulation(b, lin[2 + g % 2][:, 32 * r:32 * r + 32])
                        panels.n += 1
                if 2 <= i <= HEADS + 1:
                    g = i - 2
                    pe.wait_ge(probs_ready, g + 1)
                    if g >= 2:
                        pe.wait_ge(pt_copied, g - 1)
                    for c in range(3):
                        mm = pe.transpose(statbank(g)[:, c * P:(c + 1) * P], p1[:, g % 4, c * P:(c + 1) * P], K["ident"])
                    mm.then_inc(pt_ready, 1)
                if i >= 3:
                    g = i - 3
                    pe.wait_ge(pt_copied, g + 1)
                    if g >= 4 and g % 2 == 0:
                        pe.wait_ge(o_copied, g // 2 - 1)
                    o = lin[(g // 2) % 2][64 * (g % 2):64 * (g % 2) + 64, :]
                    v = [vt1[:, c, g * HD:(g + 1) * HD] for c in range(NT)]
                    pe.matmul(o[:, 0:P], v[0], pt1[:, g % 4, 0:P], start=True, stop=True, skip_group_check=True)
                    pe.matmul(o[:, P:T], v[0], pt1[:, g % 4, P:2 * P], start=True, stop=False, skip_group_check=True)
                    pe.matmul(o[:, P:T], v[1], pt1[:, g % 4, 2 * P:3 * P], start=False, stop=True, skip_group_check=True)\
                        .then_inc(o_ready, 1)
            pe.wait_ge(o_copied, 8)
            pe.wait_ge(mod_copied, 8)
            project(None)
            ffn()
            for m in range(KD):
                stream_sum([m])
            pe.wait_ge(extra_loaded, 64)
            for c in range(NT):
                for i in range(KD):
                    if c == 0:
                        pe.wait_ge(h_ready, seen(h_ready))
                    mm = pe.matmul(mixbank(0)[:, c * 16:(c + 1) * 16], h[:, i, c * P:(c + 1) * P], wsmall[:, i, 0:16],
                                   start=i == 0, stop=i == KD - 1, skip_group_check=True)
            mm.then_inc(ev("small_ready"), 1)
            linear(h, 8)
            pe.wait_ge(ev("adt_ready"), 1)
            for c in range(NT):
                for a0, lhs, b0, n in ((0, "upto", 0, 8), (8, "upto64", 8, 4), (12, "ones64", 8, 4), (16, "ones", 0, 8)):
                    mm = pe.matmul(mixbank(1)[:, c * 24 + a0:c * 24 + a0 + n], K[lhs], adt[:, c, b0:b0 + n],
                                   start=True, stop=True, skip_group_check=True)
            mm.then_inc(ev("cums_ready"), 1)
            linear(h, 16)

            def spread(dst, src, table):
                for i in range(4):
                    for c in range(NT):
                        mm = pe.matmul(dst[:, i, c * P:(c + 1) * P], src(i, c).to_broadcast([P, P]), table,
                                       start=True, stop=True, skip_group_check=True)
                return mm

            def turned(dst, pairs, event):
                for i, s in enumerate(pairs):
                    mm = pe.transpose(dst[:, i * P:(i + 1) * P], s, K["ident"])
                mm.then_inc(event, 1)

            def branch_panels(i, first, last):
                for j in range(first, last):
                    b = panel()
                    bank(b)
                    if j % 3:
                        product(b, h)
                    else:
                        w = ring[:, b, :].rearrange("p (k n) -> p k n", k=KH)
                        for m in range(2):
                            for k in range(KH):
                                mm = pe.matmul(lin[b][:, m * T:(m + 1) * T], w[:, k, m * P:(m + 1) * P], ybr[:, i * KH + k, :],
                                               start=k == 0, stop=k == KH - 1, skip_group_check=True)
                        mm.then_inc(panel_done, 1)
                    panels.advance(1)

            pe.wait_ge(ev("xb_ready"), 1)
            pe.wait_ge(ev("cums_copied"), 1)
            for c in range(NT):
                turned(mixbank(c), [xb[:, j, c * P:(c + 1) * P] for j in range(4)], ev("m_xt_turned"))
            turned(statbank(0), [xb[:, 4 + g, 0:P] for g in range(2)], ev("m_bt_turned"))
            for g in range(2):
                for c in range(NT):
                    mm = pe.matmul(statbank(1)[:, g * T + c * P:g * T + (c + 1) * P], xb[:, 4 + g, c * P:(c + 1) * P],
                                   xb[:, 6 + g, c * P:(c + 1) * P], start=True, stop=True, skip_group_check=True)
            mm.then_inc(ev("m_g_ready"), 1)
            linear(h, 1)
            pe.wait_ge(ev("m_xt_copied"), 2)
            spread(mixp, lambda i, c: adt[:, c, i:i + 1], K["upto"]).then_inc(ev("m_rows_ready"), 1)
            pe.wait_ge(ev("m_g_copied"), 1)
            spread(stat, lambda i, c: adt[:, c, 4 + i:5 + i], K["upto"]).then_inc(ev("m_rows_ready"), 1)
            linear(h, 4)
            pe.wait_ge(ev("m_rows_read"), 1)
            pe.wait_ge(ev("m_rows_exp"), 1)
            pe.wait_ge(ev("m_xdd_ready"), 1)
            for g in range(2):
                mm = pe.matmul(mixbank(0)[:, g * T:(g + 1) * T], m_bt[:, g * P:(g + 1) * P], m_xdd[:, g * T:(g + 1) * T],
                               start=True, stop=True, skip_group_check=True)
            mm.then_inc(ev("m_h_ready"), 1)
            linear(h, 4)
            pe.wait_ge(ev("m_rows_read"), 2)
            pe.wait_ge(ev("m_rows_exp"), 2)
            pe.wait_ge(ev("m_h_copied"), 1)
            pe.wait_ge(ev("m_scores_ready"), 1)
            for hh in range(8):
                out_h = stat[64 * (hh % 2):64 * (hh % 2) + 64, hh // 2, :]
                for c in range(NT):
                    pe.matmul(out_h[:, c * P:(c + 1) * P], m_xt[:, c, hh * HD:(hh + 1) * HD], m_seg[:, hh, c * P:(c + 1) * P],
                              start=True, stop=c == 0, skip_group_check=True)
                mm = pe.matmul(out_h[:, P:T], m_h[:, hh * HD:(hh + 1) * HD], m_cd[:, hh, :], start=False, stop=True,
                               skip_group_check=True)
            mm.then_inc(ev("m_y_ready"), 1)
            linear(h, 2)
            pe.wait_ge(ev("m_ym_ready"), 1)
            sums(sq, 2, 2)
            linear(h, 2)

            sums(sq, 4, 1)
            linear(h, 1)
            sums(sq, 4, 1)
            linear(h, 2)
            pe.wait_ge(ev("g_k_ready"), 1)
            for c in range(NT):
                turned(mixbank(c), [gq[:, 4 + j, c * P:(c + 1) * P] for j in range(4)], ev("g_kt_turned"))
            for c in range(NT):
                pe.wait_ge(ev("g_kt_copied"), c + 1)
                turned(mixbank(c), [gq[:, 8 + j, c * P:(c + 1) * P] for j in range(4)], ev("g_vt_turned"))
            spread(stat, lambda i, c: beta[:, c, i:i + 1], K["ident"]).then_inc(ev("g_beta_ready"), 1)
            pe.wait_ge(ev("ya_done"), 1)
            branch_panels(0, 0, 1)
            pe.wait_ge(ev("g_vt_copied"), 2)
            spread(mixp, lambda i, c: adt[:, c, 8 + i:9 + i], K["upto64"]).then_inc(ev("g_rows_ready"), 1)
            pe.wait_ge(ev("g_kb_ready"), 1)
            for i in range(4):
                for c in range(NT):
                    mm = pe.matmul(stat[:, i, c * P:(c + 1) * P], gq[:, 4 + i, c * P:(c + 1) * P], g_kb[:, i, c * P:(c + 1) * P],
                                   start=True, stop=True, skip_group_check=True)
            mm.then_inc(ev("g_kk_ready"), 1)
            branch_panels(0, 1, 2)
            pe.wait_ge(ev("g_rows_read"), 1)
            pe.wait_ge(ev("g_er_ready"), 1)
            for i in range(4):
                for c in range(NT):
                    mm = pe.matmul(mixp[:, i, c * P:(c + 1) * P], gq[:, 4 + i, c * P:(c + 1) * P], gq[:, i, c * P:(c + 1) * P],
                                   start=True, stop=True, skip_group_check=True)
            mm.then_inc(ev("g_kq_ready"), 1)
            pe.wait_ge(ev("g_mt_ready"), 1)
            for i in range(4):
                for c in range(NT):
                    mm = pe.transpose(stat[:, i, c * P:(c + 1) * P], g_mt[:, i, c * P:(c + 1) * P], K["ident"])
            mm.then_inc(ev("g_m_ready"), 1)
            branch_panels(0, 2, 4)
            pe.wait_ge(ev("g_at_ready"), 1)
            blocks = [(i, slice(c * P, (c + 1) * P)) for i in range(4) for c in range(NT)]
            for n in range(1, 6):
                pe.wait_ge(ev("g_d_ready"), n)
                for i, s in blocks:
                    mm = pe.matmul(mixp[:, i, s], g_ml[:, i, s], g_d[:, i, s], start=True, stop=True, skip_group_check=True)
                mm.then_inc(ev("g_w_ready"), 1)
                pe.wait_ge(ev("g_w_copied"), n)
                for i, s in blocks:
                    mm = pe.matmul(stat[:, i, s], g_w[:, i, s], g_dt[:, i, s], start=True, stop=True, skip_group_check=True)
                mm.then_inc(ev("g_ddt_ready"), 1)
                if n < 5:
                    for i, s in blocks:
                        mm = pe.matmul(mixp[:, i, s], g_dt[:, i, s], g_w[:, i, s], start=True, stop=True, skip_group_check=True)
                    mm.then_inc(ev("g_dd_ready"), 1)
                branch_panels(0, 3 + n, 4 + n)
            pe.wait_ge(ev("g_dt_final"), 1)
            for i, s in blocks:
                c = s.start // P
                mm = pe.matmul(stat[:, i, s], g_dt[:, i, s], g_vt[:, 2 * c + i // 2, (i % 2) * P:(i % 2 + 1) * P],
                               start=True, stop=True, skip_group_check=True)
            mm.then_inc(ev("g_u_ready"), 1)
            for i, s in blocks:
                c = s.start // P
                mm = pe.matmul(mixp[:, i, s], g_r2[:, 2 * c + i // 2, (i % 2) * P:(i % 2 + 1) * P], g_dt[:, i, s],
                               start=True, stop=True, skip_group_check=True)
            mm.then_inc(ev("g_wt_ready"), 1)
            branch_panels(0, 9, 10)
            pe.wait_ge(ev("g_wt_copied"), 1)
            pe.wait_ge(ev("g_u_copied"), 1)
            for ch in range(4):
                c, o = ch // 2, 64 * (ch % 2)
                s = slice(ch * 64, ch * 64 + 64)
                if ch:
                    pe.wait_ge(ev("g_s_ready"), ch)
                    for i in range(4):
                        mm = pe.matmul(mixbank(0)[o:o + 64, i * P:(i + 1) * P], g_w[:, i, s], g_s[:, i, :],
                                       start=True, stop=True, skip_group_check=True)
                    mm.then_inc(ev("g_ws_ready"), 1)
                pe.wait_ge(ev("g_vn_ready"), ch + 1)
                if ch < 3:
                    for i in range(4):
                        mm = pe.matmul(mixbank(1)[:, i * P:(i + 1) * P], g_kt[o:o + 64, 2 * c + i // 2, (i % 2) * P:(i % 2 + 1) * P],
                                       g_ml[o:o + 64, i, c * P:(c + 1) * P], start=True, stop=True, skip_group_check=True)
                    mm.then_inc(ev("g_ds_ready"), 1)
                for i in range(4):
                    mm = pe.matmul(stat[:, i, s], g_ml[o:o + 64, i, c * P:(c + 1) * P], g_at[o:o + 64, i, s],
                                   start=True, stop=ch == 0, skip_group_check=True)
                    if ch:
                        mm = pe.matmul(stat[:, i, s], g_s[:, i, :], g_qd[:, i, s],
                                       start=False, stop=True, skip_group_check=True)
                mm.then_inc(ev("g_o_ready"), 1)
            branch_panels(0, 10, 11)
            pe.wait_ge(ev("g_o_read"), 1)
            sums(sq, 4, 1)
            branch_panels(0, 11, 12)

            sums(sq, 4, 1)
            pe.wait_ge(ev("yc_done"), 1)
            branch_panels(2, 0, 2)
            sums(sq, 4, 1)
            for c in range(NT):
                turned(mixbank(c), [sq_kv[:, 8 + j, c * P:(c + 1) * P] for j in range(4)], ev("b_vt_turned"))
            branch_panels(2, 2, 3)
            pe.wait_ge(ev("b_qk_ready"), 1)
            pe.wait_ge(ev("b_vt_copied"), 2)

            def bbank(i):
                return mixbank(i) if i < 2 else statbank(i)


            for i in range(4):
                pe.matmul(bbank(i)[:, 0:T], sq_kv[:, 4 + i, 0:P], sq_kv[:, i, :], start=True, stop=True, skip_group_check=True)
                mm = pe.matmul(bbank(i)[:, T:3 * P], sq_kv[:, 4 + i, P:T], sq_kv[:, i, P:T], start=True, stop=True,
                               skip_group_check=True)
            mm.then_inc(ev("b_z_ready"), 1)
            branch_panels(2, 3, 6)
            pe.wait_ge(ev("b_nk_ready"), 1)
            for i in range(4):
                pe.matmul(bbank(i)[:, 0:T], K["after"], b_nk[:, i, 0:T], start=True, stop=False, skip_group_check=True)
                pe.matmul(bbank(i)[:, P:T], K["ones"], b_nk[:, i, T:3 * P], start=False, stop=True, skip_group_check=True)
                mm = pe.matmul(bbank(i)[:, T:3 * P], K["after"], b_nk[:, i, T:3 * P], start=False, stop=True,
                               skip_group_check=True)
            mm.then_inc(ev("b_after_ready"), 1)
            branch_panels(2, 6, 8)
            pe.wait_ge(ev("b_att_ready"), 1)
            for i in range(4):
                o = stat[:, i, :]
                v = [b_vt[:, c, i * P:(i + 1) * P] for c in range(NT)]
                pe.matmul(o[:, 0:P], v[0], b_l[:, i, 0:P], start=True, stop=True, skip_group_check=True)
                pe.matmul(o[:, P:T], v[0], b_l[:, i, P:T], start=True, stop=False, skip_group_check=True)
                mm = pe.matmul(o[:, P:T], v[1], b_l[:, i, T:3 * P], start=False, stop=True, skip_group_check=True)
            mm.then_inc(ev("b_o_ready"), 1)
            branch_panels(2, 8, 12)
            pe.wait_ge(ev("yb2_done"), 1)
            branch_panels(1, 0, 12)
            panels.settled()
            project(merged)
            for c in range(NT):
                for i in range(KD):
                    if c == 0:
                        pe.wait_ge(h_ready, seen(h_ready))
                    mm = pe.matmul(mixbank(0)[:, c * 36:(c + 1) * 36], h[:, i, c * P:(c + 1) * P], wsmall[:, i, 16:52],
                                   start=i == 0, stop=i == KD - 1, skip_group_check=True)
            mm.then_inc(ev("logits_ready"), 1)
            panels.settled()
            pe.wait_ge(M["dT"], 1)
            for g in range(4):
                pe.matmul(lin[g][:, :], e_dT[:, 0:P], cst[:, 0:512], start=True, stop=False, skip_group_check=True)
                if g:
                    pe.wait_ge(ev("ht_copied"), g)
                turned(mixbank(1), [h[:, (g % 2) * 4 + j, (g // 2) * P:(g // 2 + 1) * P] for j in range(4)], ev("ht_turned"))
            pe.wait_ge(ev("assigned"), 1)
            pe.matmul(mixbank(0)[:, 0:E], K["before"], assign[:, 0, :], start=True, stop=True, skip_group_check=True)
            pe.matmul(mixbank(0)[:, E:2 * E], K["before"], assign[:, 1, :], start=True, stop=False, skip_group_check=True)
            pe.matmul(mixbank(0)[:, E:2 * E], K["ones"], assign[:, 0, :], start=False, stop=True, skip_group_check=True)
            pe.matmul(mixbank(0)[:, 2 * E:3 * E], K["ones"], assign[:, 0, :], start=True, stop=False, skip_group_check=True)
            pe.matmul(mixbank(0)[:, 2 * E:3 * E], K["ones"], assign[:, 1, :], start=False, stop=True, skip_group_check=True)\
                .then_inc(ev("ranks_ready"), 1)
            pe.wait_ge(ev("ht_copied"), 4)

            def moe_gather(s):
                for c in range(NT):
                    for half in range(2):
                        mm = pe.matmul(statbank(0)[64 * half:64 * half + 64, :], e_sel[:, s, c, :],
                                       h_tm[:, c, half * 512:(half + 1) * 512], start=c == 0, stop=c == 1, skip_group_check=True)
                mm.then_inc(M["A"], 1)

            def moe_turn():
                for j in range(4):
                    mm = pe.transpose(statbank(1)[:, j * P:(j + 1) * P], e_hg[:, j * P:(j + 1) * P], K["ident"])
                mm.then_inc(M["B"], 1)

            def moe_combine():
                for j in range(4):
                    for half in range(2):
                        m = half * 4 + j
                        mm = pe.matmul(lin[m // 2][:, (m % 2) * T:(m % 2 + 1) * T], e_yb[64 * half:64 * half + 64, j * P:(j + 1) * P],
                                       e_dT[64 * half:64 * half + 64, T:2 * T], start=False, stop=False, skip_group_check=True)
                return mm

            pe.wait_ge(M["sel"], 1)
            moe_gather(0)
            pe.wait_ge(M["hg"], 1)
            moe_turn()
            pe.wait_ge(M["sel"], 2)
            moe_gather(1)

            def moe_step(it, s):
                pe.wait_ge(M[f"gu_loaded{s}"], it * 32 + 32)
                pe.wait_ge(M["hgT"], it * 2 + (s + 1))
                pe.wait_ge(M["hid"], it * 2 + (s + 1))
                for k in range(KD):
                    lhs = e_hgT[:, k % 4, k // 4, :]
                    for half in range(2):
                        o = mixbank(0)[64 * half:64 * half + 64, :]
                        pe.matmul(o[:, 0:T], lhs, e_wg[:, s, k, half * T:(half + 1) * T], start=k == 0, stop=k == KD - 1,
                                  skip_group_check=True)
                    for half in range(2):
                        o = mixbank(0)[64 * half:64 * half + 64, :]
                        mm = pe.matmul(o[:, T:2 * T], lhs, e_wu[:, s, k, half * T:(half + 1) * T], start=False,
                                       stop=k == KD - 1, skip_group_check=True)
                mm.then_inc(M["C"], 1)
                pe.wait_ge(M["yb"], it * 2 + (s + 1))
                pe.wait_ge(M["dT"], it * 2 + (s + 1))
                moe_combine().then_inc(M["F"], 1)
                pe.wait_ge(M["hg"], it * 2 + (s + 2))
                moe_turn()
                pe.wait_ge(M["hid"], it * 2 + (s + 2))
                pe.wait_ge(M["selw"], it * 2 + (s + 1))
                for j in range(2):
                    pe.transpose(mixbank(1)[:, j * P:(j + 1) * P], e_hid[:, j * P:(j + 1) * P], K["ident"])
                for c in range(NT):
                    mm = pe.transpose(mixbank(1)[:, T + c * P:T + (c + 1) * P], e_selw[:, s, c, :], K["ident"])
                mm.then_inc(M["D"], 1)
                pe.wait_ge(M["sel"], it * 2 + (s + 3))
                moe_gather(s)
                pe.wait_ge(M[f"d_loaded{s}"], it * 16 + 16)
                pe.wait_ge(M["dT"], it * 2 + (s + 2))
                pe.wait_ge(M["hgT"], it * 2 + (s + 2))
                for k in range(4):
                    for half in range(2):
                        mm = pe.matmul(statbank(1)[64 * half:64 * half + 64, :], e_hidT[:, k % 2, k // 2, :],
                                       e_wd[:, s, k, half * 512:(half + 1) * 512], start=k == 0, stop=k == 3, skip_group_check=True)
                mm.then_inc(M["E"], 1)

            def moe_last(e):
                pe.wait_ge(M["yb"], e + 2)
                pe.wait_ge(M["dT"], e + 2)
                moe_combine().then_inc(M["y"], 1)

            with pe.Fori(0, E // 2) as it:
                moe_step(it, 0)
                moe_step(it, 1)
            pe.wait_ge(M["flag"], 1)
            more = pe.value_load(flag_i[0:1, 0:1], min_val=0, max_val=1)
            with pe.If(more == 1):
                with pe.Fori(E // 2, NE // 2) as it:
                    moe_step(it, 0)
                    moe_step(it, 1)
                moe_last(NE - 1)
            with pe.Else():
                moe_last(E - 1)

        @block.scalar
        def _(act):
            seen = Seen()
            panels = Panels(act)

            def norm(src, tiles, groups=1, width=D):
                act.activation(sq[:, 0:tiles, :], src, ACT.Square).then_inc(sq_ready, 1)
                norm_rest(groups, width)

            next_split = [OUT0]

            def split_hi(upto):
                for n in range(next_split[0], upto):
                    next_split[0] = n + 1
                    if is_split(n):
                        act.wait_ge(panel_loaded[n % RING], 16 * (n // RING + 1))
                        act.wait_ge(panel_done, n - RING + 1)
                        act.activation(w_hi[:, n % RING, :], ring[:, n % RING, :], ACT.Copy).then_inc(w_hi_ready, 1)

            def split_hi_loop(n, it):
                act.wait_ge(panel_loaded[n % RING], it * 16 + 16 * (n // RING + 1))
                act.wait_ge(panel_done, it * RING + (n - RING + 1))
                act.activation(w_hi[:, n % RING, :], ring[:, n % RING, :], ACT.Copy).then_inc(w_hi_ready, 1)

            def stream_norm(first=False, down=False):
                for m in range(0, KD, 2 if down else 1):
                    if down:
                        act.wait_ge(bank_free[m // 2], panels.free[m // 2] + 1)
                    elif not first:
                        panels.taken(m)
                    n = 2 if down else 1
                    act.activation(sq[:, m:m + n, :], x[:, m:m + n, :], ACT.Square).then_inc(sq_ready, 1)
                    if not (first or down):
                        split_hi(min(panels.n + m + 5, panels.n + KD + 2))
                if down:
                    panels.advance_down()
                elif not first:
                    panels.advance(KD)
                norm_rest(1, D)
                if not first:
                    split_hi(panels.n + 4)

            def norm_rest(groups, width):
                act.wait_ge(sums_ready, seen(sums_ready))
                act.activation(rs[:, 0:groups, :], stat[:, 0:groups, :], ACT.Ln, bias=K["eps"], scale=1.0 / width)\
                    .then_inc(ln_done, 1)
                act.wait_ge(ln_done, seen(ln_done))
                act.activation(rs[:, 0:groups, :], rs[:, 0:groups, :], ACT.Exp, scale=-0.5).then_inc(rs_ready, 1)

            def take(dst, func=ACT.Copy, **kw):
                b = panels.done()
                act.activation(dst, lin[b][:, 0:T], func, **kw).then_inc(bank_free[b], 1)
                panels.advance(1)
                if panels.n > OUT0:
                    split_hi(panels.n + RING)

            def tap0(dst, b, w, bias):
                act.activation(dst, lin[b][:, 0:T], ACT.Identity, bias=bias, scale=w).then_inc(tap0_done, 1)

            def ffn(l):
                w2 = cols["ffn_cw"][0] + (l * 3 + 2) * 2 * KF
                cb = cols["ffn_cb"][0] + l * 2 * KF
                act.activation(sgf[:, 0, 0:1], K["one"], ACT.Silu)
                with act.Fori(0, KF // 2) as it:
                    for j in range(4):
                        if j % 2 == 0:
                            act.wait_ge(act_tile, it * 2 + (1 + l * KF + j // 2))
                        b = panels.done(j, it)
                        tile = j // 2 + KF * (j % 2)
                        tap0(ub[:, j, :], b, colp[:, ds(it * 2 + (w2 + tile), 1)], colp[:, ds(it * 2 + (cb + tile), 1)])
                        if j % 2 == 1:
                            panels.taken(j - 1, it)
                            act.activation(sgf[:, j // 2, :], ub[:, j - 1, :], ACT.Silu).then_inc(silu_done, 1)
                        split_hi_loop(panels.n + j + RING, it)
                panels.advance(2 * KF)
                for n in range(4, 6):
                    split_hi_loop(panels.n + n, 0)
                with act.Fori(0, 4) as it:
                    for j in range(4):
                        split_hi_loop(panels.n + 6 + j, it)
                next_split[0] = panels.n + KF
                split_hi(min(panels.n + KF + 2, BLOCK2))

            act.wait_ge(consts_loaded, 48)
            stream_norm(first=True)
            act.activation(c_act[:, :], col("c", 0, KD), ACT.Silu).then_inc(silu_done, 1)
            for j in range(4):
                take(sg0[:, j, :], ACT.Sigmoid, bias=col("b_in", 12 + j))
                panels.advance(1)
            for j in range(4):
                take(v0[:, j, :], ACT.Gelu_apprx_tanh, bias=col("b_in", 4 + j))
            for j in range(4):
                take(u0[:, j, :], ACT.Gelu_apprx_tanh, bias=col("b_in", j))
            with act.Fori(0, ADA0 // 4) as it:
                for j in range(4):
                    b = panels.done(j, it)
                    act.activation(modraw[:, ds(it * 4 + j, 1), :].rearrange("p n c -> p (n c)"), lin[b][:, 0:32], ACT.Copy)\
                        .then_inc(bank_free[b], 1)
            panels.advance(ADA0)
            act.wait_ge(centred, 1)
            norm(xc0, KH, width=HALF)
            split_hi(OUT0 + 4)
            act.wait_ge(centred, 2)
            norm(xc0, KH, width=HALF)
            act.wait_ge(yb_normed, 1)
            for j in range(KH):
                act.activation(cat[:, KH + j, :], cv0[:, j, :], ACT.Silu, bias=col("cln_b", j)).then_inc(yb_ready, 1)
            stream_norm()
            ffn(0)
            stream_norm(down=True)
            for n in range(16):
                if n >= 2:
                    act.wait_ge(qk_ready, n - 1)
                take(qs1[:, n % 2, :])
            for n in range(8):
                take(v1[:, n, :])
            for i in range(HEADS + 2):
                if i < HEADS:
                    act.wait_ge(max_ready, i + 1)
                    if i >= 4:
                        act.wait_ge(pt_ready, i - 3)
                    for c, (a0, a1) in enumerate(((0, P), (P, 3 * P))):
                        ins = act.activation(p1[:, i % 4, a0:a1], s1[:, i % 4, a0:a1], ACT.Exp,
                                             bias=mx1[:, 2 * i + c:2 * i + c + 1], accum_out=l1[:, 2 * i + c:2 * i + c + 1])
                    ins.then_inc(exp_ready, 1)
                if i < HEADS and i % 2 == 1:
                    g = i // 2
                    act.wait_ge(panel_done, panels.n + 3)
                    act.activation(modraw[:, 3 * g:3 * g + 3, :], lin[2 + g % 2][:, 0:96], ACT.Copy)\
                        .then_inc(mod_copied, 1)
                    panels.n += 3
                if i >= 2:
                    g = i - 2
                    act.wait_ge(pt_ready, g + 1)
                    if g >= 4:
                        act.wait_ge(o_ready, g - 3)
                    act.activation(pt1[:, g % 4, :], statbank(g)[:, 0:SC], ACT.Copy).then_inc(pt_copied, 1)
                    if i == HEADS:
                        split_hi(OUT1 + 1)
            split_hi(OUT1 + 4)
            stream_norm()
            ffn(1)
            def step(ins):
                ins.then_inc(act_step, 1)
                act.wait_ge(act_step, seen(act_step))

            def conv_tiles(dst, count, w, bias, done):
                for n in range(count + 1):
                    if n < count:
                        tap0(dst[:, n, :], panels.done(n), w(n), bias(n))
                    if n:
                        panels.taken(n - 1)
                        ins = act.activation(dst[:, n - 1, :], dst[:, n - 1, :], ACT.Silu)
                ins.then_inc(done, 1)
                panels.advance(count)

            stream_norm(down=True)
            for m in range(KD):
                act.wait_ge(ev("x_final"), m + 1)
                act.activation(sq[:, m, :], x[:, m, :], ACT.Square).then_inc(sq_ready, 1)
            norm_rest(1, D)

            def shifted(half):
                for k in range(KD):
                    act.wait_ge(ev("h_scaled"), half * KD + k + 1)
                    act.activation(h[:, k, :], h[:, k, :], ACT.Identity, bias=mod[:, 3 * half * KD + k:3 * half * KD + k + 1])\
                        .then_inc(h_ready, 1)

            shifted(0)
            act.wait_ge(ev("small_in"), 1)
            act.wait_ge(extra_loaded, 64)
            act.activation(ea, rows[:, ROWS["a_log"][0]:ROWS["a_log"][0] + 12], ACT.Exp)
            act.activation(beta_in, beta_in, ACT.Exp, scale=-1.0)
            step(act.activation(spe, spin, ACT.Abs))
            step(act.activation(spe, spe, ACT.Exp, scale=-1.0))
            act.activation(spl, spe, ACT.Ln, bias=K["one"]).then_inc(ev("small_act"), 1)
            conv_tiles(xb, 8, lambda n: col("ssm_cw", 24 + n), lambda n: col("ssm_cb", n), ev("xb_ready"))
            act.wait_ge(ev("cums_copied"), 1)
            act.activation(mdec, mdif, ACT.Exp)
            act.activation(kdec, gdif, ACT.Exp)
            act.activation(eg, cums[:, :, 8:12], ACT.Exp).then_inc(ev("decays_ready"), 1)
            for j in range(4):
                take(zs[:, j, :], ACT.Silu)
            conv_tiles(gq, 12, lambda n: col("gdn_cw", 36 + n), lambda n: 0.0, ev("gq_ready"))
            def gates(i, first, last):
                if i != BRANCHES[0] and first == 0:
                    act.wait_ge(gated, 8 * BRANCHES.index(i))
                for j in range(first, last):
                    if j % 3:
                        b = panels.done()
                        act.activation(gates8[:, 2 * (j // 3) + j % 3 - 1, :], lin[b][:, 0:T], ACT.Tanh, scale=0.5)\
                            .then_inc(bank_free[b], 1)
                    panels.advance(1)

            take(sq_kv[:, 0, :])
            for k, ps in ((0, mixp), (1, stat)):
                act.wait_ge(ev("m_rows_ready"), k + 1)
                act.activation(m_er[:, 4 * k:4 * k + 4, :], ps[:, :, P:T], ACT.Exp).then_inc(ev("m_rows_exp"), 1)
                act.wait_ge(ev("m_rows_read"), k + 1)
                seg = m_seg[:, 4 * k:4 * k + 4, :]
                act.activation(seg, seg, ACT.Exp).then_inc(ev("m_seg_exp"), 1)
            for j in range(1, 11):
                take(sq_kv[:, j, :])
            act.wait_ge(ev("m_ym_ready"), 1)
            norm(ybr[:, 0:4, :], 4, 2, T)
            take(sq_kv[:, 11, :])
            take(gg[:, 0, :])
            act.wait_ge(ev("gq_ready"), 1)
            act.wait_ge(ev("ya_done"), 1)
            norm(gq[:, 0:4, :], 4, 4, 1)
            take(gg[:, 1, :])
            act.wait_ge(ev("g_q_ready"), 1)
            norm(gq[:, 4:8, :], 4, 4, 1)
            take(gg[:, 2, :])
            take(gg[:, 3, :])
            act.wait_ge(ev("g_rows_ready"), 1)
            act.activation(g_er, mixp[:, :, :], ACT.Exp).then_inc(ev("g_er_ready"), 1)
            gates(0, 0, 2)
            act.wait_ge(ev("g_rows_read"), 1)
            act.activation(g_dec, g_dec, ACT.Exp).then_inc(ev("g_dec_ready"), 1)
            gates(0, 2, 4)
            for n in range(1, 6):
                act.wait_ge(ev("g_w_ready"), n)
                act.activation(g_w, mixp[:, :, :], ACT.Copy).then_inc(ev("g_w_copied"), 1)
                gates(0, 3 + n, 4 + n)
            act.wait_ge(ev("g_wt_ready"), 1)
            act.activation(g_w, mixp[:, :, :], ACT.Copy).then_inc(ev("g_wt_copied"), 1)
            gates(0, 9, 11)
            act.wait_ge(ev("g_o_read"), 1)
            norm(ybr[:, 8:12, :], 4, 4, P)
            gates(0, 11, 12)
            for j in range(4):
                ins = act.activation(gg[:, j, :], gg[:, j, :], ACT.Silu)
            ins.then_inc(ev("gg_ready"), 1)
            act.wait_ge(ev("yc_done"), 1)
            norm(sq_kv[:, 0:4, :], 4, 4, P)
            gates(2, 0, 2)
            act.wait_ge(ev("b_q_ready"), 1)
            norm(sq_kv[:, 4:8, :], 4, 4, P)
            gates(2, 2, 3)
            act.wait_ge(ev("b_z_ready"), 1)
            for k in range(2):
                step(act.activation(b_l[:, 2 * k:2 * k + 2, :], zbanks(k), ACT.Abs))
            step(act.activation(b_l, b_l, ACT.Exp, scale=-1.0))
            act.activation(b_l, b_l, ACT.Ln, bias=K["one"]).then_inc(ev("b_l_ready"), 1)
            gates(2, 3, 6)
            act.wait_ge(ev("b_lb_ready"), 1)
            act.activation(b_l, b_lb, ACT.Exp).then_inc(ev("b_exp_ready"), 1)
            gates(2, 6, 12)
            gates(1, 0, 12)
            stream_norm()
            shifted(1)
            for g in range(4):
                act.wait_ge(ev("ht_turned"), g + 1)
                act.activation(h_tm[:, g // 2, (g % 2) * 512:(g % 2 + 1) * 512], mixbank(1), ACT.Copy).then_inc(ev("ht_copied"), 1)
            act.wait_ge(ev("route_in"), 1)
            act.activation(r_ge, r_ge, ACT.Exp).then_inc(ev("group_exp"), 1)
            act.wait_ge(ev("top_in"), 1)
            act.activation(r_e2, r_e2, ACT.Exp).then_inc(ev("top_exp"), 1)
            act.wait_ge(M["B"], 1)
            act.activation(e_hgT_flat, statbank(1), ACT.Copy).then_inc(M["hgT"], 1)

            def moe_step(it, s):
                act.wait_ge(M["C"], it * 2 + (s + 1))
                act.wait_ge(M["hid"], it * 2 + (s + 1))
                act.activation(e_sg, mixbank(0)[:, 0:T], ACT.Silu).then_inc(M["silu"], 1)
                act.wait_ge(M["B"], it * 2 + (s + 2))
                act.activation(e_hgT_flat, statbank(1), ACT.Copy).then_inc(M["hgT"], 1)
                act.wait_ge(M["E"], it * 2 + (s + 1))
                act.activation(e_yb, statbank(1), ACT.Copy).then_inc(M["yb"], 1)

            with act.Fori(0, E // 2) as it:
                moe_step(it, 0)
                moe_step(it, 1)
            act.wait_ge(M["flag"], 1)
            more = act.value_load(flag_i[0:1, 0:1], min_val=0, max_val=1)
            with act.If(more == 1):
                with act.Fori(E // 2, NE // 2) as it:
                    moe_step(it, 0)
                    moe_step(it, 1)

        @block.gpsimd
        def _(pool):
            for first, end in ((OUT0, ADA1), (OUT1, BLOCK2)):
                first += (POOL_SLOT - first) % RING
                with pool.Fori(0, (end - first + RING - 1) // RING) as it:
                    pool.wait_ge(w_hi_ready, it * RING + (splits_before(first) + 1))
                    pool.tensor_tensor(w_lo[:, POOL_SLOT, :], ring[:, POOL_SLOT, :], w_hi[:, POOL_SLOT, :].bitcast(F32),
                                       ALU.subtract).then_inc(w_split_pool, 1)

        @block.vector
        def _(dve):
            seen = Seen()
            panels = Panels(dve)

            def link(ins):
                ins.then_inc(dve_step, 1)
                dve.wait_ge(dve_step, seen(dve_step))

            next_split = [OUT0]

            def split_lo(upto):
                for n in range(next_split[0], upto):
                    next_split[0] = n + 1
                    if is_split(n):
                        split_lo_loop(n)

            def split_lo_loop(n, it=None):
                if n % RING == POOL_SLOT:
                    return
                v = splits_before(n) + 1
                dve.wait_ge(w_hi_ready, v if it is None else it * RING + v)
                dve.tensor_tensor(w_lo[:, n % RING, :], ring[:, n % RING, :], w_hi[:, n % RING, :].bitcast(F32), ALU.subtract)\
                    .then_inc(w_split, 1)

            def split_stream(gain):
                dve.wait_ge(rs_ready, seen(rs_ready))
                at = {}
                for k in range(KD + 2):
                    if k < KD:
                        dve.scalar_tensor_tensor(h[:, k, :], x[:, k, :], gain(k), rs[:, 0, :], ALU.mult, ALU.mult)\
                            .then_inc(dve_step, 1)
                        at["whole", k] = seen(dve_step)
                    if 1 <= k <= KD:
                        dve.wait_ge(dve_step, at["whole", k - 1])
                        dve.tensor_copy(r_hi[:, k - 1, :], h[:, k - 1, :]).then_inc(dve_step, 1)
                        at["hi", k - 1] = seen(dve_step)
                    if k >= 2:
                        dve.wait_ge(dve_step, at["hi", k - 2])
                        dve.tensor_tensor(r_lo[:, k - 2, :], h[:, k - 2, :], r_hi[:, k - 2, :].bitcast(F32), ALU.subtract)\
                            .then_inc(h_ready, 1)

            def split_rows(tiles, src):
                link(dve.tensor_copy(r_hi[:, tiles, :], src))
                return dve.tensor_tensor(r_lo[:, tiles, :], src, r_hi[:, tiles, :].bitcast(F32), ALU.subtract)

            def scale_stream(gain, event):
                dve.wait_ge(rs_ready, seen(rs_ready))
                for k in range(KD):
                    dve.scalar_tensor_tensor(h[:, k, :], x[:, k, :], gain(k), rs[:, 0, :], ALU.mult, ALU.mult).then_inc(event, 1)

            def residual(count, gate=None):
                for m in range(count):
                    b = panels.done()
                    if gate is None:
                        ins = dve.tensor_tensor(x[:, m, :], x[:, m, :], lin[b][:, 0:T], ALU.add)
                    else:
                        ins = dve.scalar_tensor_tensor(x[:, m, :], lin[b][:, 0:T], gate(m), x[:, m, :], ALU.mult, ALU.add)
                    ins.then_inc(bank_free[b], 1)
                    panels.advance(1)
                    if panels.n <= BLOCK2:
                        split_lo(min(panels.n + 4, panels.n - m + KD + 1))

            def ffn(l):
                panels.settled()
                split_stream(lambda k: col("ffn_norm", l * KD + k))
                split_lo(panels.n + 4)
                first = cols["ffn_cw"][0] + l * 3 * 2 * KF
                base = seen.now(dve_step)
                taps = l * 2 * KF

                def hidden(t, it, i):
                    return t[:, ds(it * 2 + i, 1), :].rearrange("p k t -> p (k t)")

                def hidden_hi(it, i, step):
                    dve.wait_ge(dve_step, it * 8 + step)
                    dve.tensor_copy(hidden(hid_hi, it, i), sgf[:, i, :]).then_inc(dve_step, 1)

                def hidden_lo(it, i, step):
                    dve.wait_ge(dve_step, it * 8 + step)
                    dve.tensor_tensor(hidden(hid_lo, it, i), sgf[:, i, :], hidden(hid_hi, it, i).bitcast(F32), ALU.subtract)\
                        .then_inc(act_tile, 1)

                with dve.Fori(0, KF // 2) as it:
                    step = base
                    for j in range(4):
                        b = (panels.n + j) % 4
                        dve.wait_ge(tap0_done, it * 4 + (taps + j + 1))
                        tile = first + j // 2 + KF * (j % 2)
                        dve.scalar_tensor_tensor(ub[:, j, 1:T], lin[b][:, 0:T - 1], colp[:, ds(it * 2 + (tile + 2 * KF), 1)],
                                                 ub[:, j, 1:T], ALU.mult, ALU.add).then_inc(dve_step, 1)
                        tap1 = step = step + 1
                        if j == 2:
                            hidden_hi(it, 0, step - 1)
                            step += 1
                        if j < 3:
                            split_lo_loop(panels.n + j + RING, it)
                        dve.wait_ge(dve_step, it * 8 + tap1)
                        dve.scalar_tensor_tensor(ub[:, j, 2:T], lin[b][:, 0:T - 2], colp[:, ds(it * 2 + tile, 1)],
                                                 ub[:, j, 2:T], ALU.mult, ALU.add).then_inc(bank_free[b], 1)
                        if j == 2:
                            hidden_lo(it, 0, step)
                        if j % 2 == 1:
                            dve.wait_ge(silu_done, it * 2 + (1 + l * KF + j // 2 + 1))
                            panels.taken(j, it)
                            dve.tensor_tensor(sgf[:, j // 2, :], sgf[:, j // 2, :], ub[:, j, :], ALU.mult).then_inc(dve_step, 1)
                            step += 1
                    split_lo_loop(panels.n + 3 + RING, it)
                    hidden_hi(it, 1, step)
                    hidden_lo(it, 1, step + 1)
                seen(dve_step, 4 * KF)
                panels.advance(2 * KF)
                for n in range(4, 6):
                    split_lo_loop(panels.n + n)
                with dve.Fori(0, 4) as it:
                    for j in range(4):
                        split_lo_loop(panels.n + 6 + j, it)
                next_split[0] = panels.n + KF
                split_lo(min(panels.n + KF + 2, BLOCK2))
                dve.wait_ge(panel_done, panels.n + KF)
                for b in range(4):
                    dve.tensor_tensor(x[:, 2 * b:2 * b + 2, :], x[:, 2 * b:2 * b + 2, :],
                                      downbank(b).rearrange("p (m t) -> p m t", m=2), ALU.add).then_inc(bank_free[b], 1)
                panels.advance_down()

            def centre(src, n):
                dve.wait_ge(mean_ready, n + 1)
                dve.tensor_tensor(xc0, src, mixp[:, 2 * n:2 * n + 1, :].broadcast_to([P, KH, T]), ALU.subtract)\
                    .then_inc(centred, 1)
                dve.wait_ge(centred, n + 1)

            def modulations(first):
                link(dve.tensor_tensor(modraw, modraw, K["diag32"].unsqueeze(1).broadcast_to([P, 24, 32]), ALU.mult))
                link(dve.tensor_reduce(mod[:, first:first + 24], modraw, AX, ALU.add))
                link(dve.tensor_tensor(mod[:, first:first + 24], mod[:, first:first + 24], col("b_ada", first, 24), ALU.add))

            for half in range(2):
                dve.memset(hc0[:, 2 * half:2 * half + 2, 0:PADC], 0.0).then_inc(act_tile, 1)
            dve.wait_ge(act_tile, 2)
            dve.wait_ge(consts_loaded, 48)
            scale_stream(lambda k: col("even_norm", k), h_ready)
            for j in range(KH):
                panels.taken(0)
                b = panels.done(1)
                dve.scalar_tensor_tensor(hc0[:, j, PADC:], lin[b][:, 0:T], col("b_in", 8 + j), sg0[:, j, :], ALU.add, ALU.mult)\
                    .then_inc(bank_free[b], 1)
                panels.advance(2)
            panels.advance(8)
            for b in (1, 3):
                dve.wait_ge(bank_free[b], 2)
            for j in range(KH):
                dve.tensor_scalar(cv0[:, j, :], hc0[:, j, 0:T], col("conv_w", j), col("conv_b", j), ALU.mult, ALU.add)\
                    .then_inc(conv_step, 1)
            with dve.Fori(1, CONV) as tap:
                for j in range(KH):
                    dve.wait_ge(conv_step, tap * KH + (j - 3))
                    dve.scalar_tensor_tensor(cv0[:, j, :], hc0[:, j, ds(tap, T)], colp[:, ds(tap * KH + (cols["conv_w"][0] + j), 1)],
                                             cv0[:, j, :], ALU.mult, ALU.add).then_inc(conv_step, 1)
            dve.wait_ge(extra_loaded, 64)
            link(dve.tensor_tensor(wsm0, ws0, K["upto"].unsqueeze(1).broadcast_to([P, 8, P]), ALU.mult))
            panels.settled()
            centre(v0, 0)
            dve.wait_ge(rs_ready, seen(rs_ready))
            for j in range(KH):
                ins = dve.scalar_tensor_tensor(v0[:, j, :], xc0[:, j, :], col("vln_g", j), rs[:, 0, :], ALU.mult, ALU.mult)
            link(ins)
            for j in range(KH):
                ins = dve.tensor_scalar(v0[:, j, :], v0[:, j, :], col("vln_b", j), None, ALU.add)
            ins.then_inc(v_normed, 1)
            for c in range(NT):
                dve.wait_ge(vt_ready, c + 1)
                dve.tensor_copy(vt0[:, c, :], mixbank(c)).then_inc(vt_copied, 1)
            split_lo(OUT0 + 4)
            dve.wait_ge(mixed_ready, 1)
            bs = row("b_s").rearrange("p (j two t) -> p j two t", two=2, t=P)
            for half in range(2):
                for c in range(NT):
                    o = 64 * half
                    ins = dve.tensor_tensor(xc0[o:o + 64, :, c * P:(c + 1) * P], mixp[o:o + 64, :, c * P:(c + 1) * P],
                                            bs[o:o + 64, :, half, :], ALU.add)
            link(ins)
            dve.tensor_tensor(cat[:, 0:KH, :], xc0, u0, ALU.mult).then_inc(ya_ready, 1)
            dve.wait_ge(ya_ready, 1)
            split_rows(slice(0, KH), cat[:, 0:KH, :]).then_inc(r_split, 1)
            dve.wait_ge(conv_step, CONV * KH)
            centre(cv0, 1)
            dve.wait_ge(rs_ready, seen(rs_ready))
            for j in range(KH):
                ins = dve.scalar_tensor_tensor(cv0[:, j, :], xc0[:, j, :], col("cln_g", j), rs[:, 0, :], ALU.mult, ALU.mult)
            ins.then_inc(yb_normed, 1)
            for j in range(KH):
                dve.wait_ge(yb_ready, j + 1)
                split_rows(slice(KH + j, KH + j + 1), cat[:, KH + j:KH + j + 1, :]).then_inc(r_split, 1)
            panels.advance(ADA0)
            panels.settled()
            modulations(0)
            residual(8)
            ffn(0)
            panels.settled()
            split_stream(lambda k: col("odd_norm", k))
            split_lo(panels.n + 4)
            for n in range(16):
                panels.taken(0)
                panels.advance(1)
                link(dve.tensor_tensor(rc1[:, 0, :], qs1[:, n % 2, :], K["cos"], ALU.mult))
                dve.wait_ge(rot_ready, n + 1)
                link(dve.tensor_tensor(rc1[:, 1, :], stat[:, 2 * (n % 2), :], K["sin"], ALU.mult))
                dve.tensor_tensor(qk1[:, n, :], rc1[:, 0, :], rc1[:, 1, :], ALU.add).then_inc(qk_ready, 1)
                dve.wait_ge(qk_ready, n + 1)
                split_lo(panels.n + 4)
            panels.advance(8)
            split_lo(panels.n)
            for g in range(4):
                dve.wait_ge(vt1_ready, g + 1)
                dve.tensor_copy(vt1[:, g // 2, (g % 2) * 512:(g % 2 + 1) * 512], mixbank(g)).then_inc(vt1_copied, 1)
            a0 = list(K).index("bias00")
            bias_at = sum(v.shape[1] for v in list(consts.values())[:a0])
            bias = cst[:, bias_at:bias_at + SC]
            for i in range(HEADS + 3):
                if i < HEADS:
                    dve.wait_ge(scores_ready, i + 1)
                    if i >= 4:
                        dve.wait_ge(exp_ready, i - 3)
                    dve.scalar_tensor_tensor(s1[:, i % 4, :], mixbank(i)[:, 0:SC], HD ** -0.5, bias, ALU.mult, ALU.add)\
                        .then_inc(scores_read, 1)
                    dve.wait_ge(scores_read, i + 1)
                    for c, (a0, a1) in enumerate(((0, P), (P, 3 * P))):
                        ins = dve.tensor_reduce(mx1[:, 2 * i + c:2 * i + c + 1], s1[:, i % 4, a0:a1], AX, ALU.max, negate=True)
                    ins.then_inc(max_ready, 1)
                if 1 <= i <= HEADS:
                    g = i - 1
                    dve.wait_ge(exp_ready, g + 1)
                    link(dve.reciprocal(r1[:, 2 * g:2 * g + 2], l1[:, 2 * g:2 * g + 2]))
                    for c, (a0, a1) in enumerate(((0, P), (P, 3 * P))):
                        ins = dve.tensor_scalar(p1[:, g % 4, a0:a1], p1[:, g % 4, a0:a1], r1[:, 2 * g + c:2 * g + c + 1],
                                                None, ALU.mult)
                    ins.then_inc(probs_ready, 1)
                if i >= 4 and i % 2 == 0:
                    j = (i - 4) // 2
                    dve.wait_ge(o_ready, 2 * j + 2)
                    split_rows(j, lin[j % 2][:, 0:T]).then_inc(o_copied, 1)
                if i == HEADS + 1:
                    split_lo(OUT1 + 1)
            split_lo(OUT1 + 4)
            dve.wait_ge(mod_copied, 8)
            modulations(ADA0)
            for half, name in ((0, "norm_mix"), (1, "norm_ffn")):
                link(dve.scalar_tensor_tensor(gains[:, half * KD:(half + 1) * KD], mod[:, (3 * half + 1) * KD:(3 * half + 2) * KD],
                                              1.0, col(name, 0, KD), ALU.add, ALU.mult))
            panels.n += 48 - ADA0
            residual(8)
            ffn(1)
            panels.settled()
            dve.wait_ge(rs_ready, seen(rs_ready))
            for k in range(KD):
                dve.scalar_tensor_tensor(x[:, k, :], x[:, k, :], col("final_norm", k), rs[:, 0, :], ALU.mult, ALU.mult)\
                    .then_inc(ev("x_final"), 1)
            dve.wait_ge(ev("x_final"), KD)

            def modulated(half):
                scale_stream(lambda k: gains[:, half * KD + k:half * KD + k + 1], ev("h_scaled"))

            def conv_tiles(dst, count, tap_w, taps):
                for n in range(count):
                    b = (panels.n + n) % 4
                    dve.wait_ge(tap0_done, convs[0] + n + 1)
                    for s in range(1, taps):
                        ins = dve.scalar_tensor_tensor(dst[:, n, s:T], lin[b][:, 0:T - s], tap_w(taps - 1 - s, n),
                                                       dst[:, n, s:T], ALU.mult, ALU.add)
                        if s < taps - 1:
                            link(ins)
                        else:
                            ins.then_inc(bank_free[b], 1)
                convs[0] += count
                panels.advance(count)

            modulated(0)
            dve.wait_ge(ev("small_ready"), 1)
            sm = mixbank(0)[:, 0:32].rearrange("p (c n) -> p c n", c=NT)
            a0 = ROWS["dt_bias"][0]
            link(dve.tensor_tensor(spin, sm[:, :, 0:12], rows[:, a0:a0 + 12].unsqueeze(1).broadcast_to([P, NT, 12]), ALU.add))
            dve.tensor_copy(beta_in, sm[:, :, 12:16]).then_inc(ev("small_in"), 1)
            dve.wait_ge(ev("small_act"), 1)
            link(dve.scalar_tensor_tensor(spl, spin, 0.0, spl, ALU.max, ALU.add))
            link(dve.tensor_scalar(beta_in, beta_in, 1.0, None, ALU.add))
            link(dve.reciprocal(beta, beta_in))
            dve.scalar_tensor_tensor(adt, spl, -1.0, ea.unsqueeze(1).broadcast_to([P, NT, 12]), ALU.mult, ALU.mult)\
                .then_inc(ev("adt_ready"), 1)
            convs = [4 * KF]
            conv_tiles(xb, 8, lambda t, n: col("ssm_cw", t * 8 + n), 4)
            dve.wait_ge(ev("cums_ready"), 1)
            link(dve.tensor_copy(cums, mixbank(1)[:, 0:48].rearrange("p (c n) -> p c n", c=NT)))
            link(dve.tensor_tensor(mdif, cums[:, :, 16:24], cums[:, :, 0:8], ALU.subtract))
            dve.tensor_tensor(gdif, cums[:, :, 12:16], cums[:, :, 8:12], ALU.subtract).then_inc(ev("cums_copied"), 1)
            panels.advance(4)
            conv_tiles(gq, 12, lambda t, n: col("gdn_cw", t * 12 + n), 4)
            dve.wait_ge(ev("decays_ready"), 1)
            link(dve.tensor_tensor(beg, beta, eg, ALU.mult))

            panels.settled()
            panels.advance(16)

            def gate_branch(i, pair):
                b = panels.done(0)
                for m in range(2):
                    u = 2 * pair + m
                    panels.taken(1 + m)
                    dve.scalar_tensor_tensor(gtmp, gates8[:, u, :], 1.0, lin[b][:, m * T:(m + 1) * T], ALU.add, ALU.mult)\
                        .then_inc(gated, 1)
                    dve.wait_ge(gated, 8 * BRANCHES.index(i) + u + 1)
                    if i == BRANCHES[0]:
                        ins = dve.tensor_scalar(merged[:, u, :], gtmp, 0.5, None, ALU.mult)
                    else:
                        ins = dve.scalar_tensor_tensor(merged[:, u, :], gtmp, 0.5, merged[:, u, :], ALU.mult, ALU.add)
                    if m == 0:
                        link(ins)
                    else:
                        ins.then_inc(bank_free[b], 1)
                        panels.taken(0)
                panels.advance(3)
            dve.wait_ge(ev("xb_ready"), 1)
            for c in range(NT):
                dve.wait_ge(ev("m_xt_turned"), c + 1)
                dve.tensor_tensor(m_xt[:, c, :].rearrange("p (h d) -> p h d", d=HD), mixbank(c).rearrange("p (h d) -> p h d", d=HD),
                                  spl[:, c, 0:8].unsqueeze(2).broadcast_to([P, 8, HD]), ALU.mult).then_inc(ev("m_xt_copied"), 1)
            dve.wait_ge(ev("m_g_ready"), 1)
            link(dve.tensor_copy(m_bt, statbank(0)[:, 0:T]))
            dve.tensor_copy(m_g, statbank(1).rearrange("p (g t) -> p g t", g=2)).then_inc(ev("m_g_copied"), 1)
            dve.wait_ge(ev("m_xt_copied"), 1)
            dve.tensor_tensor(m_xdd.rearrange("p (h d) -> p h d", d=HD), m_xt[:, 0, :].rearrange("p (h d) -> p h d", d=HD),
                              mdec[:, 0, :].unsqueeze(2).broadcast_to([P, 8, HD]), ALU.mult).then_inc(ev("m_xdd_ready"), 1)

            def rows_to_decays(dst, ps, cum, mask):
                for c in range(NT):
                    s = slice(c * P, (c + 1) * P)
                    ins = dve.tensor_tensor(dst[:, :, s], ps[:, :, s], cum(c).unsqueeze(2).broadcast_to([P, 4, P]), ALU.subtract)
                link(ins)
                for c in range(NT):
                    s = slice(c * P, (c + 1) * P)
                    ins = dve.tensor_tensor(dst[:, :, s], dst[:, :, s], mask.unsqueeze(1).broadcast_to([P, 4, P]), ALU.add)
                return ins

            for k, ps in ((0, mixp), (1, stat)):
                dve.wait_ge(ev("m_rows_exp"), k + 1)
                rows_to_decays(m_seg[:, 4 * k:4 * k + 4, :], ps, lambda c: cums[:, c, 4 * k:4 * k + 4], K["neg_causal"])\
                    .then_inc(ev("m_rows_read"), 1)
            dve.wait_ge(ev("m_rows_exp"), 2)
            for k in range(2):
                ins = dve.tensor_tensor(m_cd[:, 4 * k:4 * k + 4, :], m_er[:, 4 * k:4 * k + 4, :],
                                        xb[:, 6 + k:7 + k, P:T].broadcast_to([P, 4, P]), ALU.mult)
            link(ins)
            dve.wait_ge(ev("m_h_ready"), 1)
            dve.tensor_copy(m_h, mixbank(0)).then_inc(ev("m_h_copied"), 1)
            dve.wait_ge(ev("m_seg_exp"), 2)
            dve.wait_ge(ev("m_g_copied"), 1)
            for k in range(2):
                seg = m_seg[:, 4 * k:4 * k + 4, :]
                ins = dve.tensor_tensor(seg, seg, m_g[:, k:k + 1, :].broadcast_to([P, 4, T]), ALU.mult)
            ins.then_inc(ev("m_scores_ready"), 1)
            dve.wait_ge(ev("m_y_ready"), 1)
            for j in range(4):
                ins = dve.scalar_tensor_tensor(ybr[:, j, :], xb[:, j, :], col("ssm_d", j), stat[:, j, :], ALU.mult, ALU.add)
            link(ins)
            dve.tensor_tensor(ybr[:, 0:4, :], ybr[:, 0:4, :], zs, ALU.mult).then_inc(ev("m_ym_ready"), 1)
            dve.wait_ge(ev("m_ym_ready"), 1)
            dve.wait_ge(rs_ready, seen(rs_ready))
            for j in range(4):
                ins = dve.scalar_tensor_tensor(ybr[:, j, :], ybr[:, j, :], col("ssm_norm", j), rs[:, j // 2, :], ALU.mult, ALU.mult)
            ins.then_inc(ev("ya_done"), 1)
            dve.wait_ge(ev("gq_ready"), 1)
            dve.wait_ge(rs_ready, seen(rs_ready))
            dve.scalar_tensor_tensor(gq[:, 0:4, :], gq[:, 0:4, :], P ** -0.5, rs[:, :, :], ALU.mult, ALU.mult).then_inc(ev("g_q_ready"), 1)
            dve.wait_ge(rs_ready, seen(rs_ready))
            dve.tensor_tensor(gq[:, 4:8, :], gq[:, 4:8, :], rs[:, :, :], ALU.mult).then_inc(ev("g_k_ready"), 1)

            def per_head(ap):
                return ap.unsqueeze(2).broadcast_to([P, 4, P])

            def tokens(buf, c):
                return buf[:, 2 * c:2 * c + 2, :].rearrange("p a t -> p (a t)").rearrange("p (h d) -> p h d", h=4)

            for c in range(NT):
                dve.wait_ge(ev("g_kt_turned"), c + 1)
                dve.tensor_copy(tokens(g_kt, c), mixbank(c).rearrange("p (h d) -> p h d", h=4)).then_inc(ev("g_kt_copied"), 1)
            for c in range(NT):
                dve.wait_ge(ev("g_vt_turned"), c + 1)
                dve.tensor_tensor(tokens(g_vt, c), mixbank(c).rearrange("p (h d) -> p h d", h=4), per_head(beta[:, c, :]),
                                  ALU.mult).then_inc(ev("g_vt_copied"), 1)
            dve.wait_ge(ev("g_beta_ready"), 1)
            dve.wait_ge(ev("g_k_ready"), 1)
            dve.tensor_tensor(g_kb, gq[:, 4:8, :], stat[:, :, :], ALU.mult).then_inc(ev("g_kb_ready"), 1)
            dve.wait_ge(ev("g_kt_copied"), 2)
            for c in range(NT):
                ins = dve.tensor_tensor(tokens(g_r2, c), tokens(g_kt, c), per_head(beg[:, c, :]), ALU.mult)
            link(ins)
            for c in range(NT):
                ins = dve.tensor_tensor(tokens(g_kt, c), tokens(g_kt, c), per_head(kdec[:, c, :]), ALU.mult)
            link(ins)
            dve.wait_ge(ev("g_er_ready"), 1)
            rows_to_decays(g_dec, mixp, lambda c: cums[:, c, 8:12], K["neg_causal64"]).then_inc(ev("g_rows_read"), 1)
            link(dve.tensor_tensor(g_qd, gq[:, 0:4, :], g_er, ALU.mult))
            dve.wait_ge(ev("g_dec_ready"), 1)

            def masks(name):
                return K[name].unsqueeze(1).broadcast_to([P, 8, P])

            def flat(ap):
                return ap.rearrange("p h (c t) -> p (h c) t", t=P)

            dve.wait_ge(ev("g_kk_ready"), 1)
            link(dve.tensor_tensor(g_mt, stat[:, :, :], g_dec, ALU.mult))
            dve.tensor_tensor(flat(g_mt), flat(g_mt), masks("before64"), ALU.mult).then_inc(ev("g_mt_ready"), 1)
            dve.wait_ge(ev("g_mt_ready"), 1)
            dve.wait_ge(ev("g_kq_ready"), 1)
            dve.tensor_tensor(g_at, mixp[:, :, :], g_dec, ALU.mult).then_inc(ev("g_at_ready"), 1)
            link(dve.tensor_tensor(flat(g_dt), flat(g_mt), masks("lowT0"), ALU.mult))
            link(dve.tensor_tensor(flat(g_dt), masks("ident"), flat(g_dt), ALU.subtract))
            link(dve.tensor_tensor(flat(g_ml), flat(g_mt), masks("lowT1"), ALU.mult))
            dve.wait_ge(ev("g_m_ready"), 1)
            link(dve.tensor_tensor(flat(g_d), flat(stat[:, :, :]), masks("low0"), ALU.mult))
            dve.tensor_tensor(flat(g_d), masks("ident"), flat(g_d), ALU.subtract).then_inc(ev("g_d_ready"), 1)
            dve.wait_ge(ev("g_d_ready"), 1)
            gate_branch(0, 0)
            for n in range(1, 6):
                if n == 3:
                    gate_branch(0, 1)
                dve.wait_ge(ev("g_ddt_ready"), n)
                if n < 5:
                    link(dve.tensor_tensor(flat(g_ml), flat(g_mt), masks(f"lowT{n + 1}"), ALU.mult))
                    dve.wait_ge(ev("g_dd_ready"), n)
                    link(dve.tensor_tensor(g_dt, g_dt, stat[:, :, :], ALU.subtract))
                    dve.tensor_tensor(g_d, g_d, mixp[:, :, :], ALU.subtract).then_inc(ev("g_d_ready"), 1)
                    dve.wait_ge(ev("g_d_ready"), n + 1)
                else:
                    dve.tensor_tensor(g_dt, g_dt, stat[:, :, :], ALU.subtract).then_inc(ev("g_dt_final"), 1)
            gate_branch(0, 2)
            dve.wait_ge(ev("g_u_ready"), 1)
            dve.tensor_copy(g_kb, stat[:, :, :]).then_inc(ev("g_u_copied"), 1)
            dve.wait_ge(ev("g_u_copied"), 1)
            for ch in range(4):
                c, o = ch // 2, 64 * (ch % 2)
                vn, u = g_ml[o:o + 64, :, c * P:(c + 1) * P], g_kb[o:o + 64, :, c * P:(c + 1) * P]
                if ch:
                    dve.wait_ge(ev("g_ws_ready"), ch)
                    dve.tensor_tensor(vn, u, mixbank(0)[o:o + 64, :].rearrange("p (h d) -> p h d", h=4), ALU.subtract)\
                        .then_inc(ev("g_vn_ready"), 1)
                else:
                    dve.tensor_copy(vn, u).then_inc(ev("g_vn_ready"), 1)
                if ch == 3:
                    break
                dve.wait_ge(ev("g_ds_ready"), ch + 1)
                dve.wait_ge(ev("g_o_ready"), ch + 1)
                ds_ = mixbank(1).rearrange("p (h d) -> p h d", h=4)
                if ch:
                    for i in range(4):
                        ins = dve.scalar_tensor_tensor(g_s[:, i, :], g_s[:, i, :], g_er[:, i, ch * 64 + 63:ch * 64 + 64],
                                                       ds_[:, i, :], ALU.mult, ALU.add)
                else:
                    ins = dve.tensor_copy(g_s, ds_)
                ins.then_inc(ev("g_s_ready"), 1)
                dve.wait_ge(ev("g_s_ready"), ch + 1)
            dve.wait_ge(ev("g_o_ready"), 4)
            dve.tensor_copy(ybr[:, 8:12, :], stat[:, :, :]).then_inc(ev("g_o_read"), 1)
            dve.wait_ge(ev("g_o_read"), 1)
            dve.wait_ge(rs_ready, seen(rs_ready))
            link(dve.scalar_tensor_tensor(ybr[:, 8:12, :], ybr[:, 8:12, :], col("gdn_norm"), rs[:, :, :], ALU.mult, ALU.mult))
            dve.wait_ge(ev("gg_ready"), 1)
            dve.tensor_tensor(ybr[:, 8:12, :], ybr[:, 8:12, :], gg, ALU.mult).then_inc(ev("yc_done"), 1)
            gate_branch(0, 3)
            link(dve.tensor_scalar(qn, col("sb_qn"), P ** -0.5, None, ALU.mult))
            dve.wait_ge(rs_ready, seen(rs_ready))
            dve.scalar_tensor_tensor(sq_kv[:, 0:4, :], sq_kv[:, 0:4, :], qn, rs[:, :, :], ALU.mult, ALU.mult).then_inc(ev("b_q_ready"), 1)
            dve.wait_ge(rs_ready, seen(rs_ready))
            dve.scalar_tensor_tensor(sq_kv[:, 4:8, :], sq_kv[:, 4:8, :], col("sb_kn"), rs[:, :, :], ALU.mult, ALU.mult)\
                .then_inc(ev("b_qk_ready"), 1)
            for c in range(NT):
                dve.wait_ge(ev("b_vt_turned"), c + 1)
                dve.tensor_copy(b_vt[:, c, :], mixbank(c)).then_inc(ev("b_vt_copied"), 1)
            gate_branch(2, 0)
            dve.wait_ge(ev("b_l_ready"), 1)
            for k in range(2):
                s = slice(2 * k, 2 * k + 2)
                dve.scalar_tensor_tensor(b_lb[:, s, :], zbanks(k), 0.0, b_l[:, s, :], ALU.min, ALU.subtract)
                ins = dve.scalar_tensor_tensor(b_nk[:, s, :], zbanks(k), 0.0, b_l[:, s, :], ALU.max, ALU.add)
            link(ins)
            before = K["before"].unsqueeze(1).broadcast_to([P, 4, P])
            dve.tensor_tensor(b_nk[:, :, 0:P], b_nk[:, :, 0:P], before, ALU.mult)
            dve.tensor_tensor(b_nk[:, :, T:3 * P], b_nk[:, :, T:3 * P], before, ALU.mult).then_inc(ev("b_nk_ready"), 1)
            gate_branch(2, 1)
            dve.wait_ge(ev("b_after_ready"), 1)
            for k in range(2):
                s = slice(2 * k, 2 * k + 2)
                ins = dve.tensor_tensor(b_lb[:, s, :], b_lb[:, s, :], zbanks(k), ALU.subtract)
            ins.then_inc(ev("b_lb_ready"), 1)
            dve.wait_ge(ev("b_exp_ready"), 1)
            dve.tensor_tensor(b_l[:, :, 0:P], b_l[:, :, 0:P], before, ALU.mult)
            dve.tensor_tensor(b_l[:, :, T:3 * P], b_l[:, :, T:3 * P], before, ALU.mult).then_inc(ev("b_att_ready"), 1)
            dve.wait_ge(ev("b_o_ready"), 1)
            dve.tensor_copy(ybr[:, 4:8, :], stat[:, :, :]).then_inc(ev("yb2_done"), 1)
            gate_branch(2, 2)
            gate_branch(2, 3)
            for pair in range(4):
                gate_branch(1, pair)
            residual(8, lambda m: mod[:, 2 * KD + m:2 * KD + m + 1])
            panels.settled()
            modulated(1)
            dve.memset(e_dT, 0.0).then_inc(M["dT"], 1)
            dve.memset(e_yb, 0.0).then_inc(M["yb"], 1)
            dve.memset(e_sg, 0.0).then_inc(M["hid"], 1)
            dve.memset(rankp, -1.0)
            dve.memset(wp, 0.0)
            dve.wait_ge(ev("logits_ready"), 1)
            a0 = ROWS["b_route"][0]
            link(dve.tensor_tensor(r_lg, mixbank(0)[:, 0:72].rearrange("p (c n) -> p c n", c=NT),
                                   rows[:, a0:a0 + 36].unsqueeze(1).broadcast_to([P, NT, 36]), ALU.add))

            def wide(ap, n):
                return ap.unsqueeze(2).broadcast_to([P, NT, n])

            def iota(n):
                return K["iota_e"][:, 0:n].unsqueeze(1).broadcast_to([P, NT, n])

            def first_max(onehot, values, best, n):
                link(dve.tensor_reduce(best, values, AX, ALU.max))
                link(dve.tensor_tensor(onehot, values, wide(best, n), ALU.is_equal))
                link(dve.scalar_tensor_tensor(onehot, onehot, -1000.0, iota(n), ALU.mult, ALU.add))
                link(dve.tensor_reduce(r_at, onehot, AX, ALU.min))
                link(dve.tensor_scalar(r_at, r_at, 1000.0, None, ALU.add))
                link(dve.tensor_tensor(onehot, iota(n), wide(r_at, n), ALU.is_equal))

            groups, experts = r_lg[:, :, 0:EG], r_lg[:, :, EG:EG + E]
            first_max(r_goh, groups, r_best, EG)
            dve.tensor_tensor(r_ge, groups, wide(r_best, EG), ALU.subtract).then_inc(ev("route_in"), 1)
            for c in range(NT):
                v = experts[:, c, :].rearrange("p (g e) -> p g e", g=EG)
                dst = r_ml[:, c, :].rearrange("p (g e) -> p g e", g=EG)
                mask = r_goh[:, c, :].unsqueeze(2).broadcast_to([P, EG, E // EG])
                link(dve.tensor_tensor(dst, v, mask, ALU.mult))
            link(dve.tensor_scalar(r_goh, r_goh, -1.0, -NEG, ALU.add, ALU.mult))
            for c in range(NT):
                dst = r_ml[:, c, :].rearrange("p (g e) -> p g e", g=EG)
                mask = r_goh[:, c, :].unsqueeze(2).broadcast_to([P, EG, E // EG])
                link(dve.tensor_tensor(dst, dst, mask, ALU.add))
            first_max(r_oh1, r_ml, r_m1, E)
            link(dve.scalar_tensor_tensor(r_ml, r_oh1, NEG, r_ml, ALU.mult, ALU.add))
            first_max(r_oh2, r_ml, r_m2, E)
            dve.tensor_tensor(r_e2, r_m2, r_m1, ALU.subtract).then_inc(ev("top_in"), 1)
            dve.tensor_tensor(assign, r_oh1, r_oh2, ALU.add).then_inc(ev("assigned"), 1)
            dve.wait_ge(ev("assigned"), 1)
            dve.wait_ge(ev("ranks_ready"), 1)
            ranks = mixbank(0)[:, 0:2 * E].rearrange("p (c n) -> p c n", c=NT)
            link(dve.scalar_tensor_tensor(r_rank, ranks, 1.0, assign, ALU.add, ALU.mult))
            link(dve.tensor_scalar(r_rank, r_rank, -1.0, None, ALU.add))
            for p in range(PASSES):
                ins = dve.tensor_scalar(rankp[:, :, p * E:(p + 1) * E], r_rank, -float(p * SLOTS), None, ALU.add)
            link(ins)

            def select(dst, e):
                for c in range(NT):
                    ins = dve.tensor_scalar(dst[:, c, :], K["iota"][:, 0:SLOTS], rankp[:, c, e], None, ALU.is_equal)
                ins.then_inc(M["sel"], 1)

            def weigh(dst, e):
                for c in range(NT):
                    ins = dve.tensor_scalar(dst[:, c, :], K["iota"], rankp[:, c, e], wp[:, c, e], ALU.is_equal, ALU.mult)
                ins.then_inc(M["selw"], 1)

            def gathered():
                dve.tensor_copy(e_hg, statbank(0)).then_inc(M["hg"], 1)

            select(e_sel[:, 0, :, :], slice(0, 1))
            select(e_sel[:, 1, :, :], slice(1, 2))
            dve.wait_ge(ev("group_exp"), 1)
            link(dve.tensor_reduce(r_pg, r_ge, AX, ALU.add))
            link(dve.reciprocal(r_pg, r_pg))
            dve.wait_ge(ev("top_exp"), 1)
            link(dve.tensor_scalar(r_w1, r_e2, 1.0, None, ALU.add))
            link(dve.reciprocal(r_w1, r_w1))
            link(dve.tensor_tensor(r_w1, r_w1, r_pg, ALU.mult))
            link(dve.tensor_tensor(r_w2, r_w1, r_e2, ALU.mult))
            link(dve.tensor_tensor(r_oh1, r_oh1, wide(r_w1, E), ALU.mult))
            link(dve.tensor_tensor(r_oh2, r_oh2, wide(r_w2, E), ALU.mult))
            for p in range(PASSES):
                ins = dve.tensor_tensor(wp[:, :, p * E:(p + 1) * E], r_oh1, r_oh2, ALU.add)
            link(ins)
            link(dve.tensor_reduce(r_cnt, mixbank(0)[:, 2 * E:3 * E], AX, ALU.max))
            dve.tensor_scalar(flag_i, r_cnt, float(SLOTS), None, ALU.is_gt).then_inc(M["flag"], 1)
            weigh(e_selw[:, 0, :, :], slice(0, 1))
            dve.wait_ge(M["A"], 1)
            gathered()
            dve.wait_ge(M["A"], 2)
            dve.wait_ge(M["B"], 1)
            gathered()

            def moe_step(it, s):
                dve.wait_ge(M["A"], it * 2 + (s + 1))
                select(e_sel[:, s, :, :], ds(it * 2 + (s + 2), 1))
                dve.wait_ge(M["silu"], it * 2 + (s + 1))
                dve.tensor_tensor(e_hid, e_sg, mixbank(0)[:, T:2 * T], ALU.mult).then_inc(M["hid"], 1)
                dve.wait_ge(M["D"], it * 2 + (s + 1))
                dve.tensor_copy(e_dT, mixbank(1)).then_inc(M["dT"], 1)
                weigh(e_selw[:, 1 - s, :, :], ds(it * 2 + (s + 1), 1))
                dve.wait_ge(M["A"], it * 2 + (s + 3))
                gathered()

            with dve.Fori(0, E // 2) as it:
                moe_step(it, 0)
                moe_step(it, 1)
            more = dve.value_load(flag_i[0:1, 0:1], min_val=0, max_val=1)
            with dve.If(more == 1):
                with dve.Fori(E // 2, NE // 2) as it:
                    moe_step(it, 0)
                    moe_step(it, 1)
            dve.wait_ge(M["y"], 1)
            for m in range(KD):
                dve.scalar_tensor_tensor(x[:, m, :], lin[m // 2][:, (m % 2) * T:(m % 2 + 1) * T],
                                         mod[:, 5 * KD + m:5 * KD + m + 1], x[:, m, :], ALU.mult, ALU.add)\
                    .then_inc(ev("x_out"), 1)


WEIGHTS = ["even_w_in", "even_w_out", "odd_w_qkv", "odd_w_o", "ffn_w_up", "ffn_w_down", "w_ada"]


def kernel(**inputs):
    import numpy as _np
    import concourse.bacc as _bacc
    from concourse import mybir as _mybir
    from concourse.bass_utils import run_bass_kernel_spmd as _run

    def tiles(v):
        return _np.asarray(v).reshape(-1, P).T

    g = {k: _np.asarray(v) for k, v in inputs.items()}
    source = {
        "even_norm": g["even_norm_g"], "b_in": g["even_b_in"], "vln_g": g["even_v_ln_g"], "vln_b": g["even_v_ln_b"],
        "conv_w": g["even_conv_w"], "conv_b": g["even_conv_b"], "cln_g": g["even_conv_ln_g"], "cln_b": g["even_conv_ln_b"],
        "odd_norm": g["odd_norm_g"], "ffn_norm": g["ffn_norm_g"], "ffn_cw": g["ffn_conv_w"], "ffn_cb": g["ffn_conv_b"],
        "final_norm": g["final_norm_g"], "c": g["c_2"], "b_ada": g["b_ada_2"], "norm_mix": g["norm_mix_2"],
        "norm_ffn": g["norm_ffn_2"], "ssm_cw": g["ssm_conv_w_2"], "ssm_cb": g["ssm_conv_b_2"], "ssm_norm": g["ssm_norm_2"],
        "ssm_d": _np.repeat(g["ssm_d_2"], HD), "sb_qn": g["sb_q_norm_2"], "sb_kn": g["sb_k_norm_2"],
        "gdn_cw": g["gdn_conv_w_2"], "gdn_norm": g["gdn_norm_2"],
    }
    layout, _ = col_layout()
    arrays = {
        "cols": _np.ascontiguousarray(_np.concatenate([tiles(source[k]) for k in layout], axis=1)),
        "x": _np.ascontiguousarray(g["x"][0].T.reshape(KD, P, T).transpose(1, 0, 2)),
        "consts": _np.concatenate(list(const_arrays().values()), axis=1),
        "rows": _np.concatenate([v.reshape(-1) for v in (
            g["even_b_s"], g["b_group_2"], g["b_router_2"], g["ssm_dt_bias_2"], g["gdn_dt_bias_2"], g["ssm_a_log_2"],
            g["gdn_a_log_2"])]),
        "even_w_s": _np.ascontiguousarray(g["even_w_s"][0].transpose(2, 0, 1)),
        "w_small": _np.ascontiguousarray(_np.concatenate(
            [g["w_in_2"][0][:, DT0:DT0 + 8], g["w_in_2"][0][:, GAB0:GAB0 + 8], g["w_group_2"][0], g["w_router_2"][0]],
            axis=1).reshape(KD, P, 52).transpose(1, 0, 2)),
        "even_w_in": g["even_w_in"][0], "even_w_out": g["even_w_out"][0], "odd_w_qkv": g["odd_w_qkv"][0],
        "odd_w_o": g["odd_w_o"][0], "ffn_w_up": g["ffn_w_up"], "ffn_w_down": g["ffn_w_down"], "w_ada": g["w_ada_2"][0],
        "w_in": g["w_in_2"][0], "w_branch": g["w_branch_2"][0], "w_out": g["w_out_2"][0],
        "w_gate": g["w_gate_2"][0], "w_up": g["w_up_2"][0], "w_down": g["w_down_2"][0],
    }
    nc = _bacc.Bacc("TRN2", target_bir_lowering=False, num_devices=1)
    aps = {k: nc.dram_tensor(f"in_{k}", v.shape, _mybir.dt.float32, kind="ExternalInput").ap() for k, v in arrays.items()}
    out = nc.dram_tensor("out_x", (P, KD, T), _mybir.dt.float32, kind="ExternalOutput").ap()
    program(nc, aps, out)
    r = _run(nc, [{f"in_{k}": v for k, v in arrays.items()}], core_ids=[0])
    y = r.results[0]["out_x"]
    return y.transpose(2, 1, 0).reshape(1, T, D)
```
